# Optimizing a Trainium2 kernel written in Bass

```python
import jax, jax.numpy as jnp
from jax import lax
import numpy as np
import math
import jax
import jax.numpy as jnp

D_MODEL = 1024
BATCH = 1
SEQ = 256
DEPTH = 2

MEM_LEN = 256
N_EVEN = (DEPTH + 1) // 2
N_ODD = DEPTH // 2

MIX_WIDTH = D_MODEL
A_WIDTH = MIX_WIDTH // 2
A_CONV = 3
B_WIDTH = MIX_WIDTH - A_WIDTH
POOL_WINDOWS = (2, 4, 8, 16)
B_GROUP = B_WIDTH // len(POOL_WINDOWS)
IN_COLS = 3 * A_WIDTH + B_WIDTH

C_CONV = 31

XATTN_HEADS = 4
XATTN_HEAD_DIM = D_MODEL // XATTN_HEADS

D_FF = ((8 * D_MODEL // 3 + 255) // 256) * 256
N_EXPERTS = 8
TOP_K = 2
D_FF_EXPERT = 7 * D_MODEL // 2

EPS = 1e-6


def rmsnorm(x, g):
    xf = x.astype(jnp.float32)
    y = xf * lax.rsqrt(jnp.mean(xf * xf, axis=-1, keepdims=True) + EPS)
    return (y * g.astype(jnp.float32)).astype(x.dtype)

def layernorm(x, g, b):
    xf = x.astype(jnp.float32)
    mu = jnp.mean(xf, axis=-1, keepdims=True)
    xc = xf - mu
    var = jnp.mean(xc * xc, axis=-1, keepdims=True)
    y = xc * lax.rsqrt(var + EPS) * g.astype(jnp.float32) + b.astype(jnp.float32)
    return y.astype(x.dtype)

def depthwise_conv(x, w):
    k = w.shape[0]
    c = x.shape[-1]
    return lax.conv_general_dilated(
        x, w[:, None, :].astype(x.dtype), window_strides=(1,),
        padding=[(k // 2, k // 2)], dimension_numbers=("NWC", "WIO", "NWC"),
        feature_group_count=c)

def centred_window_mean(u, window):
    s = u.shape[1]
    left = window // 2
    right = window - 1 - left
    t = np.arange(s)
    lo = np.maximum(t - left, 0)
    hi = np.minimum(t + right, s - 1) + 1
    uf = u.astype(jnp.float32)
    cs = jnp.concatenate([jnp.zeros_like(uf[:, :1]), jnp.cumsum(uf, axis=1)], axis=1)
    count = jnp.asarray((hi - lo).astype(np.float32))[None, :, None]
    return ((cs[:, hi] - cs[:, lo]) / count).astype(u.dtype)

def short_conv_mixer(h, gate_b, gate_c, conv_w):
    return gate_b * depthwise_conv(gate_c * h, conv_w)

def pool_mixer(u, w_groups, scale):
    outs = []
    for g, win in enumerate(POOL_WINDOWS):
        ug = u[..., g * B_GROUP:(g + 1) * B_GROUP]
        outs.append(centred_window_mean(ug, win) - ug)
    p = jnp.stack(outs, axis=2)
    y = jnp.einsum("bsgc,gcd->bsgd", p, w_groups)
    return y.reshape(u.shape) * scale

def even_mixer(xn, w_in, conv_a, pool_w, pool_scale, w_out):
    z = xn @ w_in
    h, gb, gc, u = jnp.split(z, [A_WIDTH, 2 * A_WIDTH, 3 * A_WIDTH], axis=-1)
    y = jnp.concatenate([short_conv_mixer(h, gb, gc, conv_a),
                         pool_mixer(u, pool_w, pool_scale)], axis=-1)
    return y @ w_out

def conformer_conv(xn, pw1_w, pw1_b, dw_w, dw_b, ln_g, ln_b, pw2_w, pw2_b):
    a, g = jnp.split(xn @ pw1_w + pw1_b, 2, axis=-1)
    h = a * jax.nn.sigmoid(g)
    h = depthwise_conv(h, dw_w) + dw_b
    h = jax.nn.silu(layernorm(h, ln_g, ln_b))
    return h @ pw2_w + pw2_b

def cross_attn(xn, mem, norm_mem, wq, wkv, wo):
    b, s, d = xn.shape
    m = mem.shape[1]
    q = (xn @ wq).reshape(b, s, XATTN_HEADS, XATTN_HEAD_DIM)
    k, v = jnp.split(rmsnorm(mem, norm_mem) @ wkv, 2, axis=-1)
    k = k.reshape(b, m, XATTN_HEADS, XATTN_HEAD_DIM)
    v = v.reshape(b, m, XATTN_HEADS, XATTN_HEAD_DIM)
    sc = jnp.einsum("bshd,bmhd->bhsm", q, k).astype(jnp.float32) * (XATTN_HEAD_DIM ** -0.5)
    p = jax.nn.softmax(sc, axis=-1).astype(v.dtype)
    o = jnp.einsum("bhsm,bmhd->bshd", p, v).reshape(b, s, d)
    return o @ wo

def swiglu(xn, w_gu, w_down):
    g, u = jnp.split(xn @ w_gu, 2, axis=-1)
    return (jax.nn.silu(g) * u) @ w_down

def moe_swiglu(xn, router, w_gu, w_down):
    logits = (xn @ router).astype(jnp.float32)
    top_v, top_i = lax.top_k(logits, TOP_K)
    w = jax.nn.softmax(top_v, axis=-1)
    comb = jnp.sum(jax.nn.one_hot(top_i, N_EXPERTS, dtype=jnp.float32) * w[..., None],
                   axis=-2).astype(xn.dtype)
    out = jnp.zeros_like(xn)
    for e in range(N_EXPERTS):
        out = out + comb[..., e:e + 1] * swiglu(xn, w_gu[e], w_down[e])
    return out

def first_inputs(seed: int = 0) -> dict:
    key = jax.random.key(seed)
    ks = iter(jax.random.split(key, 40))
    f32 = jnp.float32

    def nrm(shape, scale):
        return jax.random.normal(next(ks), shape, f32) * scale

    def gain(shape):
        return 1.0 + 0.02 * jax.random.normal(next(ks), shape, f32)

    D = D_MODEL
    return {
        "x": nrm((BATCH, SEQ, D), 1.0),
        "mem": nrm((BATCH, MEM_LEN, D), 1.0),
        "ev_norm_mix": gain((N_EVEN, D)),
        "ev_w_in": nrm((N_EVEN, D, IN_COLS), D ** -0.5),
        "ev_conv_a": nrm((N_EVEN, A_CONV, A_WIDTH), A_CONV ** -0.5),
        "ev_pool_w": nrm((N_EVEN, len(POOL_WINDOWS), B_GROUP, B_GROUP), B_GROUP ** -0.5),
        "ev_pool_scale": gain((N_EVEN, B_WIDTH)),
        "ev_w_out": nrm((N_EVEN, MIX_WIDTH, D), MIX_WIDTH ** -0.5),
        "ev_norm_ffn": gain((N_EVEN, D)),
        "ev_ffn_gu": nrm((N_EVEN, D, 2 * D_FF), D ** -0.5),
        "ev_ffn_down": nrm((N_EVEN, D_FF, D), D_FF ** -0.5),
        "od_norm_mix": gain((N_ODD, D)),
        "od_pw1_w": nrm((N_ODD, D, 2 * D), D ** -0.5),
        "od_pw1_b": nrm((N_ODD, 2 * D), 0.02),
        "od_dw_w": nrm((N_ODD, C_CONV, D), C_CONV ** -0.5),
        "od_dw_b": nrm((N_ODD, D), 0.02),
        "od_ln_g": gain((N_ODD, D)),
        "od_ln_b": nrm((N_ODD, D), 0.02),
        "od_pw2_w": nrm((N_ODD, D, D), D ** -0.5),
        "od_pw2_b": nrm((N_ODD, D), 0.02),
        "od_norm_moe": gain((N_ODD, D)),
        "od_router": nrm((N_ODD, D, N_EXPERTS), D ** -0.5),
        "od_moe_gu": nrm((N_ODD, N_EXPERTS, D, 2 * D_FF_EXPERT), D ** -0.5),
        "od_moe_down": nrm((N_ODD, N_EXPERTS, D_FF_EXPERT, D), D_FF_EXPERT ** -0.5),
        "xa_norm": gain((DEPTH, D)),
        "xa_norm_mem": gain((DEPTH, D)),
        "xa_wq": nrm((DEPTH, D, D), D ** -0.5),
        "xa_wkv": nrm((DEPTH, D, 2 * D), D ** -0.5),
        "xa_wo": nrm((DEPTH, D, D), D ** -0.5),
        "final_norm": gain((D,)),
    }

def first_block(x, mem,
              ev_norm_mix, ev_w_in, ev_conv_a, ev_pool_w, ev_pool_scale, ev_w_out,
              ev_norm_ffn, ev_ffn_gu, ev_ffn_down,
              od_norm_mix, od_pw1_w, od_pw1_b, od_dw_w, od_dw_b, od_ln_g, od_ln_b,
              od_pw2_w, od_pw2_b, od_norm_moe, od_router, od_moe_gu, od_moe_down,
              xa_norm, xa_norm_mem, xa_wq, xa_wkv, xa_wo, final_norm):
    h = x
    for layer in range(DEPTH):
        i = layer // 2
        if layer % 2 == 0:
            h = h + even_mixer(rmsnorm(h, ev_norm_mix[i]), ev_w_in[i], ev_conv_a[i],
                               ev_pool_w[i], ev_pool_scale[i], ev_w_out[i])
        else:
            h = h + conformer_conv(rmsnorm(h, od_norm_mix[i]), od_pw1_w[i], od_pw1_b[i],
                                   od_dw_w[i], od_dw_b[i], od_ln_g[i], od_ln_b[i],
                                   od_pw2_w[i], od_pw2_b[i])
        h = h + cross_attn(rmsnorm(h, xa_norm[layer]), mem, xa_norm_mem[layer],
                           xa_wq[layer], xa_wkv[layer], xa_wo[layer])
        if layer % 2 == 0:
            h = h + swiglu(rmsnorm(h, ev_norm_ffn[i]), ev_ffn_gu[i], ev_ffn_down[i])
        else:
            h = h + moe_swiglu(rmsnorm(h, od_norm_moe[i]), od_router[i],
                               od_moe_gu[i], od_moe_down[i])
    return rmsnorm(h, final_norm)


DEPTH_2 = 1

CHUNK = 64
Q_BLOCK = 128
MEM_HEADS = 4
MEM_DIM = D_MODEL // MEM_HEADS

FOX_DIM = 64
FOX_W = D_MODEL // 4
FOX_HEADS = FOX_W // FOX_DIM
DIFF_QK_DIM = 32
DIFF_V_DIM = 2 * DIFF_QK_DIM
DIFF_W = D_MODEL // 4
DIFF_HEADS = DIFF_W // DIFF_V_DIM
HGRN_DIM = 128
HGRN_W = D_MODEL - FOX_W - DIFF_W
HGRN_HEADS = HGRN_W // HGRN_DIM

MIX_W = FOX_W + DIFF_W + HGRN_W
IN_SIZES = (FOX_W, FOX_W, FOX_W, FOX_HEADS, DIFF_W, DIFF_W, DIFF_W, HGRN_W, HGRN_W, HGRN_W, HGRN_W)
IN_W = sum(IN_SIZES)

N_EXPERTS_2 = 16
N_GROUPS = 4
EXPERTS_PER_GROUP = N_EXPERTS_2 // N_GROUPS
EXPERT_FF = D_MODEL // 2

ALPHA = (2 * DEPTH_2) ** 0.25
BETA = (8 * DEPTH_2) ** -0.25
LN_EPS = 1e-5


def _layer_norm(x, g, b):
    xf = x.astype(jnp.float32)
    mu = jnp.mean(xf, axis=-1, keepdims=True)
    var = jnp.mean(jnp.square(xf - mu), axis=-1, keepdims=True)
    y = (xf - mu) * lax.rsqrt(var + LN_EPS) * g.astype(jnp.float32) + b.astype(jnp.float32)
    return y.astype(x.dtype)

def _rms_norm(x, g):
    xf = x.astype(jnp.float32)
    y = xf * lax.rsqrt(jnp.mean(xf * xf, axis=-1, keepdims=True) + LN_EPS) * g.astype(jnp.float32)
    return y.astype(x.dtype)

def _split_heads(t, n_heads):
    b, s, _ = t.shape
    return t.reshape(b, s, n_heads, -1).transpose(0, 2, 1, 3)

def _merge_heads(t):
    b, h, s, d = t.shape
    return t.transpose(0, 2, 1, 3).reshape(b, s, h * d)

def _to_blocks(t):
    b, h, s = t.shape[:3]
    t = t.reshape((b, h, s // Q_BLOCK, Q_BLOCK) + t.shape[3:])
    return jnp.moveaxis(t, 2, 0)

def _from_blocks(t):
    nb, b, h, q, d = t.shape
    return t.transpose(1, 2, 0, 3, 4).reshape(b, h, nb * q, d)

def _split_columns(proj):
    parts, start = [], 0
    for width in IN_SIZES:
        parts.append(proj[..., start:start + width])
        start += width
    return parts

def _forgetting_attention(q, k, v, log_f):
    s = q.shape[2]
    cum = jnp.cumsum(log_f, axis=-1)
    key_pos = jnp.arange(s)
    query_pos = key_pos.reshape(s // Q_BLOCK, Q_BLOCK)
    scale = FOX_DIM ** -0.5

    def block(args):
        q_blk, c_blk, q_pos = args
        logits = jnp.einsum('bhqd,bhkd->bhqk', q_blk, k).astype(jnp.float32) * scale
        logits = logits + c_blk[..., :, None] - cum[..., None, :]
        logits = jnp.where(key_pos[None, :] <= q_pos[:, None], logits, -jnp.inf)
        p = jax.nn.softmax(logits, axis=-1).astype(v.dtype)
        return jnp.einsum('bhqk,bhkd->bhqd', p, v)

    out = lax.map(block, (_to_blocks(q), _to_blocks(cum), query_pos))
    return _from_blocks(out)

def _differential_attention(q1, q2, k1, k2, v, lam):
    s = q1.shape[2]
    key_chunk = jnp.arange(s) // CHUNK
    query_chunk = key_chunk.reshape(s // Q_BLOCK, Q_BLOCK)
    scale = DIFF_QK_DIM ** -0.5

    def block(args):
        q1b, q2b, qc = args
        visible = key_chunk[None, :] <= qc[:, None]

        def attn_map(qb, kk):
            logits = jnp.einsum('bhqd,bhkd->bhqk', qb, kk).astype(jnp.float32) * scale
            return jax.nn.softmax(jnp.where(visible, logits, -jnp.inf), axis=-1)

        p = attn_map(q1b, k1) - lam * attn_map(q2b, k2)
        return jnp.einsum('bhqk,bhkd->bhqd', p.astype(v.dtype), v)

    out = lax.map(block, (_to_blocks(q1), _to_blocks(q2), query_chunk))
    return _from_blocks(out)

def _hgrn2_recurrence(q, k, log_f, v):
    b, h, s, dk = q.shape
    dv = v.shape[-1]
    n = s // CHUNK

    def chunks(t):
        t = t.astype(jnp.float32)
        return t.reshape(b, h, n, CHUNK, t.shape[-1]).transpose(2, 0, 1, 3, 4)

    pos = jnp.arange(CHUNK)
    causal = (pos[:, None] >= pos[None, :])[None, None, :, :, None]

    def step(state, inp):
        qc, kc, gc, vc = inp
        bc = jnp.cumsum(gc, axis=2)
        rel = jnp.where(causal, bc[:, :, :, None, :] - bc[:, :, None, :, :], -jnp.inf)
        scores = jnp.einsum('bhtd,bhsd,bhtsd->bhts', qc, kc, jnp.exp(rel))
        o = (jnp.einsum('bhts,bhsv->bhtv', scores, vc)
             + jnp.einsum('bhtd,bhdv->bhtv', qc * jnp.exp(bc), state))
        b_last = bc[:, :, -1, :]
        k_dec = kc * jnp.exp(b_last[:, :, None, :] - bc)
        state = jnp.exp(b_last)[..., None] * state + jnp.einsum('bhsd,bhsv->bhdv', k_dec, vc)
        return state, o

    state0 = jnp.zeros((b, h, dk, dv), jnp.float32)
    _, o = lax.scan(step, state0, (chunks(q), chunks(k), chunks(log_f), chunks(v)))
    return o.transpose(1, 2, 0, 3, 4).reshape(b, h, s, dv)

def _hybrid_mixer(x, w_in, fox_fb, lam_q1, lam_k1, lam_q2, lam_k2, lam_init,
                  diff_norm_g, lower_bound, hgrn_norm_g, w_out):
    proj = x @ w_in
    fq, fk, fv, ff, dq, dk, dv, hq, hf, hi, hg = _split_columns(proj)

    log_f = jax.nn.log_sigmoid(ff.astype(jnp.float32) + fox_fb.astype(jnp.float32))
    y_fox = _forgetting_attention(_split_heads(fq, FOX_HEADS), _split_heads(fk, FOX_HEADS),
                                  _split_heads(fv, FOX_HEADS), log_f.transpose(0, 2, 1))

    dq_h = _split_heads(dq, DIFF_HEADS)
    dk_h = _split_heads(dk, DIFF_HEADS)
    lam = (jnp.exp(jnp.sum(lam_q1.astype(jnp.float32) * lam_k1.astype(jnp.float32)))
           - jnp.exp(jnp.sum(lam_q2.astype(jnp.float32) * lam_k2.astype(jnp.float32)))
           + lam_init)
    y_diff = _differential_attention(dq_h[..., :DIFF_QK_DIM], dq_h[..., DIFF_QK_DIM:],
                                     dk_h[..., :DIFF_QK_DIM], dk_h[..., DIFF_QK_DIM:],
                                     _split_heads(dv, DIFF_HEADS), lam)
    y_diff = _rms_norm(y_diff, diff_norm_g) * (1.0 - lam_init)

    f_logit = hf.astype(jnp.float32)
    lb = lower_bound.astype(jnp.float32)
    log_f_h = jnp.logaddexp(jnp.log(lb), jnp.log1p(-lb) + jax.nn.log_sigmoid(f_logit))
    k_h = (1.0 - lb) * jax.nn.sigmoid(-f_logit)
    o = _hgrn2_recurrence(_split_heads(jax.nn.silu(hq), HGRN_HEADS), _split_heads(k_h, HGRN_HEADS),
                          _split_heads(log_f_h, HGRN_HEADS), _split_heads(hi, HGRN_HEADS))
    y_hgrn = _rms_norm(o, hgrn_norm_g) * jax.nn.silu(_split_heads(hg, HGRN_HEADS).astype(jnp.float32))

    y = jnp.concatenate([_merge_heads(y_fox).astype(x.dtype), _merge_heads(y_diff).astype(x.dtype),
                         _merge_heads(y_hgrn).astype(x.dtype)], axis=-1)
    return y @ w_out

def _memory_attention(x, mem, w_q, w_k, w_v, w_o):
    q = _split_heads(x @ w_q, MEM_HEADS)
    k = _split_heads(mem @ w_k, MEM_HEADS)
    v = _split_heads(mem @ w_v, MEM_HEADS)
    logits = jnp.einsum('bhqd,bhkd->bhqk', q, k).astype(jnp.float32) * MEM_DIM ** -0.5
    p = jax.nn.softmax(logits, axis=-1).astype(v.dtype)
    return _merge_heads(jnp.einsum('bhqk,bhkd->bhqd', p, v)) @ w_o

def _grouped_moe(x, router_w, router_b, w1, w3, w2):
    b, s, d = x.shape
    xt = x.reshape(b * s, d)
    n = xt.shape[0]
    scores = jax.nn.sigmoid((xt @ router_w).astype(jnp.float32))
    biased = scores + router_b.astype(jnp.float32)
    grouped = biased.reshape(n, N_GROUPS, EXPERTS_PER_GROUP)
    group_score = jnp.sum(lax.top_k(grouped, TOP_K)[0], axis=-1)
    group_sel = jnp.argmax(group_score, axis=-1)
    in_group = jnp.arange(N_GROUPS)[None, :] == group_sel[:, None]
    masked = jnp.where(in_group[:, :, None], grouped, -jnp.inf).reshape(n, N_EXPERTS_2)
    _, expert_idx = lax.top_k(masked, TOP_K)
    sel = jnp.take_along_axis(scores, expert_idx, axis=-1)
    gates = sel / jnp.sum(sel, axis=-1, keepdims=True)
    gate_dense = jnp.sum(jax.nn.one_hot(expert_idx, N_EXPERTS_2, dtype=jnp.float32) * gates[..., None], axis=1)
    out = jnp.zeros_like(xt)
    for e in range(N_EXPERTS_2):
        hid = jax.nn.silu(xt @ w1[e]) * (xt @ w3[e])
        out = out + gate_dense[:, e, None].astype(xt.dtype) * (hid @ w2[e])
    return out.reshape(b, s, d)

def second_inputs(seed: int = 0) -> dict:
    key = jax.random.key(seed)
    ks = jax.random.split(key, 26)
    f32 = jnp.float32

    def nrm(k, shape, scale):
        return jax.random.normal(k, shape, f32) * scale

    d = D_MODEL
    return {
        'x': nrm(ks[0], (BATCH, SEQ, d), 1.0),
        'mem': nrm(ks[1], (BATCH, MEM_LEN, d), 1.0),
        'ln_in_g': 1.0 + nrm(ks[2], (d,), 0.02),
        'ln_in_b': nrm(ks[3], (d,), 0.02),
        'w_in': nrm(ks[4], (DEPTH_2, d, IN_W), d ** -0.5),
        'fox_fb': jax.random.uniform(ks[5], (DEPTH_2, FOX_HEADS), f32, 1.0, 3.0),
        'lam_q1': nrm(ks[6], (DEPTH_2, DIFF_QK_DIM), 0.1),
        'lam_k1': nrm(ks[7], (DEPTH_2, DIFF_QK_DIM), 0.1),
        'lam_q2': nrm(ks[8], (DEPTH_2, DIFF_QK_DIM), 0.1),
        'lam_k2': nrm(ks[9], (DEPTH_2, DIFF_QK_DIM), 0.1),
        'diff_norm_g': 1.0 + nrm(ks[10], (DEPTH_2, DIFF_V_DIM), 0.02),
        'hgrn_lb': nrm(ks[11], (DEPTH_2, HGRN_W), 0.1),
        'hgrn_norm_g': 1.0 + nrm(ks[12], (DEPTH_2, HGRN_DIM), 0.02),
        'w_out': nrm(ks[13], (DEPTH_2, MIX_W, d), BETA * MIX_W ** -0.5),
        'mem_wq': nrm(ks[14], (DEPTH_2, d, d), d ** -0.5),
        'mem_wk': nrm(ks[15], (DEPTH_2, d, d), d ** -0.5),
        'mem_wv': nrm(ks[16], (DEPTH_2, d, d), d ** -0.5),
        'mem_wo': nrm(ks[17], (DEPTH_2, d, d), BETA * d ** -0.5),
        'router_w': nrm(ks[18], (d, N_EXPERTS_2), d ** -0.5),
        'router_b': nrm(ks[19], (N_EXPERTS_2,), 0.01),
        'w1': nrm(ks[20], (DEPTH_2, N_EXPERTS_2, d, EXPERT_FF), d ** -0.5),
        'w3': nrm(ks[21], (DEPTH_2, N_EXPERTS_2, d, EXPERT_FF), d ** -0.5),
        'w2': nrm(ks[22], (DEPTH_2, N_EXPERTS_2, EXPERT_FF, d), BETA * EXPERT_FF ** -0.5),
        'ln_g': 1.0 + nrm(ks[23], (DEPTH_2, 3, d), 0.02),
        'ln_b': nrm(ks[24], (DEPTH_2, 3, d), 0.02),
    }

def second_block(x, mem, ln_in_g, ln_in_b, w_in, fox_fb, lam_q1, lam_k1, lam_q2, lam_k2,
              diff_norm_g, hgrn_lb, hgrn_norm_g, w_out, mem_wq, mem_wk, mem_wv, mem_wo,
              router_w, router_b, w1, w3, w2, ln_g, ln_b):
    lbs = jax.nn.softmax(hgrn_lb.astype(jnp.float32), axis=0)
    lbs = jnp.cumsum(lbs, axis=0) - lbs[0]
    h = _layer_norm(x, ln_in_g, ln_in_b)
    for i in range(DEPTH_2):
        lam_init = 0.8 - 0.6 * math.exp(-0.3 * i)
        y = _hybrid_mixer(h, w_in[i], fox_fb[i], lam_q1[i], lam_k1[i], lam_q2[i], lam_k2[i],
                          lam_init, diff_norm_g[i], jnp.maximum(lbs[i], 0.0), hgrn_norm_g[i], w_out[i])
        h = _layer_norm(ALPHA * h + y, ln_g[i, 0], ln_b[i, 0])
        y = _memory_attention(h, mem, mem_wq[i], mem_wk[i], mem_wv[i], mem_wo[i])
        h = _layer_norm(ALPHA * h + y, ln_g[i, 1], ln_b[i, 1])
        y = _grouped_moe(h, router_w, router_b, w1[i], w3[i], w2[i])
        h = _layer_norm(ALPHA * h + y, ln_g[i, 2], ln_b[i, 2])
    return h


def setup_inputs(seed=0):
    out = dict(first_inputs(seed))
    for name, value in second_inputs(seed + 1).items():
        if name != "x":
            out[name + "_2"] = value
    return out


def reference(
    x, mem, ev_norm_mix, ev_w_in, ev_conv_a, ev_pool_w, ev_pool_scale, ev_w_out, ev_norm_ffn,
    ev_ffn_gu, ev_ffn_down, od_norm_mix, od_pw1_w, od_pw1_b, od_dw_w, od_dw_b, od_ln_g, od_ln_b,
    od_pw2_w, od_pw2_b, od_norm_moe, od_router, od_moe_gu, od_moe_down, xa_norm, xa_norm_mem,
    xa_wq, xa_wkv, xa_wo, final_norm, mem_2, ln_in_g_2, ln_in_b_2, w_in_2, fox_fb_2, lam_q1_2,
    lam_k1_2, lam_q2_2, lam_k2_2, diff_norm_g_2, hgrn_lb_2, hgrn_norm_g_2, w_out_2, mem_wq_2,
    mem_wk_2, mem_wv_2, mem_wo_2, router_w_2, router_b_2, w1_2, w3_2, w2_2, ln_g_2, ln_b_2,
):
    x = first_block(
        x, mem, ev_norm_mix, ev_w_in, ev_conv_a, ev_pool_w, ev_pool_scale, ev_w_out,
        ev_norm_ffn, ev_ffn_gu, ev_ffn_down, od_norm_mix, od_pw1_w, od_pw1_b, od_dw_w, od_dw_b,
        od_ln_g, od_ln_b, od_pw2_w, od_pw2_b, od_norm_moe, od_router, od_moe_gu, od_moe_down,
        xa_norm, xa_norm_mem, xa_wq, xa_wkv, xa_wo, final_norm,
    )
    return second_block(
        x, mem_2, ln_in_g_2, ln_in_b_2, w_in_2, fox_fb_2, lam_q1_2, lam_k1_2, lam_q2_2,
        lam_k2_2, diff_norm_g_2, hgrn_lb_2, hgrn_norm_g_2, w_out_2, mem_wq_2, mem_wk_2,
        mem_wv_2, mem_wo_2, router_w_2, router_b_2, w1_2, w3_2, w2_2, ln_g_2, ln_b_2,
    )


_drawn_inputs = setup_inputs


def setup_inputs(seed=0):
    import zlib

    import numpy as np

    out = dict(_drawn_inputs(seed))
    spreads = {}
    factors = {'xa_norm': 5.349,
     'lam_q2_2': 4.048,
     'lam_k2_2': 6.62,
     'diff_norm_g_2': 10.045,
     'hgrn_norm_g_2': 8.0,
     'fox_fb_2': 3.204,
     'lam_q1_2': 5.918,
     'lam_k1_2': 2.672}
    for name, (base, spread) in spreads.items():
        noise = np.random.default_rng([zlib.crc32(name.encode()), seed]).standard_normal(out[name].shape)
        drawn = base * np.exp(spread * noise) if base else spread * noise
        out[name] = jnp.asarray(drawn.astype(out[name].dtype))
    for name, factor in factors.items():
        out[name] = (out[name] * factor).astype(out[name].dtype)
    return out
```

```python
from contextlib import ExitStack

import numpy as np

import concourse.bass as bass
from concourse import mybir

F32 = mybir.dt.float32
I32 = mybir.dt.int32
ALU = mybir.AluOpType
ACT = mybir.ActivationFunctionType
X = mybir.AxisListType.X

P = 128
T = 256
HALVES = T // P
D = 1024
KC = D // P
PANEL = 512
SLOTS = 7
MOE2_SLOTS = 6
D_FF = 2816
EPS, LN_EPS = 1e-6, 1e-5
ALPHA = 2.0 ** 0.25
LAM_INIT = 0.2
WINDOWS = (2, 4, 8, 16)
CONV = 31
MASKED = -1e30
REMOVED = 3e38
HEAD_ORDER = (0, 2, 1, 3)

CONST_COLS = {}


def constant_table():
    r = np.arange(P)
    parts = []

    def put(name, a):
        CONST_COLS[name] = (sum(p.shape[1] for p in parts), a.shape[1])
        parts.append(np.asarray(a, np.float32))

    put("ident", np.eye(P))
    put("ones", np.ones((P, P)))
    put("upto", r[:, None] <= r[None, :])
    put("before", r[:, None] < r[None, :])
    put("iota", np.broadcast_to(r[None, :], (P, P)))
    resident = sum(p.shape[1] for p in parts)
    for lv in range(7):
        m = 1 << lv
        start = r // (2 * m) * (2 * m)
        border = start + m - 1
        late = r % (2 * m) >= m
        span = np.where(late[None, :], (r[:, None] > border[None, :]) & (r[:, None] <= r[None, :]),
                        (r[:, None] > r[None, :]) & (r[:, None] <= border[None, :]))
        put(f"span{lv}", span)
    put("after", r[:, None] > r[None, :])
    for lv in range(7):
        m = 1 << lv
        put(f"pair{lv}", (r[:, None] // (2 * m) == r[None, :] // (2 * m))
            & (r[:, None] % (2 * m) < m) & (r[None, :] % (2 * m) >= m))
    q, k = np.arange(T), np.arange(T)
    for name, ok in (("causal", k[None, :] <= q[:, None]), ("chunked", k[None, :] // 64 <= q[:, None] // 64)):
        a = np.where(ok, 0.0, MASKED).reshape(HALVES, P, T).transpose(1, 0, 2).reshape(P, HALVES * T)
        put(name, a)
    inv = []
    for w in WINDOWS:
        lo = np.maximum(q - w // 2, 0)
        hi = np.minimum(q + w - 1 - w // 2, T - 1) + 1
        inv.append(1.0 / (hi - lo).astype(np.float32))
    put("window", np.broadcast_to(np.concatenate(inv)[None], (P, len(WINDOWS) * T)))
    return np.concatenate(parts, 1), resident


CONSTANTS, RESIDENT = constant_table()

VECTORS = [("ev_norm_mix", 8), ("ev_conv_a", 12), ("ev_pool_scale", 4), ("ev_norm_ffn", 8), ("od_norm_mix", 8),
           ("od_pw1_b", 16), ("od_dw_b", 8), ("od_ln_g", 8), ("od_ln_b", 8), ("od_norm_moe", 8),
           ("xa_norm", 16), ("xa_norm_mem", 16), ("od_dw_w", 248)]
VEC_AT = {}
for _name, _rows in VECTORS:
    VEC_AT[_name] = sum(r for _, r in VECTORS[:len(VEC_AT)])
VEC_TILES = -(-sum(r for _, r in VECTORS) // P)
VEC_ROWS = sum(r for _, r in VECTORS)
VEC_LOADS = sum((VEC_AT[n] + r - 1) // P - VEC_AT[n] // P + 1 for n, r in VECTORS)

UNITS = []
UNIT = {}


def _unit(name, weight, c0, n, columns, src, layer=0):
    UNIT[name] = len(UNITS)
    UNITS.append((weight, layer, c0, n, columns, src))


def _attention(tag, layer, wk, wv, wq, wo, v0):
    for j in range(2):
        _unit(f"{tag}k{j}", wk, j * PANEL, PANEL, True, "memory", layer)
    for j in range(2):
        _unit(f"{tag}v{j}", wv, v0 + j * PANEL, PANEL, False, "memory", layer)
    for j in range(2):
        _unit(f"{tag}q{j}", wq, j * PANEL, PANEL, True, "x", layer)
    for j in range(2):
        _unit(f"{tag}o{j}", wo, j * PANEL, PANEL, False, "attended", layer)


for _j, _n in enumerate(("h", "gb", "gc", "u")):
    _unit("in_" + _n, "ev_w_in", _j * PANEL, PANEL, True, "x")
for _j in range(2):
    _unit(f"mix{_j}", "ev_w_out", _j * PANEL, PANEL, False, "mixed")
_attention("A", 0, "xa_wkv", "xa_wkv", "xa_wq", "xa_wo", D)
FFN_AT = len(UNITS)
for _j in range(2):
    _unit(f"gate{_j}", "od_pw1_w", D + _j * PANEL, PANEL, True, "x")
    _unit(f"value{_j}", "od_pw1_w", _j * PANEL, PANEL, True, "x")
for _j in range(2):
    _unit(f"pw2_{_j}", "od_pw2_w", _j * PANEL, PANEL, False, "conformed")
_attention("B", 1, "xa_wkv", "xa_wkv", "xa_wq", "xa_wo", D)
MOE1_AT = len(UNITS)
_unit("fqk", "w_in_2", 0, 512, True, "x")
_unit("dqk", "w_in_2", 772, 512, True, "x")
_unit("hq", "w_in_2", 1540, 512, True, "x")
_unit("fv", "w_in_2", 512, 260, False, "x")
_unit("dv", "w_in_2", 1284, 256, False, "x")
_unit("hf", "w_in_2", 2052, 512, False, "x")
_unit("hi", "w_in_2", 2564, 512, False, "x")
_unit("hg", "w_in_2", 3076, 512, False, "x")
for _j in range(2):
    _unit(f"out{_j}", "w_out_2", _j * PANEL, PANEL, False, "x")
_attention("C", 0, "mem_wk_2", "mem_wv_2", "mem_wq_2", "mem_wo_2", 0)
FFN_TURNS = D_FF // T

MOES = {
    1: dict(groups=8, members=1, chunks=7, slots=SLOTS, experts=8),
    2: dict(groups=4, members=4, chunks=1, slots=MOE2_SLOTS, experts=16),
}


def program(nc, ins, const_in, out):
    ctx = ExitStack()
    with ctx:
        def sb(name, shape, dt=F32):
            return ctx.enter_context(nc.sbuf_tensor(name, shape, dt))

        sems = {}

        def S(name):
            if name not in sems:
                sems[name] = ctx.enter_context(nc.semaphore(name))
            return sems[name]

        ring = sb("ring", [P, SLOTS, KC * PANEL])
        const = sb("const", [P, RESIDENT])
        H = sb("H", [P, HALVES, D])
        XS = sb("XS", [P, HALVES, D])
        XT = sb("XT", [P, KC, T])
        work = sb("work", [P, 12 * 1024])
        brow = sb("brow", [P, 2, D])
        cols = sb("cols", [P, VEC_TILES * P])
        small = sb("small", [P, 512])
        count = sb("count", [P, 2], I32)
        sq_junk = sb("squares", [P, D])
        ps = ctx.enter_context(nc.psum_tensor("ps", [P, 8, 512], F32))

        def c_(name):
            a, n = CONST_COLS[name]
            if a >= RESIDENT:
                return XT[:, :, :].rearrange("p k t -> p (k t)")[:, a - RESIDENT:a - RESIDENT + n]
            return const[:, a:a + n]

        def w_(off, *shape):
            n = int(np.prod(shape))
            v = work[:, off:off + n]
            if len(shape) == 2:
                return v.rearrange("p (a b) -> p a b", b=shape[1])
            if len(shape) == 3:
                return v.rearrange("p (a b c) -> p a b c", b=shape[1], c=shape[2])
            return v

        small_top = [0]

        def sm(*shape):
            n = int(np.prod(shape))
            v = small[:, small_top[0]:small_top[0] + n]
            small_top[0] += n
            assert small_top[0] <= 512
            if len(shape) == 2:
                return v.rearrange("p (a b) -> p a b", b=shape[1])
            return v

        def vec(name, r=0):
            a = VEC_AT[name] + r
            return cols[:, a:a + 1]

        IDENT, ONES = c_("ident"), c_("ones")
        prob = {n: w_(8192 if n in (3, 4) else 0, 2, 4, T) for n in range(1, 6)}
        ssq, var, std, rstd = sm(2), sm(2), sm(2), sm(2)
        mean = sm(2)
        mx, nbias, den, rden = sm(8), sm(8), sm(8), sm(8)
        lam4 = sm(4, 32)
        lamp, lame, nlam = sm(2), sm(2), sm(1)
        dgain = sm(64)
        foxb = sm(4)
        ffl, ffa, logf_fox = sm(2, 4), sm(2, 4), sm(2, 4)
        dss, dstd, drs = sm(2, 4), sm(2, 4), sm(2, 4)
        rbias = sm(16)
        hgain = c_("ident")
        big_small = sb("big_small", [P, 640])
        hgain = big_small[:, 0:128]
        router = big_small[:, 128:256].rearrange("p (k e) -> p k e", e=16)
        LG = big_small[:, 256:288].rearrange("p (a e) -> p a e", e=16)
        BI = big_small[:, 288:320].rearrange("p (a e) -> p a e", e=16)
        TA = big_small[:, 320:352].rearrange("p (a e) -> p a e", e=16)
        O0 = big_small[:, 352:384].rearrange("p (a e) -> p a e", e=16)
        O1 = big_small[:, 384:416].rearrange("p (a e) -> p a e", e=16)
        CB = big_small[:, 416:480].rearrange("p (a e) -> p a e", e=32)
        RK = big_small[:, 480:512].rearrange("p (a e) -> p a e", e=16)
        SEL = big_small[:, 512:528].rearrange("p (a e) -> p a e", e=8)
        V0, V1 = big_small[:, 528:536], big_small[:, 536:544]
        VI = big_small[:, 544:552]
        IOM = big_small[:, 552:568]
        PAIRW = big_small[:, 568:574].rearrange("p (k a) -> p k a", a=2)
        CMAX = big_small[:, 574:575]
        TOT = big_small[:, 576:584]
        router1 = sb("router1", [P, KC, 8])
        poolw = w_(11264, 4, P)

        sources = {"x": XT, "memory": w_(2048, KC, T), "mixed": w_(6144, KC, T), "attended": w_(10240, KC, T),
                   "conformed": w_(10240, KC, T)}
        PAIRS = [ps[:, 0:2, :], ps[:, 2:4, :]]

        def k_major(w, layer, c0, n):
            return w[layer, :, c0:c0 + n].rearrange("(k p) n -> p k n", p=P)

        panels = []
        unit_panel, ffn_panel = {}, {}
        for u in range(len(UNITS) + 1):
            if u == FFN_AT:
                gu, dn = ins["ev_ffn_gu"], ins["ev_ffn_down"]
                for f in range(FFN_TURNS):
                    ffn_panel["gu", f] = len(panels)
                    panels.append(([((0, 256), k_major(gu, 0, f * T, T)), ((256, 256), k_major(gu, 0, D_FF + f * T, T))],
                                   "ffn_hidden_products", f + 1))
                    ffn_panel["down", f] = len(panels)
                    panels.append(([("rows", dn[0, f * T:(f + 1) * T, :].rearrange("(k p) n -> p k n", p=P))],
                                   "ffn_down_products", f + 1))
            if u == MOE1_AT:
                moe1_panel = len(panels)
            if u == len(UNITS):
                break
            weight, layer, c0, n, columns, _ = UNITS[u]
            unit_panel[u] = len(panels)
            panels.append(([((0, n), k_major(ins[weight], layer, c0, n))], f"unit_ready{u % 2}", u // 2 + 1))

        def slot(i):
            return (i - moe1_panel) % SLOTS if i >= moe1_panel else i % SLOTS

        landed, landed_count = [], {}
        for i, (pieces, _, _) in enumerate(panels):
            landed_count[slot(i)] = landed_count.get(slot(i), 0) + 16 * len(pieces)
            landed.append((slot(i), landed_count[slot(i)]))

        def slot_kn(i):
            return ring[:, i, :].rearrange("p (k n) -> p k n", n=PANEL)

        def slot_rows(i):
            return ring[:, i, :].rearrange("p (k n) -> p k n", n=D)

        def wait_panel(eng, i):
            s, v = landed[i]
            eng.wait_ge(S(f"landed{s}"), v)

        def unit_ready(eng, u):
            eng.wait_ge(S(f"unit_ready{u % 2}"), u // 2 + 1)

        class Steps:

            def __init__(self, eng, sem, base=0):
                self.eng, self.sem, self.base, self.n = eng, sem, base, 0

            def __call__(self, ins):
                self.n += 1
                ins.then_inc(self.sem, 1)
                self.eng.wait_ge(self.sem, self.base + self.n)

        block = ctx.enter_context(nc.Block())

        def moe_sem(k, name):
            return S(f"moe{k}_{name}")

        @block.sync
        def _(sync):
            def load(i, wait):
                pieces, sem, value = panels[i]
                if wait:
                    sync.wait_ge(S(panels[i - SLOTS][1]), panels[i - SLOTS][2])
                for where, src in pieces:
                    n = src.shape[2]
                    if where == "rows":
                        dst = slot_rows(slot(i))[:, 0:src.shape[1], :]
                    else:
                        dst = slot_kn(slot(i))[:, :, where[0]:where[0] + n]
                    sync.dma_start(dst, src).then_inc(S(f"landed{slot(i)}"), 16)

            def experts(k, gu_parts, down):
                c = MOES[k]
                ring_slots, per_group = c["slots"], 3 * c["members"] * c["chunks"]
                sync.sem_inc(moe_sem(k, "slots_free"), ring_slots)

                def group(g, turn):
                    j = 0
                    for m in range(c["members"]):
                        for ch in range(c["chunks"]):
                            for part in range(3):
                                s = j % ring_slots
                                sync.wait_ge(moe_sem(k, "slots_free"), turn * per_group + (j + 1))
                                src = gu_parts[part](g, m, ch) if part < 2 else down(g, m, ch)
                                dst = slot_kn(s) if part < 2 else slot_rows(s)
                                sync.dma_start(dst, src).then_inc(moe_sem(k, f"landed{s}"), 16)
                                j += 1

                with sync.Fori(0, c["groups"]) as g:
                    group(g, g)
                sync.wait_ge(moe_sem(k, "turns_ready"), 1)
                turns = sync.value_load(count[0:1, k - 1:k], min_val=c["groups"], max_val=2 * c["groups"])
                with sync.If(turns > c["groups"]):
                    with sync.Fori(0, c["groups"]) as g:
                        group(g, g + c["groups"])
                with sync.Else():
                    sync.nop()
                if k == 1:
                    sync.wait_ge(moe_sem(k, "slots_free"), turns * per_group + ring_slots)

            n_dense = moe1_panel
            for i in range(n_dense):
                load(i, i >= SLOTS)
            for i in range(moe1_panel - SLOTS, moe1_panel):
                sync.wait_ge(S(panels[i][1]), panels[i][2])
            gu1, dn1 = ins["od_moe_gu"], ins["od_moe_down"]
            F1 = 7 * PANEL

            def gu1_src(part):
                return lambda g, m, ch: gu1[0, bass.ds(g, 1), :, part * F1 + ch * PANEL:part * F1 + (ch + 1) * PANEL]\
                    .rearrange("a (k p) n -> p (a k) n", p=P)

            experts(1, (gu1_src(0), gu1_src(1)),
                    lambda g, m, ch: dn1[0, bass.ds(g, 1), ch * PANEL:(ch + 1) * PANEL, :]
                    .rearrange("a (k p) n -> p (a k) n", p=P))
            for i in range(moe1_panel, len(panels)):
                load(i, i - SLOTS >= moe1_panel)
            for i in range(len(panels) - SLOTS, len(panels)):
                sync.wait_ge(S(panels[i][1]), panels[i][2])

            def expert2(w):
                v = w[0].rearrange("(g m) a b -> g m a b", m=4)
                return lambda g, m, ch: v[bass.ds(g, 1), m, :, :].rearrange("a (k p) n -> p (a k) n", p=P)

            experts(2, (expert2(ins["w1_2"]), expert2(ins["w3_2"])), expert2(ins["w2_2"]))

        @block.gpsimd
        def _(pool):
            pool.dma_start(H[:, :, :], ins["x"][0].rearrange("(a p) d -> p a d", p=P)).then_inc(S("x_loaded"), 16)
            vrows = w_(10240, VEC_TILES, P)
            for name, rows in VECTORS:
                v = ins[name]
                flat = v.rearrange("a (r q) -> (a r) q", q=P) if len(v.shape) == 2 else \
                    v.rearrange("a k (r q) -> (a k r) q", q=P)
                at, done = VEC_AT[name], 0
                while done < rows:
                    t, r = divmod(at + done, P)
                    n = min(rows - done, P - r)
                    pool.dma_start(vrows[r:r + n, t, :], flat[done:done + n, :]).then_inc(S("vectors_loaded"), 16)
                    done += n
            pool.dma_start(const[:, :], const_in[:, 0:RESIDENT]).then_inc(S("const_loaded"), 16)
            a, n = CONST_COLS["window"]
            pool.dma_start(w_(8192, 4 * T), const_in[:, a:a + n]).then_inc(S("window_loaded"), 16)
            pool.dma_start(poolw, ins["ev_pool_w"][0].rearrange("g c d -> c g d")).then_inc(S("poolw_loaded"), 16)
            pool.dma_start(router1[:, :, :], ins["od_router"][0].rearrange("(k p) e -> p k e", p=P)).then_inc(S("small_loaded"), 16)
            pool.dma_start(router, ins["router_w_2"].rearrange("(k p) e -> p k e", p=P)).then_inc(S("small_loaded"), 16)
            for dst, src in ((rbias, ins["router_b_2"]), (foxb, ins["fox_fb_2"][0]), (dgain, ins["diff_norm_g_2"][0]),
                             (hgain, ins["hgrn_norm_g_2"][0]), (lam4[:, 0, :], ins["lam_q1_2"][0]),
                             (lam4[:, 1, :], ins["lam_k1_2"][0]), (lam4[:, 2, :], ins["lam_q2_2"][0]),
                             (lam4[:, 3, :], ins["lam_k2_2"][0])):
                pool.dma_start(dst, src.partition_broadcast(P)).then_inc(S("small_loaded"), 16)

            def memory(n, name):
                if n == 0:
                    pool.wait_ge(S("mixer_finished"), 1)
                elif n == 1:
                    pool.wait_ge(S("conv_finished"), 1)
                else:
                    pool.wait_ge(S("hybrid_finished"), 1)
                pool.dma_start(w_(0, HALVES, D), ins[name][0].rearrange("(a p) d -> p a d", p=P)).then_inc(S("memory_loaded"), 16)

            loads = {0: 0, 1: 0}

            def row(b, src):
                if loads[b]:
                    pool.wait_ge(S(f"brow{b}_used"), loads[b])
                loads[b] += 1
                pool.dma_start(brow[:, b, :], src).then_inc(S(f"brow{b}_loaded"), 16)

            row(0, ins["od_pw2_b"][0].partition_broadcast(P))
            row(1, ins["final_norm"].partition_broadcast(P))
            memory(0, "mem")
            memory(1, "mem")
            row(0, ins["ln_in_g_2"].partition_broadcast(P))
            row(1, ins["ln_in_b_2"].partition_broadcast(P))
            a = CONST_COLS["causal"][0]
            row(0, const_in[:, a:a + D])
            pool.wait_ge(S("fox_scored"), 1)
            pool.dma_start(XT[:, :, :].rearrange("p k t -> p (k t)")[:, 0:a - RESIDENT], const_in[:, RESIDENT:a])\
                .then_inc(S("levels_loaded"), 16)
            row(1, ins["ln_g_2"][0, 0].partition_broadcast(P))
            row(0, ins["ln_b_2"][0, 0].partition_broadcast(P))
            memory(2, "mem_2")
            for j in (1, 2):
                row(1, ins["ln_g_2"][0, j].partition_broadcast(P))
                row(0, ins["ln_b_2"][0, j].partition_broadcast(P))
            pool.wait_ge(S("h_final"), 1)
            pool.dma_start(out[0].rearrange("(a p) d -> p a d", p=P), H[:, :, :]).then_inc(S("out_stored"), 16)
            pool.wait_ge(S("out_stored"), 16)

        @block.tensor
        def _(pe):
            mm = nc.tensor.matmul
            seen = {"turn": 0}

            def project(name):
                u = UNIT[name]
                _, _, _, n, columns, src = UNITS[u]
                x, pair = sources[src], PAIRS[u % 2]
                if u >= 2:
                    pe.wait_ge(S(f"unit_read{u % 2}"), u // 2)
                wait_panel(pe, unit_panel[u])
                w = slot_kn(slot(unit_panel[u]))
                if columns:
                    for fb in range(n // P):
                        for kc in range(KC):
                            last = mm(pair[:, fb // 2, fb % 2 * T:fb % 2 * T + T], w[:, kc, fb * P:(fb + 1) * P],
                                      x[:, kc, :], start=(kc == 0), stop=(kc == KC - 1))
                else:
                    for tc in range(HALVES):
                        for kc in range(KC):
                            last = mm(pair[:, tc, 0:n], x[:, kc, tc * P:(tc + 1) * P], w[:, kc, 0:n],
                                      start=(kc == 0), stop=(kc == KC - 1))
                last.then_inc(S(f"unit_ready{u % 2}"), 1)

            def turn(src, ready, n):
                pe.wait_ge(S(ready), n)
                if seen["turn"]:
                    pe.wait_ge(S("columns_by_act"), seen["turn"])
                    pe.wait_ge(S("columns_by_vector"), seen["turn"])
                seen["turn"] += 1
                for kc in range(KC):
                    for tc in range(HALVES):
                        o = kc % 2 * T + tc * P
                        last = nc.tensor.transpose(ps[:, 4 + kc // 2, o:o + P], src[:, tc, kc * P:(kc + 1) * P], IDENT)
                last.then_inc(S("turned"), 1)

            def columns_ready():
                pe.wait_ge(S("columns_by_act"), seen["turn"])
                pe.wait_ge(S("columns_by_vector"), seen["turn"])

            def turn_probabilities(n):
                pe.wait_ge(S("probs_ready"), n)
                pr = prob[n]
                for h in range(4):
                    for mc in range(2):
                        for tc in range(2):
                            j = h * 2 + mc
                            last = nc.tensor.transpose(ps[:, 4 + j // 2, j % 2 * T + tc * P:j % 2 * T + (tc + 1) * P],
                                                       pr[:, tc, h, mc * P:(mc + 1) * P], IDENT)
                last.then_inc(S("probs_turned"), 1)
                pe.wait_ge(S("probsT_by_act"), n)
                pe.wait_ge(S("probsT_by_vector"), n)

            def attention(tag, n, prepare):
                prepare()
                n_probs = n - (tag == "C")
                for j in range(2):
                    project(f"{tag}k{j}")
                for j in range(2):
                    project(f"{tag}v{j}")
                turn({"A": XS, "B": XS, "C": H}[tag], {"A": "xs_ready", "B": "xs_ready", "C": "h_ready"}[tag],
                     {"A": 3, "B": 7, "C": 2}[tag])
                columns_ready()
                for j in range(2):
                    project(f"{tag}q{j}")
                QT, KT, V, PT = w_(8192, KC, T), w_(4096, KC, T), w_(6144, HALVES, D), w_(2048, KC, T)
                for name in (f"{tag}k1", f"{tag}v1", f"{tag}q0", f"{tag}q1"):
                    u = UNIT[name]
                    pe.wait_ge(S(f"unit_read{u % 2}"), u // 2 + 1)
                for tc in range(2):
                    for h in range(4):
                        j = tc * 4 + h
                        for c in range(2):
                            last = mm(ps[:, 4 + j // 2, j % 2 * T:j % 2 * T + T], QT[:, 2 * h + c, tc * P:(tc + 1) * P],
                                      KT[:, 2 * h + c, :], start=(c == 0), stop=(c == 1))
                last.then_inc(S("scores_ready"), 1)
                turn_probabilities(n_probs)
                for f in range(KC):
                    for mc in range(2):
                        last = mm(ps[:, 4 + f // 2, f % 2 * T:f % 2 * T + T], V[:, mc, f * P:(f + 1) * P],
                                  PT[:, f // 2 * 2 + mc, :], start=(mc == 0), stop=(mc == 1))
                last.then_inc(S("attended"), 1)
                k = "ABC".index(tag) + 1
                pe.wait_ge(S("attended_by_act"), k)
                pe.wait_ge(S("attended_by_vector"), k)
                for j in range(2):
                    project(f"{tag}o{j}")

            pe.wait_ge(S("vectors_loaded"), 16 * VEC_LOADS)
            pe.wait_ge(S("const_loaded"), 16)
            for t in range(VEC_TILES):
                n = min(P, VEC_ROWS - t * P)
                last = nc.tensor.transpose(ps[:, 4, t * P:t * P + n], w_(10240, VEC_TILES, P)[0:n, t, :], IDENT[0:n, 0:n])
            last.then_inc(S("vectors_turned"), 1)
            pe.wait_ge(S("cols_ready"), 1)
            turn(XS, "xs_ready", 1)
            columns_ready()
            for n in ("h", "gb", "gc", "u"):
                project("in_" + n)
            pe.wait_ge(S("poolw_loaded"), 16)
            pe.wait_ge(S("pooled"), 1)
            for g in range(4):
                last = mm(ps[:, 4 + g // 2, g % 2 * T:g % 2 * T + T], poolw[:, g, :], w_(5120, 4, T)[:, g, :],
                          start=True, stop=True)
            last.then_inc(S("pool_mixed"), 1)
            pe.wait_ge(S("mixed_by_act"), 1)
            pe.wait_ge(S("mixed_by_vector"), 1)
            for j in range(2):
                project(f"mix{j}")
            attention("A", 1, lambda: (turn(w_(0, HALVES, D), "xs_ready", 2), columns_ready()))
            turn(XS, "xs_ready", 4)
            columns_ready()
            for u in (FFN_AT - 1, FFN_AT - 2):
                pe.wait_ge(S(f"unit_read{u % 2}"), u // 2 + 1)

            def hidden(f):
                i = ffn_panel["gu", f]
                wait_panel(pe, i)
                w, pair = slot_kn(slot(i)), PAIRS[f % 2]
                if f >= 2:
                    pe.wait_ge(S("ffn_hidden"), f - 1)
                for part in range(2):
                    for fb in range(2):
                        for kc in range(KC):
                            c = part * T + fb * P
                            last = mm(pair[:, part, fb * T:(fb + 1) * T], w[:, kc, c:c + P], XT[:, kc, :],
                                      start=(kc == 0), stop=(kc == KC - 1))
                last.then_inc(S("ffn_hidden_products"), 1)

            def down(f):
                i = ffn_panel["down", f]
                wait_panel(pe, i)
                pe.wait_ge(S("ffn_hidden"), f + 1)
                w, hT = slot_rows(slot(i)), w_(512 * (f % 3), 2, T)
                for tc in range(2):
                    for n in range(2):
                        for fb in range(2):
                            last = mm(ps[:, 4 + tc * 2 + n, :], hT[:, fb, tc * P:(tc + 1) * P],
                                      w[:, fb, n * 512:(n + 1) * 512], start=(f == 0 and fb == 0),
                                      stop=(f == FFN_TURNS - 1 and fb == 1))
                last.then_inc(S("ffn_down_products"), 1)

            hidden(0)
            for f in range(1, FFN_TURNS):
                hidden(f)
                down(f - 1)
            down(FFN_TURNS - 1)
            pe.wait_ge(S("ffn_added"), 1)
            turn(XS, "xs_ready", 5)
            columns_ready()
            for j in range(2):
                project(f"gate{j}")
                project(f"value{j}")
            CO, SQ = w_(4096, KC, T), w_(6144, KC, T)
            pe.wait_ge(S("convolved"), 1)
            for kc in range(KC):
                last = mm(ps[:, 4, 0:T], ONES, CO[:, kc, :], start=(kc == 0), stop=(kc == KC - 1))
            last.then_inc(S("feature_sums"), 1)
            pe.wait_ge(S("squared"), 1)
            for kc in range(KC):
                last = mm(ps[:, 5, 0:T], ONES, SQ[:, kc, :], start=(kc == 0), stop=(kc == KC - 1))
            last.then_inc(S("feature_sums"), 1)
            pe.wait_ge(S("conformed"), 1)
            for j in range(2):
                project(f"pw2_{j}")
            attention("B", 2, lambda: (turn(w_(0, HALVES, D), "xs_ready", 6), columns_ready()))

            def route(k, ready, value, src):
                turn(src, ready, value)
                columns_ready()
                pe.wait_ge(S("small_loaded"), 16 * 10)
                E, G = MOES[k]["experts"], MOES[k]["groups"]
                rt = router1 if k == 1 else router
                for tc in range(2):
                    for kc in range(KC):
                        last = mm(ps[:, 4, tc * 16:tc * 16 + E], XT[:, kc, tc * P:(tc + 1) * P], rt[:, kc, :],
                                  start=(kc == 0), stop=(kc == KC - 1))
                last.then_inc(S("logits_ready"), 1)
                pe.wait_ge(S("chosen"), k)
                before = c_("before")
                mm(ps[:, 5, 0:G], before, SEL[:, 0, 0:G], start=True, stop=True)
                mm(ps[:, 5, 8:8 + G], ONES, SEL[:, 0, 0:G], start=True, stop=False)
                mm(ps[:, 5, 8:8 + G], before, SEL[:, 1, 0:G], start=False, stop=True)
                mm(ps[:, 5, 16:16 + G], ONES, SEL[:, 0, 0:G], start=True, stop=False)
                mm(ps[:, 5, 16:16 + G], ONES, SEL[:, 1, 0:G], start=False, stop=True).then_inc(S("ranks_ready"), 1)

            def experts(k, x):
                c = MOES[k]
                M, NS = c["members"], c["slots"]
                halves = 2 * M * c["chunks"]
                per_group = 3 * M * c["chunks"]
                PR, PG, PT = w_(2048, 2, P), w_(2304, 4, 2, P), w_(3328, 2, P)
                XG, Y = w_(0, KC, P), w_(1024, D)
                uses = {s: sum(1 for j in range(per_group) if j % NS == s) for s in range(NS)}
                pe.wait_ge(moe_sem(k, "turns_ready"), 1)
                turns = pe.value_load(count[0:1, k - 1:k], min_val=c["groups"], max_val=2 * c["groups"])
                with pe.Fori(0, turns) as it:
                    pe.wait_ge(moe_sem(k, "picked"), it + 1)
                    pe.wait_ge(moe_sem(k, "added"), it + 1)
                    for m in range(M):
                        for tc in range(2):
                            mm(ps[:, 6, m * P:(m + 1) * P], ONES, PG[:, m, tc, :], start=(tc == 0), stop=(tc == 1))
                    for tc in range(2):
                        nc.tensor.transpose(ps[:, 7, tc * P:(tc + 1) * P], PR[:, tc, :], IDENT)
                    for kc in range(KC):
                        for tc in range(2):
                            last = mm(ps[:, 4 + kc // 4, kc % 4 * P:kc % 4 * P + P], x[:, tc, kc * P:(kc + 1) * P],
                                      PR[:, tc, :], start=(tc == 0), stop=(tc == 1))
                    last.then_inc(moe_sem(k, "gathered"), 1)
                    pe.wait_ge(moe_sem(k, "gathered_by_act"), it + 1)
                    pe.wait_ge(moe_sem(k, "gathered_by_vector"), it + 1)

                    def arrived(j):
                        s = j % NS
                        pe.wait_ge(moe_sem(k, f"landed{s}"), it * (16 * uses[s]) + 16 * (j // NS + 1))
                        return s

                    def hidden(hc):
                        j = 3 * (hc // 2)
                        for part in range(2):
                            s = arrived(j + part)
                            for fb in range(2):
                                o = hc % 2 * T + fb * P
                                for kc in range(KC):
                                    last = mm(ps[:, hc % 2, part * T + fb * P:part * T + (fb + 1) * P],
                                              slot_kn(s)[:, kc, o:o + P], XG[:, kc, :],
                                              start=(kc == 0), stop=(kc == KC - 1))
                        last.then_inc(moe_sem(k, "hidden_products"), 1)

                    def down(hc):
                        s = arrived(3 * (hc // 2) + 2)
                        pe.wait_ge(moe_sem(k, "hidden"), it * halves + (hc + 3))
                        hT = w_(4096 + 256 * (hc % 2), 2, P)
                        for n in range(2):
                            for fb in range(2):
                                last = mm(ps[:, 2 + n, :], hT[:, fb, :],
                                          slot_rows(s)[:, hc % 2 * 2 + fb, n * 512:(n + 1) * 512],
                                          start=(hc == 0 and fb == 0), stop=(hc == halves - 1 and fb == 1))
                        if hc % 2:
                            last.then_inc(moe_sem(k, "slots_free"), 3)

                    hidden(0)
                    for hc in range(1, halves):
                        hidden(hc)
                        down(hc - 1)
                    down(halves - 1)
                    pe.wait_ge(moe_sem(k, "outputs_by_act"), it + 1)
                    pe.wait_ge(moe_sem(k, "outputs_by_vector"), it + 1)
                    for tc in range(2):
                        for n in range(2):
                            last = mm(ps[:, 4 + tc * 2 + n, :], PT[:, tc, :], Y[:, n * 512:(n + 1) * 512],
                                      start=True, stop=True)
                    last.then_inc(moe_sem(k, "scattered"), 1)
                return turns

            route(1, "xs_ready", 8, XS)
            turns = experts(1, XS)
            pe.wait_ge(moe_sem(1, "added"), turns + 1)
            turn(H, "h_ready", 1)
            columns_ready()
            for n in ("fqk", "dqk", "hq", "fv", "dv", "hf", "hi", "hg"):
                project(n)
            FQK, DQK, QH, KH = w_(0, 4, T), w_(1024, 4, T), w_(2048, 4, T), w_(3072, 4, T)
            LF, HI = w_(4096, 2, 512), w_(5120, 2, 512)
            FV, DV = w_(7168, 2, 256), w_(7680, 2, 256)
            PT = w_(10240, KC, T)
            pe.wait_ge(S("fox_log"), 1)
            upto, ones = c_("upto"), ONES
            mm(ps[:, 4, 0:4], upto, logf_fox[:, 0, :], start=True, stop=True)
            mm(ps[:, 4, 4:8], ones, logf_fox[:, 0, :], start=True, stop=False)
            mm(ps[:, 4, 4:8], upto, logf_fox[:, 1, :], start=False, stop=True).then_inc(S("fox_sums"), 1)
            for h in range(4):
                o = ps[:, 6 + h // 2, h % 2 * T:h % 2 * T + T]
                mm(o[:, 0:P], logf_fox[:, 0, h:h + 1].broadcast_to([P, P]), upto, start=True, stop=True)
                mm(o[:, P:T], logf_fox[:, 0, h:h + 1].broadcast_to([P, P]), ones, start=True, stop=False)
                last = mm(o[:, P:T], logf_fox[:, 1, h:h + 1].broadcast_to([P, P]), upto, start=False, stop=True)
            last.then_inc(S("fox_sums"), 1)
            pe.wait_ge(S("fox_bias"), 1)
            pe.wait_ge(S("recurrent_keys"), 1)
            KR = w_(8192, 2, 512)
            for h in range(4):
                for tc in range(2):
                    last = nc.tensor.transpose(ps[:, 4 + h // 2, h % 2 * T + tc * P:h % 2 * T + (tc + 1) * P],
                                               KR[:, tc, h * P:(h + 1) * P], IDENT)
            last.then_inc(S("keys_turned"), 1)
            pe.wait_ge(S("keys_columns"), 1)

            def small_attention(n, scores, v):
                scores()
                turn_probabilities(n)
                for tc in range(2):
                    for place, h in enumerate(HEAD_ORDER):
                        for mc in range(2):
                            last = mm(ps[:, 4, tc * T + h * 64:tc * T + h * 64 + 64], PT[:, place * 2 + mc, tc * P:(tc + 1) * P],
                                      v[:, mc, h * 64:(h + 1) * 64], start=(mc == 0), stop=(mc == 1))
                last.then_inc(S("small_attended"), 1)

            def fox_scores():
                u = UNIT["hg"]
                pe.wait_ge(S(f"unit_read{(u - 1) % 2}"), (u - 1) // 2 + 1)
                pe.wait_ge(S(f"unit_read{u % 2}"), u // 2 + 1)
                for tc in range(2):
                    for place, h in enumerate(HEAD_ORDER):
                        j, p0 = tc * 4 + place, 64 * (h % 2)
                        last = mm(ps[:, 4 + j // 2, j % 2 * T:j % 2 * T + T],
                                  FQK[p0:p0 + 64, h // 2, tc * P:(tc + 1) * P], FQK[p0:p0 + 64, 2 + h // 2, :],
                                  start=True, stop=True)
                last.then_inc(S("scores_ready"), 1)

            def diff_scores(which):
                for tc in range(2):
                    for place, h in enumerate(HEAD_ORDER):
                        j, p0 = tc * 4 + place, 64 * (h % 2) + 32 * which
                        last = mm(ps[:, 4 + j // 2, j % 2 * T:j % 2 * T + T],
                                  DQK[p0:p0 + 32, h // 2, tc * P:(tc + 1) * P], DQK[p0:p0 + 32, 2 + h // 2, :],
                                  start=True, stop=True)
                last.then_inc(S("scores_ready"), 1)

            small_attention(3, fox_scores, FV)
            pe.wait_ge(S("small_read"), 1)

            def both_maps():
                diff_scores(0)
                pe.wait_ge(S("diff_map"), 1)
                diff_scores(1)

            small_attention(4, both_maps, DV)
            pe.wait_ge(S("small_read"), 2)
            E, QE, KE, ST = w_(8192, 4, T), w_(9216, 4, T), w_(10240, 4, T), w_(11264, 8, P)
            for h in range(4):
                for tc in range(2):
                    last = mm(ps[:, h // 2, h % 2 * T + tc * P:h % 2 * T + (tc + 1) * P],
                              KH[:, h, tc * P:(tc + 1) * P], QH[:, h, tc * P:(tc + 1) * P], start=True, stop=True)
            last.then_inc(S("level_scores"), 1)
            pe.wait_ge(S("levels_loaded"), 16)
            for lv in range(8):
                if lv:
                    pe.wait_ge(S("level_exp"), lv)
                for h in range(4):
                    for tc in range(2):
                        sp = c_(f"span{lv}") if lv < 7 else (c_("after") if tc == 0 else upto)
                        last = mm(ps[:, 4 + h // 2, h % 2 * T + tc * P:h % 2 * T + (tc + 1) * P],
                                  LF[:, tc, h * P:(h + 1) * P], sp, start=True, stop=True)
                last.then_inc(S("level_spans"), 1)
                pe.wait_ge(S("level_decayed"), lv + 1)
                pe.wait_ge(S("level_merged"), lv + 1)
                if lv < 7:
                    for h in range(4):
                        for tc in range(2):
                            last = mm(ps[:, h // 2, h % 2 * T + tc * P:h % 2 * T + (tc + 1) * P],
                                      KE[:, h, tc * P:(tc + 1) * P], QE[:, h, tc * P:(tc + 1) * P], start=True, stop=True)
                else:
                    for h in range(4):
                        last = mm(ps[:, 0, h * P:(h + 1) * P], KE[:, h, 0:P], QE[:, h, P:T], start=True, stop=True)
                last.then_inc(S("level_scores"), 1)
            pe.wait_ge(S("level_merged"), 9)
            CR = w_(8192, 4, P)
            for h in range(4):
                v = lambda tc: HI[:, tc, h * P:(h + 1) * P]
                mm(ps[:, 2, h * P:(h + 1) * P], ST[:, 2 * h, :], v(0), start=True, stop=True)
                mm(ps[:, 3, h * P:(h + 1) * P], ST[:, 2 * h + 1, :], v(1), start=True, stop=False)
                last = mm(ps[:, 3, h * P:(h + 1) * P], CR[:, h, :], v(0), start=False, stop=True)
            last.then_inc(S("recurrence_out"), 1)
            turn(XS, "xs_ready", 9)
            columns_ready()
            for j in range(2):
                project(f"out{j}")
            attention("C", 6, lambda: (turn(w_(0, HALVES, D), "memory_loaded", 48), columns_ready()))
            route(2, "h_ready", 3, H)
            experts(2, H)

        @block.scalar
        def _(act):
            A = nc.scalar.activation
            n_ = {"sq": 0, "sqrt": 0, "turn": 0}
            step = Steps(act, S("scalar_step"))

            def squares(src, ready, n):
                act.wait_ge(S(ready), n)
                if n_["sq"]:
                    act.wait_ge(S("variance_ready"), n_["sqrt"])
                n_["sq"] += 1
                step(A(sq_junk[:, :], src[:, 0, :], ACT.Square, accum_out=ssq[:, 0:1]))
                A(sq_junk[:, :], src[:, 1, :], ACT.Square, accum_out=ssq[:, 1:2]).then_inc(S("squares_summed"), 1)

            def root(n=2, src=None, dst=None):
                n_["sqrt"] += 1
                act.wait_ge(S("variance_ready"), n_["sqrt"])
                A(dst if dst is not None else std, src if src is not None else var, ACT.Sqrt).then_inc(S("deviation_ready"), 1)

            def rms(src, ready, n):
                squares(src, ready, n)
                root()

            def columns(dst, gain, banks=(4, 5)):
                n_["turn"] += 1
                act.wait_ge(S("turned"), n_["turn"])
                for kc in range(4):
                    src = ps[:, 4 + kc // 2, kc % 2 * T:kc % 2 * T + T]
                    if gain is None:
                        last = A(dst[:, kc, :], src, ACT.Copy)
                    else:
                        last = A(dst[:, kc, :], src, ACT.Copy, scale=vec(gain[0], gain[1] + kc))
                last.then_inc(S("columns_by_act"), 1)

            def take(name, dst, func=ACT.Copy, **kw):
                u = UNIT[name]
                unit_ready(act, u)
                A(dst, PAIRS[u % 2], func, **kw).then_inc(S(f"unit_read{u % 2}"), 1)

            def take_columns(name, dst):
                u = UNIT[name]
                unit_ready(act, u)
                A(dst, PAIRS[u % 2].rearrange("p a (b t) -> p (a b) t", t=T), ACT.Copy).then_inc(S(f"unit_read{u % 2}"), 1)

            def softmax(n, scale, dst, src_sbuf=None):
                act.wait_ge(S("softmax_bias"), n)
                for j in range(8):
                    src = ps[:, 4 + j // 2, j % 2 * T:j % 2 * T + T] if src_sbuf is None else src_sbuf[:, j // 4, j % 4, :]
                    last = A(dst[:, j // 4, j % 4, :], src, ACT.Exp, bias=nbias[:, j:j + 1], scale=scale,
                             accum_out=den[:, j:j + 1])
                last.then_inc(S("exponentials"), 1)

            def probs_columns(n, dst):
                act.wait_ge(S("probs_turned"), n)
                A(dst[:, 0:4, :], ps[:, 4:6, :].rearrange("p a (b t) -> p (a b) t", t=T), ACT.Copy).then_inc(S("probsT_by_act"), 1)

            def attention(tag, n, gain_mem, gain_x, ready):
                layer = gain_mem
                MT, KT, V, QT, PT, OT = (w_(o, KC, T) for o in (2048, 4096, 6144, 8192, 2048, 10240))
                if tag != "C":
                    rms(w_(0, HALVES, D), "memory_loaded", 16 * ("AB".index(tag) + 1))
                    columns(MT, ("xa_norm_mem", 8 * layer))
                else:
                    columns(MT, None)
                take_columns(f"{tag}k0", KT[:, 0:4, :])
                take(f"{tag}v0", w_(6144, HALVES, D)[:, :, 0:512])
                if tag != "C":
                    rms(H, *ready)
                    columns(XT, ("xa_norm", 8 * layer))
                else:
                    columns(XT, None)
                take_columns(f"{tag}q0", QT[:, 0:4, :])
                softmax(n, 1.0 / 16, w_(0, 2, 4, T))
                probs_columns(n - (tag == "C"), PT)
                act.wait_ge(S("attended"), "ABC".index(tag) + 1)
                A(OT[:, 0:4, :], ps[:, 4:6, :].rearrange("p a (b t) -> p (a b) t", t=T), ACT.Copy).then_inc(S("attended_by_act"), 1)

            act.wait_ge(S("vectors_turned"), 1)
            A(cols[:, 0:VEC_ROWS], ps[:, 4, 0:VEC_ROWS], ACT.Copy).then_inc(S("cols_ready"), 1)
            act.wait_ge(S("cols_ready"), 1)
            rms(H, "x_loaded", 16)
            columns(XT, ("ev_norm_mix", 0))
            take_columns("in_h", w_(0, 4, T))
            take_columns("in_gb", w_(1024, 4, T))
            act.wait_ge(S("pool_mixed"), 1)
            for g in range(4):
                last = A(w_(6144, KC, T)[:, 4 + g, :], ps[:, 4 + g // 2, g % 2 * T:g % 2 * T + T], ACT.Copy,
                         scale=vec("ev_pool_scale", g))
            last.then_inc(S("mixed_by_act"), 1)
            attention("A", 1, 0, 0, ("h_updated", 1))
            rms(H, "h_updated", 2)
            columns(XT, ("ev_norm_ffn", 0))
            for f in range(FFN_TURNS):
                act.wait_ge(S("ffn_hidden_products"), f + 1)
                if f >= 2:
                    act.wait_ge(S("ffn_hidden"), f - 1)
                A(w_(2048 + 512 * (f % 2), 512), PAIRS[f % 2][:, 0, :], ACT.Silu).then_inc(S("ffn_silu"), 1)
            rms(H, "ffn_added", 1)
            columns(XT, ("od_norm_mix", 0))
            for j in range(2):
                u = UNIT[f"gate{j}"]
                unit_ready(act, u)
                if j:
                    act.wait_ge(S("glu"), 1)
                src = PAIRS[u % 2].rearrange("p a (b t) -> p (a b) t", t=T)
                for b in range(4):
                    last = A(w_(0, 4, T)[:, b, :], src[:, b, :], ACT.Sigmoid, bias=vec("od_pw1_b", 8 + 4 * j + b))
                last.then_inc(S(f"unit_read{u % 2}"), 1)
            root(src=w_(8448, T), dst=w_(8704, T))
            act.wait_ge(S("standard"), 1)
            for kc in range(KC):
                last = A(w_(10240, KC, T)[:, kc, :], w_(4096, KC, T)[:, kc, :], ACT.Silu, scale=vec("od_ln_g", kc),
                         bias=vec("od_ln_b", kc))
            last.then_inc(S("conformed"), 1)
            attention("B", 2, 1, 1, ("h_updated", 3))

            def experts(k, gain):
                c = MOES[k]
                M = c["members"]
                halves, per_group = 2 * M * c["chunks"], 3 * M * c["chunks"]
                XG, Y, GB = w_(0, KC, P), w_(1024, D), w_(3584, M, P)
                act.wait_ge(moe_sem(k, "turns_ready"), 1)
                turns = act.value_load(count[0:1, k - 1:k], min_val=c["groups"], max_val=2 * c["groups"])
                with act.Fori(0, turns) as it:
                    act.wait_ge(moe_sem(k, "gathered"), it + 1)
                    for j in range(4):
                        src = ps[:, 5, j * P:(j + 1) * P]
                        if gain:
                            A(XG[:, 4 + j, :], src, ACT.Copy, scale=vec(gain, 4 + j))
                        else:
                            A(XG[:, 4 + j, :], src, ACT.Copy)
                    A(GB, ps[:, 6, 0:M * P].rearrange("p (m t) -> p m t", t=P), ACT.Copy)\
                        .then_inc(moe_sem(k, "gathered_by_act"), 1)
                    for hc in range(halves):
                        act.wait_ge(moe_sem(k, "hidden_products"), it * halves + (hc + 1))
                        act.wait_ge(moe_sem(k, "hidden"), it * halves + (hc + 1))
                        A(w_(4608 + 256 * (hc % 2), T), ps[:, hc % 2, 0:T], ACT.Silu).then_inc(moe_sem(k, "silu"), 1)
                    act.wait_ge(moe_sem(k, "slots_free"), it * per_group + (per_group + c["slots"]))
                    A(Y[:, 0:512], ps[:, 2, :], ACT.Copy).then_inc(moe_sem(k, "outputs_by_act"), 1)

            rms(H, "h_updated", 4)
            columns(XT, ("od_norm_moe", 0))
            act.wait_ge(S("logit_gap"), 1)
            A(PAIRW[:, 1, :], PAIRW[:, 0, :], ACT.Exp).then_inc(S("gap_exp"), 1)
            experts(1, "od_norm_moe")
            rms(H, "moe_done", 1)
            root()
            columns(XT, None)
            take_columns("dqk", w_(1024, 4, T))
            u = UNIT["hq"]
            unit_ready(act, u)
            A(w_(2048, 4, T), PAIRS[u % 2].rearrange("p a (b t) -> p (a b) t", t=T), ACT.Silu).then_inc(S(f"unit_read{u % 2}"), 1)
            act.wait_ge(S("lam_sums"), 1)
            A(lame, lamp, ACT.Exp).then_inc(S("lam_exp"), 1)
            act.wait_ge(S("fox_logits"), 1)
            step(A(ffa, ffl, ACT.Abs))
            step(A(ffa, ffa, ACT.Exp, scale=-1.0))
            A(ffa, ffa, ACT.Ln, bias=1.0).then_inc(S("fox_log1p"), 1)
            HFZ, HFA, KR = w_(9216, 2, 512), w_(4096, 2, 512), w_(8192, 2, 512)
            act.wait_ge(S("forget_logits"), 1)
            step(A(HFA, HFZ, ACT.Abs))
            step(A(HFA, HFA, ACT.Exp, scale=-1.0))
            A(HFA, HFA, ACT.Ln, bias=1.0).then_inc(S("forget_log1p"), 1)
            A(KR, HFZ, ACT.Sigmoid, scale=-1.0).then_inc(S("recurrent_keys"), 1)
            take("hi", w_(5120, 2, 512))
            u = UNIT["hg"]
            unit_ready(act, u)
            A(w_(6144, 2, 512), PAIRS[u % 2], ACT.Silu).then_inc(S(f"unit_read{u % 2}"), 1)
            act.wait_ge(S("keys_turned"), 1)
            A(w_(3072, 4, T), ps[:, 4:6, :].rearrange("p a (b t) -> p (a b) t", t=T), ACT.Copy).then_inc(S("keys_columns"), 1)
            PR, PT = w_(8192, 2, 4, T), w_(10240, KC, T)
            softmax(3, 1.0, PR, PR)
            probs_columns(3, PT)
            softmax(4, 1.0, PR, PR)
            softmax(5, 1.0, w_(10240, 2, 4, T), w_(10240, 2, 4, T))
            probs_columns(4, PT)
            root(src=dss, dst=dstd)
            for lv in range(8):
                act.wait_ge(S("level_spans"), lv + 1)
                if lv:
                    act.wait_ge(S("level_decayed"), lv)
                else:
                    act.wait_ge(S("diff_done"), 1)
                A(w_(8192, 4, T), ps[:, 4:6, :].rearrange("p a (b t) -> p (a b) t", t=T), ACT.Exp).then_inc(S("level_exp"), 1)
            root(src=dss, dst=dstd)
            columns(XT, None)
            root()
            attention("C", 6, 0, 0, None)
            root()
            columns(XT, None)
            act.wait_ge(S("logits_ready"), 2)
            A(LG, ps[:, 4, 0:32].rearrange("p (a e) -> p a e", e=16), ACT.Sigmoid).then_inc(S("router_scores"), 1)
            experts(2, None)
            root()

        @block.vector
        def _(dve):
            V = nc.vector
            step = Steps(dve, S("vector_step"))
            n_ = {"sq": 0, "rt": 0, "xs": 0, "turn": 0, "b0": 0, "b1": 0}
            MUL, ADD, SUB = ALU.mult, ALU.add, ALU.subtract

            def rsqrt(dst=None, src=None):
                n_["rt"] += 1
                dve.wait_ge(S("deviation_ready"), n_["rt"])
                step(V.reciprocal(dst if dst is not None else rstd, src if src is not None else std))

            def rms(src, dst, eps):
                n_["sq"] += 1
                dve.wait_ge(S("squares_summed"), n_["sq"])
                V.tensor_scalar(var, ssq, 1.0 / D, eps, MUL, ADD).then_inc(S("variance_ready"), 1)
                rsqrt()
                for tc in range(2):
                    last = V.tensor_scalar(dst[:, tc, :], src[:, tc, :], rstd[:, tc:tc + 1], None, MUL)
                last.then_inc(S("xs_ready"), 1)

            def columns(dst, gain):
                n_["turn"] += 1
                dve.wait_ge(S("turned"), n_["turn"])
                for kc in range(4, 8):
                    src = ps[:, 4 + kc // 2, kc % 2 * T:kc % 2 * T + T]
                    if gain is None:
                        last = V.tensor_copy(dst[:, kc, :], src)
                    else:
                        last = V.tensor_scalar(dst[:, kc, :], src, vec(gain[0], gain[1] + kc), None, MUL)
                last.then_inc(S("columns_by_vector"), 1)

            def take(name, dst):
                u = UNIT[name]
                unit_ready(dve, u)
                V.tensor_copy(dst, PAIRS[u % 2]).then_inc(S(f"unit_read{u % 2}"), 1)

            def take_columns(name, dst):
                u = UNIT[name]
                unit_ready(dve, u)
                V.tensor_copy(dst, PAIRS[u % 2].rearrange("p a (b t) -> p (a b) t", t=T)).then_inc(S(f"unit_read{u % 2}"), 1)

            def add_unit(name, j, scale=None, signal=None):
                u = UNIT[name]
                unit_ready(dve, u)
                h = H[:, :, j * 512:(j + 1) * 512]
                if scale is None:
                    ins = V.tensor_tensor(h, h, PAIRS[u % 2], ADD)
                else:
                    ins = V.scalar_tensor_tensor(h, h, scale, PAIRS[u % 2], MUL, ADD)
                ins.then_inc(S(f"unit_read{u % 2}"), 1)

            def update_done(name):
                u = UNIT[name]
                for w in (u - 1, u):
                    dve.wait_ge(S(f"unit_read{w % 2}"), w // 2 + 1)

            def use_row(b, last):
                last.then_inc(S(f"brow{b}_used"), 1)
                dve.wait_ge(S(f"brow{b}_used"), n_[f"b{b}"])

            def row(b):
                n_[f"b{b}"] += 1
                dve.wait_ge(S(f"brow{b}_loaded"), 16 * n_[f"b{b}"])
                return brow[:, b, :]

            def layer_norm(signal):
                step(V.tensor_reduce(mean, H[:, :, :], X, ADD))
                step(V.tensor_scalar(mean, mean, 1.0 / D, None, MUL))
                for tc in range(2):
                    last = V.tensor_scalar(H[:, tc, :], H[:, tc, :], mean[:, tc:tc + 1], None, SUB)
                step(last)
                for tc in range(2):
                    last = V.tensor_tensor_reduce(out=XS[:, tc, :], in0=H[:, tc, :], in1=H[:, tc, :], scale=1.0, scalar=0.0,
                                                  op0=MUL, op1=ADD, accum_out=ssq[:, tc:tc + 1])
                step(last)
                V.tensor_scalar(var, ssq, 1.0 / D, LN_EPS, MUL, ADD).then_inc(S("variance_ready"), 1)
                rsqrt()
                g = row(gain_row[0])
                for tc in range(2):
                    last = V.scalar_tensor_tensor(H[:, tc, :], H[:, tc, :], rstd[:, tc:tc + 1], g, MUL, MUL)
                use_row(gain_row[0], last)
                b = row(1 - gain_row[0])
                last = V.tensor_tensor(H[:, :, :], H[:, :, :], b.rearrange("p (a n) -> p a n", a=1).broadcast_to([P, 2, D]), ADD)
                use_row(1 - gain_row[0], last)
                gain_row[0] = 1
                dve.sem_inc(S(signal), 1)

            gain_row = [0]

            def scores_max(n, src, scale, out_n):
                step(V.tensor_reduce(mx, src, X, ALU.max))
                V.tensor_scalar(nbias, mx, -scale, None, MUL).then_inc(S("softmax_bias"), 1)

            def normalise(n, probs):
                dve.wait_ge(S("exponentials"), n)
                step(V.reciprocal(rden, den))
                flat = probs.rearrange("p a h t -> p (a h) t")
                return V.tensor_tensor(flat, flat, rden.rearrange("p (a b) -> p a b", b=1).broadcast_to([P, 8, T]), MUL)

            def probs_columns(n, dst):
                dve.wait_ge(S("probs_turned"), n)
                V.tensor_copy(dst[:, 4:8, :], ps[:, 6:8, :].rearrange("p a (b t) -> p (a b) t", t=T)).then_inc(S("probsT_by_vector"), 1)

            def attention(tag, n, layer):
                MT, KT, VV, QT, PT, OT = (w_(o, KC, T) for o in (2048, 4096, 6144, 8192, 2048, 10240))
                if tag != "C":
                    rms(w_(0, HALVES, D), w_(0, HALVES, D), EPS)
                    columns(MT, ("xa_norm_mem", 8 * layer))
                else:
                    columns(MT, None)
                take_columns(f"{tag}k1", KT[:, 4:8, :])
                take(f"{tag}v1", w_(6144, HALVES, D)[:, :, 512:1024])
                if tag != "C":
                    rms(H, XS, EPS)
                    columns(XT, ("xa_norm", 8 * layer))
                else:
                    columns(XT, None)
                take_columns(f"{tag}q1", QT[:, 4:8, :])
                dve.wait_ge(S("scores_ready"), n)
                scores_max(n, ps[:, 4:8, :].rearrange("p a (b t) -> p (a b) t", t=T), 1.0 / 16, n)
                normalise(n, w_(0, 2, 4, T)).then_inc(S("probs_ready"), 1)
                probs_columns(n - (tag == "C"), PT)
                dve.wait_ge(S("attended"), "ABC".index(tag) + 1)
                V.tensor_copy(OT[:, 4:8, :], ps[:, 6:8, :].rearrange("p a (b t) -> p (a b) t", t=T)).then_inc(S("attended_by_vector"), 1)
                for j in range(2):
                    add_unit(f"{tag}o{j}", j, ALPHA if tag == "C" else None)
                update_done(f"{tag}o1")

            dve.wait_ge(S("x_loaded"), 16)
            dve.wait_ge(S("cols_ready"), 1)
            rms(H, XS, EPS)
            columns(XT, ("ev_norm_mix", 0))
            AP_, UP = w_(2048, 4, 258), w_(3200, 4, 272)
            V.memset(AP_, 0.0)
            step(V.memset(UP, 0.0))
            u = UNIT["in_gc"]
            unit_ready(dve, u)
            dve.wait_ge(S(f"unit_read{UNIT['in_h'] % 2}"), 1)
            V.tensor_tensor(AP_[:, :, 1:257], w_(0, 4, T), PAIRS[u % 2].rearrange("p a (b t) -> p (a b) t", t=T), MUL)\
                .then_inc(S(f"unit_read{u % 2}"), 1)
            take_columns("in_u", UP[:, :, 8:264])
            dve.wait_ge(S("unit_read0"), 2)
            dve.wait_ge(S("unit_read1"), 2)
            CT, MIXT, INV, PO = w_(9216, 4, T), w_(6144, KC, T), w_(8192, 4, T), w_(5120, 4, T)
            dve.wait_ge(S("window_loaded"), 16)
            for k in range(3):
                for b in range(4):
                    wv = vec("ev_conv_a", 4 * k + b)
                    if k == 0:
                        last = V.tensor_scalar(CT[:, b, :], AP_[:, b, 0:T], wv, None, MUL)
                    else:
                        last = V.scalar_tensor_tensor(CT[:, b, :], AP_[:, b, k:k + T], wv, CT[:, b, :], MUL, ADD)
                step(last)
            V.tensor_tensor(MIXT[:, 0:4, :], CT, w_(1024, 4, T), MUL).then_inc(S("mixed_by_vector"), 1)
            SA, SB_ = w_(4352, 272), w_(4640, 272)
            for g, win in enumerate(WINDOWS):
                cur, size, nxt = UP[:, g, :], 1, SA
                while size < win:
                    n = 272 - 2 * size
                    step(V.tensor_tensor(nxt[:, 0:n], cur[:, 0:n], cur[:, size:size + n], ADD))
                    cur, nxt, size = nxt, (SB_ if nxt is SA else SA), size * 2
                at = 8 - win // 2
                step(V.tensor_tensor(PO[:, g, :], cur[:, at:at + T], INV[:, g, :], MUL))
                last = V.tensor_tensor(PO[:, g, :], PO[:, g, :], UP[:, g, 8:264], SUB)
                step(last)
            dve.sem_inc(S("pooled"), 1)
            dve.wait_ge(S("mixed_by_act"), 1)
            dve.wait_ge(S("mixed_by_vector"), 1)
            for j in range(2):
                add_unit(f"mix{j}", j)
            update_done("mix1")
            dve.sem_inc(S("mixer_finished"), 1)
            dve.sem_inc(S("h_updated"), 1)
            attention("A", 1, 0)
            dve.sem_inc(S("h_updated"), 1)
            rms(H, XS, EPS)
            columns(XT, ("ev_norm_ffn", 0))
            for f in range(FFN_TURNS):
                dve.wait_ge(S("ffn_silu"), f + 1)
                if f >= 3:
                    dve.wait_ge(S("ffn_down_products"), f - 2)
                V.tensor_tensor(w_(512 * (f % 3), 512), w_(2048 + 512 * (f % 2), 512), PAIRS[f % 2][:, 1, :], MUL)\
                    .then_inc(S("ffn_hidden"), 1)
            dve.wait_ge(S("ffn_down_products"), FFN_TURNS)
            V.tensor_tensor(H[:, :, :], H[:, :, :], ps[:, 4:8, :].rearrange("p (a b) n -> p a (b n)", a=2), ADD)\
                .then_inc(S("ffn_added"), 1)
            dve.wait_ge(S("ffn_added"), 1)
            rms(H, XS, EPS)
            columns(XT, ("od_norm_mix", 0))
            HC, CO, SQ = w_(1024, KC, 286), w_(4096, KC, T), w_(6144, KC, T)
            MEAN, VAR, STD, RST = w_(8192, T), w_(8448, T), w_(8704, T), w_(8960, T)
            step(V.memset(HC, 0.0))
            for j in range(2):
                u, ug = UNIT[f"value{j}"], UNIT[f"gate{j}"]
                unit_ready(dve, u)
                dve.wait_ge(S(f"unit_read{ug % 2}"), ug // 2 + 1)
                src = PAIRS[u % 2].rearrange("p a (b t) -> p (a b) t", t=T)
                for b in range(4):
                    last = V.scalar_tensor_tensor(HC[:, 4 * j + b, 15:15 + T], src[:, b, :], vec("od_pw1_b", 4 * j + b),
                                                  w_(0, 4, T)[:, b, :], ADD, MUL)
                last.then_inc(S(f"unit_read{u % 2}"), 1)
                dve.wait_ge(S(f"unit_read{u % 2}"), u // 2 + 1)
                dve.sem_inc(S("glu"), 1)
            for k in range(CONV):
                for kc in range(KC):
                    wv = vec("od_dw_w", KC * k + kc)
                    if k == 0:
                        last = V.tensor_scalar(CO[:, kc, :], HC[:, kc, 0:T], wv, vec("od_dw_b", kc), MUL, ADD)
                    else:
                        last = V.scalar_tensor_tensor(CO[:, kc, :], HC[:, kc, k:k + T], wv, CO[:, kc, :], MUL, ADD)
                step(last)
            dve.sem_inc(S("convolved"), 1)
            dve.wait_ge(S("feature_sums"), 1)
            step(V.tensor_scalar(MEAN, ps[:, 4, 0:T], 1.0 / D, None, MUL))
            rep = lambda a: a.rearrange("p (a t) -> p a t", a=1).broadcast_to([P, KC, T])
            step(V.tensor_tensor(CO, CO, rep(MEAN), SUB))
            V.tensor_tensor(SQ, CO, CO, MUL).then_inc(S("squared"), 1)
            dve.wait_ge(S("feature_sums"), 2)
            V.tensor_scalar(VAR, ps[:, 5, 0:T], 1.0 / D, EPS, MUL, ADD).then_inc(S("variance_ready"), 1)
            rsqrt(RST, STD)
            V.tensor_tensor(CO, CO, rep(RST), MUL).then_inc(S("standard"), 1)
            b = row(0)
            use_row(0, V.tensor_tensor(H[:, :, :], H[:, :, :], b.rearrange("p (a n) -> p a n", a=1).broadcast_to([P, 2, D]), ADD))
            for j in range(2):
                add_unit(f"pw2_{j}", j)
            update_done("pw2_1")
            dve.sem_inc(S("conv_finished"), 1)
            dve.sem_inc(S("h_updated"), 1)
            attention("B", 2, 1)
            dve.sem_inc(S("h_updated"), 1)

            def first_best(values, a, n, best, pick, tmp):
                v3 = lambda t: t.rearrange("p (a n) -> p a n", n=1).broadcast_to([P, a, n])
                iom = IOM[:, 0:n].rearrange("p (a n) -> p a n", a=1).broadcast_to([P, a, n])
                step(V.tensor_reduce(best, values, X, ALU.max))
                step(V.tensor_tensor(tmp, values, v3(best), ALU.is_equal))
                step(V.tensor_tensor(tmp, tmp, iom, MUL))
                step(V.tensor_reduce(VI[:, 0:a], tmp, X, ALU.min))
                step(V.tensor_tensor(pick, iom, v3(VI[:, 0:a]), ALU.is_equal))

            def remove(values, pick):
                step(V.scalar_tensor_tensor(values, pick, -REMOVED, values, MUL, ADD))

            def ranks(k):
                c = MOES[k]
                G, M = c["groups"], c["members"]
                dve.wait_ge(S("ranks_ready"), k)
                r = ps[:, 5, 0:16].rearrange("p (a e) -> p a e", e=8)[:, :, 0:G]
                step(V.scalar_tensor_tensor(RK[:, :, 0:G], r, 1.0, SEL[:, :, 0:G], ADD, MUL))
                step(V.tensor_scalar(RK[:, :, 0:G], RK[:, :, 0:G], -1.0, None, ADD))
                V.tensor_scalar(RK[:, :, G:2 * G], RK[:, :, 0:G], -float(P), None, ADD)
                V.tensor_copy(CB[:, :, G * M:2 * G * M], CB[:, :, 0:G * M])
                step(V.tensor_reduce(CMAX, ps[:, 5, 16:16 + G], X, ALU.max))
                step(V.tensor_scalar(CMAX, CMAX, float(P), float(G), ALU.is_gt, MUL))
                V.tensor_scalar(count[:, k - 1:k], CMAX, float(G), None, ADD).then_inc(moe_sem(k, "turns_ready"), 1)

            def experts(k, dst, gain):
                c = MOES[k]
                M = c["members"]
                halves, per_group = 2 * M * c["chunks"], 3 * M * c["chunks"]
                PR, PG, PT, GB = w_(2048, 2, P), w_(2304, 4, 2, P), w_(3328, 2, P), w_(3584, M, P)
                XG, Y = w_(0, KC, P), w_(1024, D)
                iota = c_("iota")
                dve.sem_inc(moe_sem(k, "added"), 1)
                dve.sem_inc(moe_sem(k, "hidden"), 2)
                dve.wait_ge(moe_sem(k, "turns_ready"), 1)
                turns = dve.value_load(count[0:1, k - 1:k], min_val=c["groups"], max_val=2 * c["groups"])
                with dve.Fori(0, turns) as it:
                    for m in range(M):
                        for tc in range(2):
                            V.tensor_scalar(PG[:, m, tc, :], iota, RK[:, tc, bass.ds(it, 1)],
                                            CB[:, tc, bass.ds(it * M + m, 1)], ALU.is_equal, MUL)
                    for tc in range(2):
                        last = V.tensor_scalar(PR[:, tc, :], iota, RK[:, tc, bass.ds(it, 1)], None, ALU.is_equal)
                    last.then_inc(moe_sem(k, "picked"), 1)
                    dve.wait_ge(moe_sem(k, "gathered"), it + 1)
                    for j in range(4):
                        src = ps[:, 4, j * P:(j + 1) * P]
                        if gain:
                            V.tensor_scalar(XG[:, j, :], src, vec(gain, j), None, MUL)
                        else:
                            V.tensor_copy(XG[:, j, :], src)
                    V.tensor_copy(PT, ps[:, 7, 0:T].rearrange("p (a t) -> p a t", t=P)).then_inc(moe_sem(k, "gathered_by_vector"), 1)
                    dve.wait_ge(moe_sem(k, "gathered_by_act"), it + 1)
                    for hc in range(halves):
                        m = hc // (2 * c["chunks"])
                        UG = w_(5120 + 256 * (hc % 2), 2, P)
                        dve.wait_ge(moe_sem(k, "silu"), it * halves + (hc + 1))
                        V.tensor_tensor(UG, ps[:, hc % 2, T:2 * T].rearrange("p (a t) -> p a t", t=P),
                                        GB[:, m:m + 1, :].broadcast_to([P, 2, P]), MUL).then_inc(moe_sem(k, "gated"), 1)
                        dve.wait_ge(moe_sem(k, "gated"), it * halves + (hc + 1))
                        V.tensor_tensor(w_(4096 + 256 * (hc % 2), 2, P), w_(4608 + 256 * (hc % 2), 2, P), UG, MUL)\
                            .then_inc(moe_sem(k, "hidden"), 1)
                    dve.wait_ge(moe_sem(k, "slots_free"), it * per_group + (per_group + c["slots"]))
                    V.tensor_copy(Y[:, 512:1024], ps[:, 3, :]).then_inc(moe_sem(k, "outputs_by_vector"), 1)
                    dve.wait_ge(moe_sem(k, "scattered"), it + 1)
                    V.tensor_tensor(dst[:, :, :], dst[:, :, :], ps[:, 4:8, :].rearrange("p (a b) n -> p a (b n)", a=2), ADD)\
                        .then_inc(moe_sem(k, "added"), 1)
                    dve.wait_ge(moe_sem(k, "added"), it + 2)

            rms(H, XS, EPS)
            columns(XT, ("od_norm_moe", 0))
            dve.wait_ge(S("const_loaded"), 16)
            step(V.tensor_scalar(IOM, c_("iota")[:, 0:16], -99.0, None, ADD))
            dve.wait_ge(S("logits_ready"), 1)
            e8 = lambda t: t[:, :, 0:8]
            step(V.tensor_copy(e8(LG), ps[:, 4, 0:32].rearrange("p (a e) -> p a e", e=16)[:, :, 0:8]))
            first_best(e8(LG), 2, 8, V0[:, 0:2], e8(O0), e8(TA))
            remove(e8(LG), e8(O0))
            first_best(e8(LG), 2, 8, V1[:, 0:2], e8(O1), e8(TA))
            V.tensor_tensor(PAIRW[:, 0, :], V1[:, 0:2], V0[:, 0:2], SUB).then_inc(S("logit_gap"), 1)
            step(V.tensor_tensor(SEL, e8(O0), e8(O1), ADD))
            dve.sem_inc(S("chosen"), 1)
            dve.wait_ge(S("gap_exp"), 1)
            step(V.tensor_scalar(PAIRW[:, 2, :], PAIRW[:, 1, :], 1.0, None, ADD))
            step(V.reciprocal(PAIRW[:, 2, :], PAIRW[:, 2, :]))
            r3 = lambda t, n: t.rearrange("p (a n) -> p a n", n=1).broadcast_to([P, 2, n])
            step(V.scalar_tensor_tensor(e8(CB), e8(O1), 1.0, r3(PAIRW[:, 1, :], 8), MUL, MUL))
            step(V.tensor_tensor(e8(CB), e8(CB), e8(O0), ADD))
            step(V.tensor_tensor(e8(CB), e8(CB), r3(PAIRW[:, 2, :], 8), MUL))
            ranks(1)
            experts(1, H, "od_norm_moe")
            dve.sem_inc(S("moe_done"), 1)
            n_["sq"] += 1
            dve.wait_ge(S("squares_summed"), n_["sq"])
            V.tensor_scalar(var, ssq, 1.0 / D, EPS, MUL, ADD).then_inc(S("variance_ready"), 1)
            rsqrt()
            g = row(1)
            for tc in range(2):
                last = V.scalar_tensor_tensor(H[:, tc, :], H[:, tc, :], rstd[:, tc:tc + 1], g, MUL, MUL)
            use_row(1, last)
            layer_norm("h_ready")
            columns(XT, None)
            take_columns("fqk", w_(0, 4, T))
            dve.wait_ge(S("small_loaded"), 16 * 10)
            step(V.tensor_tensor(lam4[:, 0::2, :], lam4[:, 0::2, :], lam4[:, 1::2, :], MUL))
            V.tensor_reduce(lamp, lam4[:, 0::2, :], X, ADD).then_inc(S("lam_sums"), 1)
            dve.wait_ge(S("lam_exp"), 1)
            step(V.tensor_tensor(nlam, lame[:, 1:2], lame[:, 0:1], SUB))
            step(V.tensor_scalar(nlam, nlam, -LAM_INIT, None, ADD))
            u = UNIT["fv"]
            unit_ready(dve, u)
            V.tensor_tensor(ffl, PAIRS[u % 2][:, :, 256:260], foxb.rearrange("p (a n) -> p a n", a=1).broadcast_to([P, 2, 4]), ADD)
            V.tensor_copy(w_(7168, 2, 256), PAIRS[u % 2][:, :, 0:256]).then_inc(S(f"unit_read{u % 2}"), 1)
            dve.wait_ge(S(f"unit_read{u % 2}"), u // 2 + 1)
            V.tensor_scalar(logf_fox, ffl, 0.0, None, ALU.min).then_inc(S("fox_logits"), 1)
            dve.wait_ge(S("fox_log1p"), 1)
            dve.wait_ge(S("fox_logits"), 1)
            V.tensor_tensor(logf_fox, logf_fox, ffa, SUB).then_inc(S("fox_log"), 1)
            u = UNIT["dv"]
            unit_ready(dve, u)
            V.tensor_copy(w_(7680, 2, 256), PAIRS[u % 2][:, :, 0:256]).then_inc(S(f"unit_read{u % 2}"), 1)
            HFZ, HFA = w_(9216, 2, 512), w_(4096, 2, 512)
            take("hf", HFZ)
            u = UNIT["hf"]
            dve.wait_ge(S(f"unit_read{u % 2}"), u // 2 + 1)
            dve.sem_inc(S("forget_logits"), 1)
            dve.wait_ge(S("forget_log1p"), 1)
            step(V.scalar_tensor_tensor(HFA, HFZ, 0.0, HFA, ALU.min, SUB))
            DB = XT[:, :, :].rearrange("p (a h) t -> p a h t", a=2)
            dve.wait_ge(S("fox_sums"), 2)
            cs = ffa
            step(V.tensor_copy(cs, ps[:, 4, 0:8].rearrange("p (a e) -> p a e", e=4)))
            masks = row(0).rearrange("p (k a t) -> p k a t", k=2, a=2)
            u = UNIT["hg"]
            for w in (u - 1, u):
                unit_ready(dve, w)
            for tc in range(2):
                for place, h in enumerate(HEAD_ORDER):
                    last = V.scalar_tensor_tensor(DB[:, tc, place, :], ps[:, 6 + h // 2, h % 2 * T:h % 2 * T + T], -1.0,
                                                  masks[:, 0, tc, :], MUL, ADD)
            step(last)
            for tc in range(2):
                for place, h in enumerate(HEAD_ORDER):
                    last = V.tensor_scalar(DB[:, tc, place, :], DB[:, tc, place, :], cs[:, tc, h:h + 1], None, ADD)
            step(last)
            dve.sem_inc(S("fox_bias"), 1)
            PR, PR2, PT = w_(8192, 2, 4, T), w_(10240, 2, 4, T), w_(10240, KC, T)

            def masked_scores(n, scale, bias, dst):
                dve.wait_ge(S("scores_ready"), n)
                for tc in range(2):
                    last = V.scalar_tensor_tensor(dst[:, tc, :, :], ps[:, 4 + 2 * tc:6 + 2 * tc, :].rearrange("p a (b t) -> p (a b) t", t=T),
                                                  scale, bias(tc), MUL, ADD)
                step(last)

            dve.wait_ge(S("keys_turned"), 1)
            masked_scores(3, 0.125, lambda tc: DB[:, tc, :, :], PR)
            dve.sem_inc(S("fox_scored"), 1)
            scores_max(3, PR.rearrange("p a h t -> p (a h) t"), 1.0, 3)
            normalise(3, PR).then_inc(S("probs_ready"), 1)
            probs_columns(3, PT)
            dve.wait_ge(S("small_attended"), 1)
            V.tensor_copy(XS[:, :, 0:256], ps[:, 4, :].rearrange("p (a n) -> p a n", a=2)).then_inc(S("small_read"), 1)
            for which in range(2):
                dst = (PR, PR2)[which]
                masked_scores(4 + which, 32.0 ** -0.5,
                              lambda tc: masks[:, 1, tc:tc + 1, :].broadcast_to([P, 4, T]), dst)
                if which == 0:
                    dve.sem_inc(S("diff_map"), 1)
                scores_max(4 + which, dst.rearrange("p a h t -> p (a h) t"), 1.0, 0)
                step(normalise(4 + which, dst))
            use_row(0, V.scalar_tensor_tensor(PR.rearrange("p a h t -> p (a h t)"), PR2.rearrange("p a h t -> p (a h t)"), nlam[:, 0:1],
                                              PR.rearrange("p a h t -> p (a h t)"), MUL, ADD))
            dve.sem_inc(S("probs_ready"), 1)
            probs_columns(4, PT)
            dve.wait_ge(S("small_attended"), 2)
            OD = XS[:, :, 256:512]
            V.tensor_copy(OD, ps[:, 4, :].rearrange("p (a n) -> p a n", a=2)).then_inc(S("small_read"), 1)
            dve.wait_ge(S("small_read"), 2)

            def head_norm(src, scratch, n, d, gain, extra):
                step(V.tensor_tensor(scratch, src, src, MUL))
                step(V.tensor_reduce(dss, scratch, X, ADD))
                V.tensor_scalar(dss, dss, 1.0 / d, LN_EPS, MUL, ADD).then_inc(S("variance_ready"), 1)
                rsqrt(drs, dstd)
                for tc in range(2):
                    last = V.scalar_tensor_tensor(src[:, tc], src[:, tc], extra,
                                                  drs[:, tc, :].rearrange("p (h n) -> p h n", n=1).broadcast_to([P, 4, d]), MUL, MUL)
                step(last)
                for tc in range(2):
                    last = V.tensor_tensor(src[:, tc], src[:, tc], gain.rearrange("p (a n) -> p a n", a=1).broadcast_to([P, 4, d]), MUL)
                step(last)

            h4 = lambda t: t.rearrange("p a (h d) -> p a h d", h=4)
            head_norm(h4(OD), h4(w_(8192, 2, 256)), 4, 64, dgain, 1.0 - LAM_INIT)
            dve.sem_inc(S("diff_done"), 1)
            E, QE, KE, ST = w_(8192, 4, T), w_(9216, 4, T), w_(10240, 4, T), w_(11264, 8, P)
            QH, KH = w_(2048, 4, T), w_(3072, 4, T)
            step(V.memset(ST, 0.0))
            dve.wait_ge(S("keys_columns"), 1)
            dve.wait_ge(S("levels_loaded"), 16)
            CR = w_(8192, 4, P)
            scores = ps[:, 0:2, :].rearrange("p a (b t) -> p (a b) t", t=P)
            for lv in range(9):
                dve.wait_ge(S("level_scores"), lv + 1)
                if lv < 8:
                    mask = (IDENT if lv == 0 else c_(f"pair{lv - 1}")).bitcast(I32)
                    V.copy_predicated(ST, mask.rearrange("p (a t) -> p a t", a=1).broadcast_to([P, 8, P]), scores)\
                        .then_inc(S("level_merged"), 1)
                    dve.wait_ge(S("level_merged"), lv + 1)
                    dve.wait_ge(S("level_exp"), lv + 1)
                    V.tensor_tensor(QE, QH, E, MUL)
                    V.tensor_tensor(KE, KH, E, MUL).then_inc(S("level_decayed"), 1)
                    dve.wait_ge(S("level_decayed"), lv + 1)
                else:
                    V.tensor_copy(CR, ps[:, 0, :].rearrange("p (h t) -> p h t", t=P)).then_inc(S("level_merged"), 1)
            dve.wait_ge(S("recurrence_out"), 1)
            OH = XS[:, :, 512:1024]
            step(V.tensor_copy(OH, ps[:, 2:4, :]))
            head_norm(h4(OH), h4(w_(9216, 2, 512)), 4, 128, hgain, 1.0)
            V.tensor_tensor(OH, OH, w_(6144, 2, 512), MUL).then_inc(S("xs_ready"), 1)
            dve.wait_ge(S("xs_ready"), 9)
            columns(XT, None)
            dve.sem_inc(S("hybrid_finished"), 1)
            for j in range(2):
                add_unit(f"out{j}", j, ALPHA)
            update_done("out1")
            layer_norm("h_ready")
            attention("C", 6, 0)
            layer_norm("h_ready")
            V.tensor_scalar(XS[:, :, :], H[:, :, :], ALPHA, None, MUL)
            columns(XT, None)
            dve.wait_ge(S("router_scores"), 1)
            step(V.tensor_tensor(BI, LG, rbias.rearrange("p (a n) -> p a n", a=1).broadcast_to([P, 2, 16]), ADD))
            g4 = lambda t: t.rearrange("p a (g m) -> p (a g) m", m=4)
            WK = TA
            first_best(g4(BI), 8, 4, V0, g4(O0), g4(TA))
            step(V.tensor_copy(O1, BI))
            remove(O1, O0)
            step(V.tensor_reduce(V1, g4(O1), X, ALU.max))
            step(V.tensor_tensor(V0, V0, V1, ADD))
            gs = V0.rearrange("p (a g) -> p a g", g=4)
            first_best(gs, 2, 4, V1[:, 0:2], SEL[:, :, 0:4], TA[:, :, 0:4])
            dve.sem_inc(S("chosen"), 1)
            step(V.tensor_scalar(O1[:, :, 0:4], SEL[:, :, 0:4], -1.0, REMOVED, ADD, MUL))
            step(V.tensor_copy(V0.rearrange("p (a g) -> p a g", g=4), O1[:, :, 0:4]))
            step(V.tensor_tensor(g4(BI), g4(BI), V0.rearrange("p (a n) -> p a n", n=1).broadcast_to([P, 8, 4]), ADD))
            first_best(BI, 2, 16, V1[:, 0:2], O0, TA)
            remove(BI, O0)
            first_best(BI, 2, 16, V1[:, 0:2], O1, TA)
            step(V.tensor_tensor(O0, O0, O1, ADD))
            step(V.tensor_tensor(O0, O0, LG, MUL))
            step(V.tensor_reduce(V1[:, 0:2], O0, X, ADD))
            step(V.reciprocal(V1[:, 0:2], V1[:, 0:2]))
            step(V.tensor_tensor(CB[:, :, 0:16], O0, r3(V1[:, 0:2], 16), MUL))
            ranks(2)
            experts(2, XS, None)
            step(V.tensor_copy(H[:, :, :], XS[:, :, :]))
            layer_norm("h_ready")
            dve.sem_inc(S("h_final"), 1)


_NAMES = ("x mem ev_norm_mix ev_w_in ev_conv_a ev_pool_w ev_pool_scale ev_w_out ev_norm_ffn ev_ffn_gu ev_ffn_down "
          "od_norm_mix od_pw1_w od_pw1_b od_dw_w od_dw_b od_ln_g od_ln_b od_pw2_w od_pw2_b od_norm_moe od_router "
          "od_moe_gu od_moe_down xa_norm xa_norm_mem xa_wq xa_wkv xa_wo final_norm mem_2 ln_in_g_2 ln_in_b_2 w_in_2 "
          "fox_fb_2 lam_q1_2 lam_k1_2 lam_q2_2 lam_k2_2 diff_norm_g_2 hgrn_norm_g_2 w_out_2 mem_wq_2 mem_wk_2 "
          "mem_wv_2 mem_wo_2 router_w_2 router_b_2 w1_2 w3_2 w2_2 ln_g_2 ln_b_2").split()


def kernel(**inputs):
    import concourse.bacc as bacc
    from concourse.bass_utils import run_bass_kernel_spmd

    nc = bacc.Bacc("TRN2", target_bir_lowering=False, num_devices=1)
    arrays, ins = {}, {}
    for name in _NAMES:
        a = np.ascontiguousarray(inputs[name])
        arrays["in_" + name] = a
        ins[name] = nc.dram_tensor("in_" + name, a.shape, F32, kind="ExternalInput").ap()
    arrays["constants"] = CONSTANTS
    const_in = nc.dram_tensor("constants", CONSTANTS.shape, F32, kind="ExternalInput").ap()
    out = nc.dram_tensor("out", (1, T, D), F32, kind="ExternalOutput").ap()
    program(nc, ins, const_in, out)
    r = run_bass_kernel_spmd(nc, [arrays], core_ids=[0])
    return r.results[0]["out"]
```

```python
from contextlib import ExitStack

import numpy as np

import concourse.bass as bass
from concourse import mybir

F32 = mybir.dt.float32
F32R = mybir.dt.float32r
I32 = mybir.dt.int32
ALU = mybir.AluOpType
ACT = mybir.ActivationFunctionType
X = mybir.AxisListType.X

P = 128
T = 256
HALVES = T // P
D = 1024
KC = D // P
PANEL = 512
HALF = KC * PANEL // 2
SLOTS = 3
SPLITS = 3
D_FF = 2816
EPS, LN_EPS = 1e-6, 1e-5
ALPHA = 2.0 ** 0.25
LAM_INIT = 0.2
WINDOWS = (2, 4, 8, 16)
CONV = 31
MASKED = -1e30
REMOVED = 3e38
HEAD_ORDER = (0, 2, 1, 3)

CONST_COLS = {}


def constant_table():
    r = np.arange(P)
    parts = []

    def put(name, a):
        CONST_COLS[name] = (sum(p.shape[1] for p in parts), a.shape[1])
        parts.append(np.asarray(a, np.float32))

    put("ident", np.eye(P))
    put("ones", np.ones((P, P)))
    put("upto", r[:, None] <= r[None, :])
    put("before", r[:, None] < r[None, :])
    put("iota", np.broadcast_to(r[None, :], (P, P)))
    resident = sum(p.shape[1] for p in parts)
    for lv in range(7):
        m = 1 << lv
        start = r // (2 * m) * (2 * m)
        border = start + m - 1
        late = r % (2 * m) >= m
        span = np.where(late[None, :], (r[:, None] > border[None, :]) & (r[:, None] <= r[None, :]),
                        (r[:, None] > r[None, :]) & (r[:, None] <= border[None, :]))
        put(f"span{lv}", span)
    put("after", r[:, None] > r[None, :])
    for lv in range(7):
        m = 1 << lv
        put(f"pair{lv}", (r[:, None] // (2 * m) == r[None, :] // (2 * m))
            & (r[:, None] % (2 * m) < m) & (r[None, :] % (2 * m) >= m))
    q, k = np.arange(T), np.arange(T)
    for name, ok in (("causal", k[None, :] <= q[:, None]), ("chunked", k[None, :] // 64 <= q[:, None] // 64)):
        a = np.where(ok, 0.0, MASKED).reshape(HALVES, P, T).transpose(1, 0, 2).reshape(P, HALVES * T)
        put(name, a)
    inv = []
    for w in WINDOWS:
        lo = np.maximum(q - w // 2, 0)
        hi = np.minimum(q + w - 1 - w // 2, T - 1) + 1
        inv.append(1.0 / (hi - lo).astype(np.float32))
    put("window", np.broadcast_to(np.concatenate(inv)[None], (P, len(WINDOWS) * T)))
    return np.concatenate(parts, 1), resident


CONSTANTS, RESIDENT = constant_table()

VECTORS = [("ev_norm_mix", 8), ("ev_conv_a", 12), ("ev_pool_scale", 4), ("ev_norm_ffn", 8), ("od_norm_mix", 8),
           ("od_pw1_b", 16), ("od_dw_b", 8), ("od_ln_g", 8), ("od_ln_b", 8), ("od_norm_moe", 8),
           ("xa_norm", 16), ("xa_norm_mem", 16), ("od_dw_w", 248)]
VEC_AT = {}
for _name, _rows in VECTORS:
    VEC_AT[_name] = sum(r for _, r in VECTORS[:len(VEC_AT)])
VEC_TILES = -(-sum(r for _, r in VECTORS) // P)
VEC_ROWS = sum(r for _, r in VECTORS)
VEC_LOADS = sum((VEC_AT[n] + r - 1) // P - VEC_AT[n] // P + 1 for n, r in VECTORS)

UNITS = []
UNIT = {}


def _unit(name, weight, c0, n, columns, src, layer=0):
    UNIT[name] = len(UNITS)
    UNITS.append((weight, layer, c0, n, columns, src))


def _memory_units(tag, layer, wk, wv, v0):
    for j in range(2):
        _unit(f"{tag}k{j}", wk, j * PANEL, PANEL, True, "memory", layer)
    for j in range(2):
        _unit(f"{tag}v{j}", wv, v0 + j * PANEL, PANEL, False, "memory", layer)


def _query_units(tag, layer, wq, wo):
    for j in range(2):
        _unit(f"{tag}q{j}", wq, j * PANEL, PANEL, True, "x", layer)
    for j in range(2):
        _unit(f"{tag}o{j}", wo, j * PANEL, PANEL, False, "attended", layer)


for _j, _n in enumerate(("h", "gb", "gc", "u")):
    _unit("in_" + _n, "ev_w_in", _j * PANEL, PANEL, True, "x")
_memory_units("A", 0, "xa_wkv", "xa_wkv", D)
for _j in range(2):
    _unit(f"mix{_j}", "ev_w_out", _j * PANEL, PANEL, False, "mixed")
_query_units("A", 0, "xa_wq", "xa_wo")
FFN_AT = len(UNITS)
for _j in range(2):
    _unit(f"gate{_j}", "od_pw1_w", D + _j * PANEL, PANEL, True, "x")
    _unit(f"value{_j}", "od_pw1_w", _j * PANEL, PANEL, True, "x")
_memory_units("B", 1, "xa_wkv", "xa_wkv", D)
for _j in range(2):
    _unit(f"pw2_{_j}", "od_pw2_w", _j * PANEL, PANEL, False, "conformed")
_query_units("B", 1, "xa_wq", "xa_wo")
MOE1_AT = len(UNITS)
_unit("fqk", "w_in_2", 0, 512, True, "x")
_unit("dqk", "w_in_2", 772, 512, True, "x")
_unit("hq", "w_in_2", 1540, 512, True, "x")
_unit("fv", "w_in_2", 512, 260, False, "x")
_unit("dv", "w_in_2", 1284, 256, False, "x")
_unit("hf", "w_in_2", 2052, 512, False, "x")
_unit("hi", "w_in_2", 2564, 512, False, "x")
_unit("hg", "w_in_2", 3076, 512, False, "x")
for _j in range(2):
    _unit(f"out{_j}", "w_out_2", _j * PANEL, PANEL, False, "x")
_memory_units("C", 0, "mem_wk_2", "mem_wv_2", 0)
_query_units("C", 0, "mem_wq_2", "mem_wo_2")
FFN_TURNS = D_FF // T

MOES = {
    1: dict(groups=8, members=1, chunks=7, slots=7, experts=8),
    2: dict(groups=4, members=4, chunks=1, slots=6, experts=16),
}


def stream(c):
    n = c["members"] * c["chunks"]
    order = [("gate", 0), ("up", 0)]
    for k in range(1, n):
        order += [("gate", k), ("up", k), ("down", k - 1)]
    order.append(("down", n - 1))
    return [(kind, k, half) for kind, k in order for half in range(2)]


def chunk_at(k):
    return 0 if k == 0 else 4 + 6 * (k - 1)


def program(nc, ins, const_in, out):
    ctx = ExitStack()
    with ctx:
        def sb(name, shape, dt=F32):
            return ctx.enter_context(nc.sbuf_tensor(name, shape, dt))

        sems = {}

        def S(name):
            if name not in sems:
                sems[name] = ctx.enter_context(nc.semaphore(name))
            return sems[name]

        ring = sb("ring", [P, 7, HALF])
        w_high = sb("w_high", [P, SPLITS, HALF], F32R)
        w_low = sb("w_low", [P, SPLITS, HALF], F32R)
        x_high = sb("x_high", [P, KC, P], F32R)
        x_low = sb("x_low", [P, KC, P], F32R)
        h_high = sb("h_high", [P, 4, P], F32R)
        h_low = sb("h_low", [P, 4, P], F32R)
        const = sb("const", [P, RESIDENT])
        H = sb("H", [P, HALVES, D])
        XS = sb("XS", [P, HALVES, D])
        XT = sb("XT", [P, KC, T])
        work = sb("work", [P, 12 * 1024])
        brow = sb("brow", [P, 2, D])
        cols = sb("cols", [P, VEC_TILES * P])
        small = sb("small", [P, 512])
        count = sb("count", [P, 2], I32)
        ps = ctx.enter_context(nc.psum_tensor("ps", [P, 8, 512], F32))

        def c_(name):
            a, n = CONST_COLS[name]
            if a >= RESIDENT:
                return XT[:, :, :].rearrange("p k t -> p (k t)")[:, a - RESIDENT:a - RESIDENT + n]
            return const[:, a:a + n]

        def w_(off, *shape):
            n = int(np.prod(shape))
            v = work[:, off:off + n]
            if len(shape) == 2:
                return v.rearrange("p (a b) -> p a b", b=shape[1])
            if len(shape) == 3:
                return v.rearrange("p (a b c) -> p a b c", b=shape[1], c=shape[2])
            return v

        small_top = [0]

        def sm(*shape):
            n = int(np.prod(shape))
            v = small[:, small_top[0]:small_top[0] + n]
            small_top[0] += n
            assert small_top[0] <= 512
            if len(shape) == 2:
                return v.rearrange("p (a b) -> p a b", b=shape[1])
            return v

        def vec(name, r=0):
            a = VEC_AT[name] + r
            return cols[:, a:a + 1]

        IDENT, ONES = c_("ident"), c_("ones")
        prob = {n: w_(8192 if n in (3, 4) else 0, 2, 4, T) for n in range(1, 6)}
        ssq, var, std, rstd = sm(2), sm(2), sm(2), sm(2)
        mean = sm(2)
        mx, nbias, den, rden = sm(8), sm(8), sm(8), sm(8)
        lam4 = sm(4, 32)
        lamp, lame, nlam = sm(2), sm(2), sm(1)
        dgain = sm(64)
        foxb = sm(4)
        ffl, ffa, logf_fox = sm(2, 4), sm(2, 4), sm(2, 4)
        dss, dstd, drs = sm(2, 4), sm(2, 4), sm(2, 4)
        rbias = sm(16)
        hgain = c_("ident")
        big_small = sb("big_small", [P, 640])
        gates = sb("gates", [P, 120])
        hgain = big_small[:, 0:128]
        router = big_small[:, 128:256].rearrange("p (k e) -> p k e", e=16)
        LG = big_small[:, 256:288].rearrange("p (a e) -> p a e", e=16)
        BI = big_small[:, 288:320].rearrange("p (a e) -> p a e", e=16)
        TA = big_small[:, 320:352].rearrange("p (a e) -> p a e", e=16)
        O0 = big_small[:, 352:384].rearrange("p (a e) -> p a e", e=16)
        O1 = big_small[:, 384:416].rearrange("p (a e) -> p a e", e=16)
        CB = gates[:, 0:72].rearrange("p (a e) -> p a e", e=36)
        RK = gates[:, 72:106].rearrange("p (a e) -> p a e", e=17)
        CBS = gates[:, 106:114].rearrange("p (a e) -> p a e", e=4)
        GS = gates[:, 114:118]
        SEL = big_small[:, 512:528].rearrange("p (a e) -> p a e", e=8)
        V0, V1 = big_small[:, 528:536], big_small[:, 536:544]
        VI = big_small[:, 544:552]
        IOM = big_small[:, 552:568]
        PAIRW = big_small[:, 568:574].rearrange("p (k a) -> p k a", a=2)
        CMAX = big_small[:, 574:575]
        TOT = big_small[:, 576:584]
        router1 = sb("router1", [P, KC, 8])
        poolw = brow[:, 0, 0:512].rearrange("p (g n) -> p g n", n=P)

        sources = {"x": XT, "memory": XT, "mixed": w_(10240, KC, T), "attended": XT, "conformed": w_(2304, KC, T)}
        PAIRS = [ps[:, 0:2, :], ps[:, 2:4, :]]

        def k_major(w, layer, c0, n):
            return w[layer, :, c0:c0 + n].rearrange("(k p) n -> p k n", p=P)

        panels = []
        unit_panel, ffn_panel = {}, {}
        for u in range(len(UNITS) + 1):
            if u == FFN_AT:
                gu, dn = ins["ev_ffn_gu"], ins["ev_ffn_down"]
                for f in range(FFN_TURNS):
                    ffn_panel["gu", f] = len(panels)
                    panels.append(([((0, 256), k_major(gu, 0, f * T, T)), ((256, 256), k_major(gu, 0, D_FF + f * T, T))],
                                   "ffn_hidden_products", f + 1))
                    ffn_panel["down", f] = len(panels)
                    panels.append(([("rows", dn[0, f * T:(f + 1) * T, :].rearrange("(k p) n -> p k n", p=P))],
                                   "ffn_down_products", f + 1))
            if u == MOE1_AT:
                moe1_panel = len(panels)
            if u == len(UNITS):
                break
            weight, layer, c0, n, columns, _ = UNITS[u]
            unit_panel[u] = len(panels)
            panels.append(([((0, n), k_major(ins[weight], layer, c0, n))], f"unit_ready{u % 2}", u // 2 + 1))

        def slot(i):
            return (i - moe1_panel) % SLOTS if i >= moe1_panel else i % SLOTS

        landed, landed_count = [], {}
        for i, (pieces, _, _) in enumerate(panels):
            landed_count[slot(i)] = landed_count.get(slot(i), 0) + 16 * len(pieces)
            landed.append((slot(i), landed_count[slot(i)]))

        def slot_kn(i):
            return ring[:, 2 * i:2 * i + 2, :].rearrange("p a (k n) -> p (a k) n", n=PANEL)

        def slot_rows(i):
            return ring[:, 2 * i:2 * i + 2, :].rearrange("p a (k n) -> p (a k) n", n=D)

        def wait_panel(eng, i):
            s, v = landed[i]
            eng.wait_ge(S(f"landed{s}"), v)

        def unit_ready(eng, u):
            eng.wait_ge(S(f"unit_ready{u % 2}"), u // 2 + 1)

        class Steps:

            def __init__(self, eng, sem, base=0):
                self.eng, self.sem, self.base, self.n = eng, sem, base, 0

            def __call__(self, ins):
                self.n += 1
                ins.then_inc(self.sem, 1)
                self.eng.wait_ge(self.sem, self.base + self.n)

        block = ctx.enter_context(nc.Block())

        def moe_sem(k, name):
            return S(f"moe{k}_{name}")

        @block.sync
        def _(sync):
            def load(i, wait):
                pieces, sem, value = panels[i]
                if wait:
                    sync.wait_ge(S(panels[i - SLOTS][1]), panels[i - SLOTS][2])
                for where, src in pieces:
                    n = src.shape[2]
                    if where == "rows":
                        dst = slot_rows(slot(i))[:, 0:src.shape[1], :]
                    else:
                        dst = slot_kn(slot(i))[:, :, where[0]:where[0] + n]
                    sync.dma_start(dst, src).then_inc(S(f"landed{slot(i)}"), 16)

            def experts(k, source):
                c = MOES[k]
                slots, halves = c["slots"], stream(c)
                sync.sem_inc(moe_sem(k, "split"), slots)

                def group(g, turn):
                    for j, (kind, chunk, half) in enumerate(halves):
                        sync.wait_ge(moe_sem(k, "split"), turn * len(halves) + (j + 1))
                        src = source(kind, g, chunk, half)
                        dst = ring[:, j % slots, :].rearrange("p (k n) -> p k n", n=src.shape[2])
                        sync.dma_start(dst, src).then_inc(moe_sem(k, f"landed{j % slots}"), 16)

                with sync.Fori(0, c["groups"]) as g:
                    group(g, g)
                sync.wait_ge(moe_sem(k, "turns_ready"), 1)
                turns = sync.value_load(count[0:1, k - 1:k], min_val=c["groups"], max_val=2 * c["groups"])
                with sync.If(turns > c["groups"]):
                    with sync.Fori(0, c["groups"]) as g:
                        group(g, g + c["groups"])
                with sync.Else():
                    sync.nop()
                if k == 1:
                    sync.wait_ge(moe_sem(k, "split"), turns * len(halves) + slots)

            last = {0: 0, 1: 10, 2: 14, 3: 36, 4: 46}
            n_dense = moe1_panel
            for i in range(n_dense):
                load(i, i >= SLOTS)
            for i in range(moe1_panel - SLOTS, moe1_panel):
                sync.wait_ge(S(panels[i][1]), panels[i][2])
            gu1, dn1 = ins["od_moe_gu"], ins["od_moe_down"]

            def first_mixture(kind, g, chunk, half):
                if kind == "down":
                    r = chunk * PANEL + half * 256
                    return dn1[0, bass.ds(g, 1), r:r + 256, :].rearrange("a (k p) n -> p (a k) n", p=P)
                c0 = chunk * PANEL + (7 * PANEL if kind == "up" else 0)
                return gu1[0, bass.ds(g, 1), half * 512:(half + 1) * 512, c0:c0 + PANEL]\
                    .rearrange("a (k p) n -> p (a k) n", p=P)

            experts(1, first_mixture)
            for i in range(moe1_panel, len(panels)):
                load(i, i - SLOTS >= moe1_panel)
            for i in range(len(panels) - SLOTS, len(panels)):
                sync.wait_ge(S(panels[i][1]), panels[i][2])

            second = {"gate": ins["w1_2"], "up": ins["w3_2"], "down": ins["w2_2"]}

            def second_mixture(kind, g, member, half):
                rows = 256 if kind == "down" else 512
                v = second[kind][0].rearrange("(g m) a b -> g m a b", m=4)
                return v[bass.ds(g, 1), member, half * rows:(half + 1) * rows, :].rearrange("a (k p) n -> p (a k) n", p=P)

            experts(2, second_mixture)

        @block.gpsimd
        def _(pool):
            pool.dma_start(H[:, :, :], ins["x"][0].rearrange("(a p) d -> p a d", p=P)).then_inc(S("x_loaded"), 16)
            vrows = w_(0, VEC_TILES, P)
            for name, rows in VECTORS:
                v = ins[name]
                flat = v.rearrange("a (r q) -> (a r) q", q=P) if len(v.shape) == 2 else \
                    v.rearrange("a k (r q) -> (a k r) q", q=P)
                at, done = VEC_AT[name], 0
                while done < rows:
                    t, r = divmod(at + done, P)
                    n = min(rows - done, P - r)
                    pool.dma_start(vrows[r:r + n, t, :], flat[done:done + n, :]).then_inc(S("vectors_loaded"), 16)
                    done += n
            pool.dma_start(const[:, :], const_in[:, 0:RESIDENT]).then_inc(S("const_loaded"), 16)
            a, n = CONST_COLS["window"]
            pool.dma_start(w_(4736, 4 * T), const_in[:, a:a + n]).then_inc(S("window_loaded"), 16)
            pool.dma_start(poolw, ins["ev_pool_w"][0].rearrange("g c d -> c g d")).then_inc(S("poolw_loaded"), 16)
            pool.dma_start(router1[:, :, :], ins["od_router"][0].rearrange("(k p) e -> p k e", p=P)).then_inc(S("small_loaded"), 16)
            pool.dma_start(router, ins["router_w_2"].rearrange("(k p) e -> p k e", p=P)).then_inc(S("small_loaded"), 16)
            for dst, src in ((rbias, ins["router_b_2"]), (foxb, ins["fox_fb_2"][0]), (dgain, ins["diff_norm_g_2"][0]),
                             (hgain, ins["hgrn_norm_g_2"][0]), (lam4[:, 0, :], ins["lam_q1_2"][0]),
                             (lam4[:, 1, :], ins["lam_k1_2"][0]), (lam4[:, 2, :], ins["lam_q2_2"][0]),
                             (lam4[:, 3, :], ins["lam_k2_2"][0])):
                pool.dma_start(dst, src.partition_broadcast(P)).then_inc(S("small_loaded"), 16)

            def memory(turns, name):
                pool.wait_ge(S("turned"), turns)
                pool.dma_start(XS[:, :, :], ins[name][0].rearrange("(a p) d -> p a d", p=P)).then_inc(S("memory_loaded"), 16)

            loads = {0: 0, 1: 0}

            def row(b, src):
                if loads[b]:
                    pool.wait_ge(S(f"brow{b}_used"), loads[b])
                loads[b] += 1
                pool.dma_start(brow[:, b, :], src).then_inc(S(f"brow{b}_loaded"), 16)

            row(1, ins["final_norm"].partition_broadcast(P))
            memory(1, "mem")
            pool.wait_ge(S("pool_mixed"), 1)
            row(0, ins["od_pw2_b"][0].partition_broadcast(P))
            memory(5, "mem")
            row(0, ins["ln_in_g_2"].partition_broadcast(P))
            row(1, ins["ln_in_b_2"].partition_broadcast(P))
            a = CONST_COLS["causal"][0]
            row(0, const_in[:, a:a + D])
            pool.wait_ge(S("fox_scored"), 1)
            pool.dma_start(XT[:, :, :].rearrange("p k t -> p (k t)")[:, 0:a - RESIDENT], const_in[:, RESIDENT:a])\
                .then_inc(S("levels_loaded"), 16)
            row(1, ins["ln_g_2"][0, 0].partition_broadcast(P))
            row(0, ins["ln_b_2"][0, 0].partition_broadcast(P))
            memory(10, "mem_2")
            for j in (1, 2):
                row(1, ins["ln_g_2"][0, j].partition_broadcast(P))
                row(0, ins["ln_b_2"][0, j].partition_broadcast(P))
            pool.wait_ge(S("h_final"), 1)
            pool.dma_start(out[0].rearrange("(a p) d -> p a d", p=P), H[:, :, :]).then_inc(S("out_stored"), 16)
            pool.wait_ge(S("out_stored"), 16)

        @block.tensor
        def _(pe):
            mm = nc.tensor.matmul
            seen = {"turn": 0}

            def project(name):
                u = UNIT[name]
                _, _, _, n, columns, src = UNITS[u]
                x, pair = sources[src], PAIRS[u % 2]
                if u >= 2:
                    pe.wait_ge(S(f"unit_read{u % 2}"), u // 2)
                wait_panel(pe, unit_panel[u])
                w = slot_kn(slot(unit_panel[u]))
                if columns:
                    for fb in range(n // P):
                        for kc in range(KC):
                            last = mm(pair[:, fb // 2, fb % 2 * T:fb % 2 * T + T], w[:, kc, fb * P:(fb + 1) * P],
                                      x[:, kc, :], start=(kc == 0), stop=(kc == KC - 1))
                else:
                    for tc in range(HALVES):
                        for kc in range(KC):
                            last = mm(pair[:, tc, 0:n], x[:, kc, tc * P:(tc + 1) * P], w[:, kc, 0:n],
                                      start=(kc == 0), stop=(kc == KC - 1))
                last.then_inc(S(f"unit_ready{u % 2}"), 1)

            def turn(src, ready, n):
                pe.wait_ge(S(ready), n)
                if seen["turn"]:
                    pe.wait_ge(S("columns_by_act"), seen["turn"])
                    pe.wait_ge(S("columns_by_vector"), seen["turn"])
                seen["turn"] += 1
                for kc in range(KC):
                    for tc in range(HALVES):
                        o = kc % 2 * T + tc * P
                        last = nc.tensor.transpose(ps[:, 4 + kc // 2, o:o + P], src[:, tc, kc * P:(kc + 1) * P], IDENT)
                last.then_inc(S("turned"), 1)

            def columns_ready():
                pe.wait_ge(S("columns_by_act"), seen["turn"])
                pe.wait_ge(S("columns_by_vector"), seen["turn"])

            def turn_probabilities(n):
                pe.wait_ge(S("probs_ready"), n)
                pr = prob[n]
                for h in range(4):
                    for mc in range(2):
                        for tc in range(2):
                            j = h * 2 + mc
                            last = nc.tensor.transpose(ps[:, 4 + j // 2, j % 2 * T + tc * P:j % 2 * T + (tc + 1) * P],
                                                       pr[:, tc, h, mc * P:(mc + 1) * P], IDENT)
                last.then_inc(S("probs_turned"), 1)
                pe.wait_ge(S("probsT_by_act"), n)
                pe.wait_ge(S("probsT_by_vector"), n)

            def memory_projections(tag, ready, value):
                turn(XS, ready, value)
                columns_ready()
                for j in range(2):
                    project(f"{tag}k{j}")
                for j in range(2):
                    project(f"{tag}v{j}")

            def attention(tag, n, src, ready, value):
                turn(src, ready, value)
                columns_ready()
                for j in range(2):
                    project(f"{tag}q{j}")
                QT, KT, V, PT = w_(10240, KC, T), w_(6144, KC, T), w_(8192, HALVES, D), w_(2048, KC, T)
                for name in (f"{tag}v0", f"{tag}v1", f"{tag}q0", f"{tag}q1"):
                    u = UNIT[name]
                    pe.wait_ge(S(f"unit_read{u % 2}"), u // 2 + 1)
                for tc in range(2):
                    for h in range(4):
                        j = tc * 4 + h
                        for c in range(2):
                            last = mm(ps[:, 4 + j // 2, j % 2 * T:j % 2 * T + T], QT[:, 2 * h + c, tc * P:(tc + 1) * P],
                                      KT[:, 2 * h + c, :], start=(c == 0), stop=(c == 1))
                last.then_inc(S("scores_ready"), 1)
                turn_probabilities(n - (tag == "C"))
                for f in range(KC):
                    for mc in range(2):
                        last = mm(ps[:, 4 + f // 2, f % 2 * T:f % 2 * T + T], V[:, mc, f * P:(f + 1) * P],
                                  PT[:, f // 2 * 2 + mc, :], start=(mc == 0), stop=(mc == 1))
                last.then_inc(S("attended"), 1)
                k = "ABC".index(tag) + 1
                pe.wait_ge(S("attended_by_act"), k)
                pe.wait_ge(S("attended_by_vector"), k)
                for j in range(2):
                    project(f"{tag}o{j}")

            pe.wait_ge(S("vectors_loaded"), 16 * VEC_LOADS)
            pe.wait_ge(S("const_loaded"), 16)
            for t in range(VEC_TILES):
                n = min(P, VEC_ROWS - t * P)
                last = nc.tensor.transpose(ps[:, 4, t * P:t * P + n], w_(0, VEC_TILES, P)[0:n, t, :], IDENT[0:n, 0:n])
            last.then_inc(S("vectors_turned"), 1)
            pe.wait_ge(S("cols_ready"), 1)
            turn(XS, "xs_ready", 1)
            columns_ready()
            for n in ("h", "gb", "gc", "u"):
                project("in_" + n)
            memory_projections("A", "xs_ready", 2)
            pe.wait_ge(S("poolw_loaded"), 16)
            pe.wait_ge(S("pooled"), 1)
            for g in range(4):
                last = mm(ps[:, 4 + g // 2, g % 2 * T:g % 2 * T + T], poolw[:, g, :], w_(0, 4, T)[:, g, :],
                          start=True, stop=True)
            last.then_inc(S("pool_mixed"), 1)
            pe.wait_ge(S("mixed_by_act"), 1)
            pe.wait_ge(S("mixed_by_vector"), 1)
            for j in range(2):
                project(f"mix{j}")
            attention("A", 1, XS, "xs_ready", 3)
            turn(XS, "xs_ready", 4)
            columns_ready()
            for u in (FFN_AT - 1, FFN_AT - 2):
                pe.wait_ge(S(f"unit_read{u % 2}"), u // 2 + 1)

            def hidden(f):
                i = ffn_panel["gu", f]
                wait_panel(pe, i)
                w, pair = slot_kn(slot(i)), PAIRS[f % 2]
                if f >= 2:
                    pe.wait_ge(S("ffn_hidden"), f - 1)
                for part in range(2):
                    for fb in range(2):
                        for kc in range(KC):
                            c = part * T + fb * P
                            last = mm(pair[:, part, fb * T:(fb + 1) * T], w[:, kc, c:c + P], XT[:, kc, :],
                                      start=(kc == 0), stop=(kc == KC - 1))
                last.then_inc(S("ffn_hidden_products"), 1)

            def down(f):
                i = ffn_panel["down", f]
                wait_panel(pe, i)
                pe.wait_ge(S("ffn_hidden"), f + 1)
                w, hT = slot_rows(slot(i)), w_(512 * (f % 3), 2, T)
                for tc in range(2):
                    for n in range(2):
                        for fb in range(2):
                            last = mm(ps[:, 4 + tc * 2 + n, :], hT[:, fb, tc * P:(tc + 1) * P],
                                      w[:, fb, n * 512:(n + 1) * 512], start=(f == 0 and fb == 0),
                                      stop=(f == FFN_TURNS - 1 and fb == 1))
                last.then_inc(S("ffn_down_products"), 1)

            hidden(0)
            for f in range(1, FFN_TURNS):
                hidden(f)
                down(f - 1)
            down(FFN_TURNS - 1)
            pe.wait_ge(S("ffn_added"), 1)
            turn(XS, "xs_ready", 5)
            columns_ready()
            for j in range(2):
                project(f"gate{j}")
                project(f"value{j}")
            memory_projections("B", "xs_ready", 6)
            CO, SQ = w_(2304, KC, T), w_(0, KC, T)
            pe.wait_ge(S("convolved"), 1)
            for kc in range(KC):
                last = mm(ps[:, 4, 0:T], ONES, CO[:, kc, :], start=(kc == 0), stop=(kc == KC - 1))
            last.then_inc(S("feature_sums"), 1)
            pe.wait_ge(S("squared"), 1)
            for kc in range(KC):
                last = mm(ps[:, 5, 0:T], ONES, SQ[:, kc, :], start=(kc == 0), stop=(kc == KC - 1))
            last.then_inc(S("feature_sums"), 1)
            pe.wait_ge(S("conformed"), 1)
            for j in range(2):
                project(f"pw2_{j}")
            attention("B", 2, XS, "xs_ready", 7)

            def route(k, ready, value, src):
                turn(src, ready, value)
                columns_ready()
                pe.wait_ge(S("small_loaded"), 16 * 10)
                E, G = MOES[k]["experts"], MOES[k]["groups"]
                rt = router1 if k == 1 else router
                for tc in range(2):
                    for kc in range(KC):
                        last = mm(ps[:, 4, tc * 16:tc * 16 + E], XT[:, kc, tc * P:(tc + 1) * P], rt[:, kc, :],
                                  start=(kc == 0), stop=(kc == KC - 1))
                last.then_inc(S("logits_ready"), 1)
                pe.wait_ge(S("chosen"), k)
                before = c_("before")
                mm(ps[:, 5, 0:G], before, SEL[:, 0, 0:G], start=True, stop=True)
                mm(ps[:, 5, 8:8 + G], ONES, SEL[:, 0, 0:G], start=True, stop=False)
                mm(ps[:, 5, 8:8 + G], before, SEL[:, 1, 0:G], start=False, stop=True)
                mm(ps[:, 5, 16:16 + G], ONES, SEL[:, 0, 0:G], start=True, stop=False)
                mm(ps[:, 5, 16:16 + G], ONES, SEL[:, 1, 0:G], start=False, stop=True).then_inc(S("ranks_ready"), 1)

            def experts(k, x):
                c = MOES[k]
                M, NS, C, halves = c["members"], c["slots"], c["members"] * c["chunks"], stream(c)
                N = len(halves)
                PR, PT, Y, HID = w_(0, 2, P), w_(256, 2, P), w_(512, D), w_(1536, 4, P)

                def gather(turn):
                    pe.wait_ge(moe_sem(k, "picked"), turn + 1)
                    for tc in range(2):
                        mm(ps[:, 7, 0:M], PR[:, tc, :], CBS[:, tc, 0:M], start=(tc == 0), stop=(tc == 1))
                    for kc in range(KC):
                        for tc in range(2):
                            last = mm(ps[:, 5 + kc // 4, kc % 4 * P:kc % 4 * P + P], x[:, tc, kc * P:(kc + 1) * P],
                                      PR[:, tc, :], start=(tc == 0), stop=(tc == 1))
                    last.then_inc(moe_sem(k, "gathered"), 1)

                def turn_picks():
                    for tc in range(2):
                        last = nc.tensor.transpose(ps[:, 7, T + tc * P:T + (tc + 1) * P], PR[:, tc, :], IDENT)
                    last.then_inc(moe_sem(k, "picks_turned"), 1)

                def product(out_, x_parts, w_parts, start, stop):
                    (xh, xl), (wh, wl) = x_parts, w_parts
                    mm(out_, xh, wh, start=start, stop=False)
                    mm(out_, xl, wh, start=False, stop=False)
                    return mm(out_, xh, wl, start=False, stop=stop)

                pe.sem_inc(moe_sem(k, "read"), SPLITS)
                gather(0)
                pe.wait_ge(moe_sem(k, "gathered_split"), 1)
                turn_picks()
                pe.wait_ge(moe_sem(k, "turns_ready"), 1)
                turns = pe.value_load(count[0:1, k - 1:k], min_val=c["groups"], max_val=2 * c["groups"])
                with pe.Fori(0, turns) as it:
                    pe.wait_ge(moe_sem(k, "gathered_split"), it + 1)

                    def turn_hidden(ch):
                        pe.wait_ge(moe_sem(k, "gated"), it * C + (ch + 2))
                        for fb in range(4):
                            last = nc.tensor.transpose(ps[:, 4, fb * P:(fb + 1) * P], HID[:, fb, :], IDENT)
                        last.then_inc(moe_sem(k, "hidden_turned"), 1)

                    for j, (kind, ch, half) in enumerate(halves):
                        pe.wait_ge(moe_sem(k, "split"), it * N + (j + 1 + NS))
                        wh, wl = w_high[:, j % SPLITS, :], w_low[:, j % SPLITS, :]
                        if kind == "down":
                            if half == 0:
                                if ch == C - 1:
                                    gather(it + 1)
                                pe.wait_ge(moe_sem(k, "hidden_split"), it * C + (ch + 1))
                            for f in range(2):
                                fb = 2 * half + f
                                for n in range(2):
                                    o = f * D + n * 512
                                    last = product(ps[:, 2 + n, :], (h_high[:, fb, :], h_low[:, fb, :]),
                                                   (wh[:, o:o + 512], wl[:, o:o + 512]),
                                                   start=(ch == 0 and fb == 0), stop=(ch == C - 1 and fb == 3))
                        else:
                            bank = 0 if kind == "gate" else 1
                            if half == 0:
                                pe.wait_ge(moe_sem(k, "silu" if kind == "gate" else "gated"), it * C + (ch + 1))
                            for f in range(4):
                                kc, o = 4 * half + f, f * PANEL
                                last = product(ps[:, bank, :], (x_high[:, kc, :], x_low[:, kc, :]),
                                               (wh[:, o:o + PANEL], wl[:, o:o + PANEL]),
                                               start=(kc == 0), stop=(kc == KC - 1))
                        last.then_inc(moe_sem(k, "read"), 1)
                        for t in range(C):
                            if j == chunk_at(t) + 5:
                                turn_hidden(t)
                    pe.wait_ge(moe_sem(k, "outputs_by_act"), it + 1)
                    pe.wait_ge(moe_sem(k, "outputs_by_vector"), it + 1)
                    pe.wait_ge(moe_sem(k, "gathered_split"), it + 2)
                    pe.wait_ge(moe_sem(k, "picks_ready"), it + 1)
                    for j in range(4):
                        if j >= 2:
                            pe.wait_ge(moe_sem(k, "added"), it * 4 + (j - 1))
                        mm(ps[:, 5 + j % 2, :], PT[:, j // 2, :], Y[:, j % 2 * 512:(j % 2 + 1) * 512],
                           start=True, stop=True).then_inc(moe_sem(k, "scattered"), 1)
                    turn_picks()
                    pe.wait_ge(moe_sem(k, "added"), it * 4 + 4)
                pe.wait_ge(moe_sem(k, "picks_ready"), turns + 1)

            route(1, "xs_ready", 8, XS)
            experts(1, XS)
            turn(H, "h_ready", 1)
            columns_ready()
            for n in ("fqk", "dqk", "hq", "fv", "dv", "hf", "hi", "hg"):
                project(n)
            FQK, DQK, QH, KH = w_(0, 4, T), w_(1024, 4, T), w_(2048, 4, T), w_(3072, 4, T)
            LF, HI = w_(4096, 2, 512), w_(5120, 2, 512)
            FV, DV = w_(7168, 2, 256), w_(7680, 2, 256)
            PT = w_(10240, KC, T)
            pe.wait_ge(S("fox_log"), 1)
            upto, ones = c_("upto"), ONES
            mm(ps[:, 4, 0:4], upto, logf_fox[:, 0, :], start=True, stop=True)
            mm(ps[:, 4, 4:8], ones, logf_fox[:, 0, :], start=True, stop=False)
            mm(ps[:, 4, 4:8], upto, logf_fox[:, 1, :], start=False, stop=True).then_inc(S("fox_sums"), 1)
            for h in range(4):
                o = ps[:, 6 + h // 2, h % 2 * T:h % 2 * T + T]
                mm(o[:, 0:P], logf_fox[:, 0, h:h + 1].broadcast_to([P, P]), upto, start=True, stop=True)
                mm(o[:, P:T], logf_fox[:, 0, h:h + 1].broadcast_to([P, P]), ones, start=True, stop=False)
                last = mm(o[:, P:T], logf_fox[:, 1, h:h + 1].broadcast_to([P, P]), upto, start=False, stop=True)
            last.then_inc(S("fox_sums"), 1)
            pe.wait_ge(S("fox_bias"), 1)
            pe.wait_ge(S("recurrent_keys"), 1)
            KR = w_(8192, 2, 512)
            for h in range(4):
                for tc in range(2):
                    last = nc.tensor.transpose(ps[:, 4 + h // 2, h % 2 * T + tc * P:h % 2 * T + (tc + 1) * P],
                                               KR[:, tc, h * P:(h + 1) * P], IDENT)
            last.then_inc(S("keys_turned"), 1)
            pe.wait_ge(S("keys_columns"), 1)

            def small_attention(n, scores, v):
                scores()
                turn_probabilities(n)
                for tc in range(2):
                    for place, h in enumerate(HEAD_ORDER):
                        for mc in range(2):
                            last = mm(ps[:, 4, tc * T + h * 64:tc * T + h * 64 + 64], PT[:, place * 2 + mc, tc * P:(tc + 1) * P],
                                      v[:, mc, h * 64:(h + 1) * 64], start=(mc == 0), stop=(mc == 1))
                last.then_inc(S("small_attended"), 1)

            def fox_scores():
                u = UNIT["hg"]
                pe.wait_ge(S(f"unit_read{(u - 1) % 2}"), (u - 1) // 2 + 1)
                pe.wait_ge(S(f"unit_read{u % 2}"), u // 2 + 1)
                for tc in range(2):
                    for place, h in enumerate(HEAD_ORDER):
                        j, p0 = tc * 4 + place, 64 * (h % 2)
                        last = mm(ps[:, 4 + j // 2, j % 2 * T:j % 2 * T + T],
                                  FQK[p0:p0 + 64, h // 2, tc * P:(tc + 1) * P], FQK[p0:p0 + 64, 2 + h // 2, :],
                                  start=True, stop=True)
                last.then_inc(S("scores_ready"), 1)

            def diff_scores(which):
                for tc in range(2):
                    for place, h in enumerate(HEAD_ORDER):
                        j, p0 = tc * 4 + place, 64 * (h % 2) + 32 * which
                        last = mm(ps[:, 4 + j // 2, j % 2 * T:j % 2 * T + T],
                                  DQK[p0:p0 + 32, h // 2, tc * P:(tc + 1) * P], DQK[p0:p0 + 32, 2 + h // 2, :],
                                  start=True, stop=True)
                last.then_inc(S("scores_ready"), 1)

            small_attention(3, fox_scores, FV)
            pe.wait_ge(S("small_read"), 1)

            def both_maps():
                diff_scores(0)
                pe.wait_ge(S("diff_map"), 1)
                diff_scores(1)

            small_attention(4, both_maps, DV)
            pe.wait_ge(S("small_read"), 2)
            E, QE, KE, ST = w_(8192, 4, T), w_(9216, 4, T), w_(10240, 4, T), w_(11264, 8, P)
            for h in range(4):
                for tc in range(2):
                    last = mm(ps[:, h // 2, h % 2 * T + tc * P:h % 2 * T + (tc + 1) * P],
                              KH[:, h, tc * P:(tc + 1) * P], QH[:, h, tc * P:(tc + 1) * P], start=True, stop=True)
            last.then_inc(S("level_scores"), 1)
            pe.wait_ge(S("levels_loaded"), 16)
            for lv in range(8):
                if lv:
                    pe.wait_ge(S("level_exp"), lv)
                for h in range(4):
                    for tc in range(2):
                        sp = c_(f"span{lv}") if lv < 7 else (c_("after") if tc == 0 else upto)
                        last = mm(ps[:, 4 + h // 2, h % 2 * T + tc * P:h % 2 * T + (tc + 1) * P],
                                  LF[:, tc, h * P:(h + 1) * P], sp, start=True, stop=True)
                last.then_inc(S("level_spans"), 1)
                pe.wait_ge(S("level_decayed"), lv + 1)
                pe.wait_ge(S("level_merged"), lv + 1)
                if lv < 7:
                    for h in range(4):
                        for tc in range(2):
                            last = mm(ps[:, h // 2, h % 2 * T + tc * P:h % 2 * T + (tc + 1) * P],
                                      KE[:, h, tc * P:(tc + 1) * P], QE[:, h, tc * P:(tc + 1) * P], start=True, stop=True)
                else:
                    for h in range(4):
                        last = mm(ps[:, 0, h * P:(h + 1) * P], KE[:, h, 0:P], QE[:, h, P:T], start=True, stop=True)
                last.then_inc(S("level_scores"), 1)
            pe.wait_ge(S("level_merged"), 9)
            CR = w_(8192, 4, P)
            for h in range(4):
                v = lambda tc: HI[:, tc, h * P:(h + 1) * P]
                mm(ps[:, 2, h * P:(h + 1) * P], ST[:, 2 * h, :], v(0), start=True, stop=True)
                mm(ps[:, 3, h * P:(h + 1) * P], ST[:, 2 * h + 1, :], v(1), start=True, stop=False)
                last = mm(ps[:, 3, h * P:(h + 1) * P], CR[:, h, :], v(0), start=False, stop=True)
            last.then_inc(S("recurrence_out"), 1)
            turn(XS, "xs_ready", 9)
            columns_ready()
            for j in range(2):
                project(f"out{j}")
            memory_projections("C", "memory_loaded", 48)
            attention("C", 6, H, "h_ready", 2)
            route(2, "h_ready", 3, H)
            experts(2, H)

        @block.scalar
        def _(act):
            A = nc.scalar.activation
            n_ = {"sq": 0, "sqrt": 0, "turn": 0}
            step = Steps(act, S("scalar_step"))

            def squares(src, ready, n, junk=XS):
                act.wait_ge(S(ready), n)
                if n_["sq"]:
                    act.wait_ge(S("variance_ready"), n_["sqrt"])
                n_["sq"] += 1
                step(A(junk[:, 0, :], src[:, 0, :], ACT.Square, accum_out=ssq[:, 0:1]))
                A(junk[:, 1, :], src[:, 1, :], ACT.Square, accum_out=ssq[:, 1:2]).then_inc(S("squares_summed"), 1)

            def root(n=2, src=None, dst=None):
                n_["sqrt"] += 1
                act.wait_ge(S("variance_ready"), n_["sqrt"])
                A(dst if dst is not None else std, src if src is not None else var, ACT.Sqrt).then_inc(S("deviation_ready"), 1)

            def rms(src, ready, n, junk=XS):
                squares(src, ready, n, junk)
                root()

            def columns(dst, gain, banks=(4, 5)):
                n_["turn"] += 1
                act.wait_ge(S("turned"), n_["turn"])
                for kc in range(4):
                    src = ps[:, 4 + kc // 2, kc % 2 * T:kc % 2 * T + T]
                    if gain is None:
                        last = A(dst[:, kc, :], src, ACT.Copy)
                    else:
                        last = A(dst[:, kc, :], src, ACT.Copy, scale=vec(gain[0], gain[1] + kc))
                last.then_inc(S("columns_by_act"), 1)

            def take(name, dst, func=ACT.Copy, **kw):
                u = UNIT[name]
                unit_ready(act, u)
                A(dst, PAIRS[u % 2], func, **kw).then_inc(S(f"unit_read{u % 2}"), 1)

            def take_columns(name, dst):
                u = UNIT[name]
                unit_ready(act, u)
                A(dst, PAIRS[u % 2].rearrange("p a (b t) -> p (a b) t", t=T), ACT.Copy).then_inc(S(f"unit_read{u % 2}"), 1)

            def softmax(n, scale, dst, src_sbuf=None):
                act.wait_ge(S("softmax_bias"), n)
                for j in range(8):
                    src = ps[:, 4 + j // 2, j % 2 * T:j % 2 * T + T] if src_sbuf is None else src_sbuf[:, j // 4, j % 4, :]
                    last = A(dst[:, j // 4, j % 4, :], src, ACT.Exp, bias=nbias[:, j:j + 1], scale=scale,
                             accum_out=den[:, j:j + 1])
                last.then_inc(S("exponentials"), 1)

            def probs_columns(n, dst):
                act.wait_ge(S("probs_turned"), n)
                A(dst[:, 0:4, :], ps[:, 4:6, :].rearrange("p a (b t) -> p (a b) t", t=T), ACT.Copy).then_inc(S("probsT_by_act"), 1)

            def memory_norm(tag):
                rms(XS, "memory_loaded", 16 * ("ABC".index(tag) + 1), junk=w_(10240, HALVES, D))

            def memory_projections(tag, gain):
                if gain:
                    columns(XT, gain)
                for j in range(2):
                    take_columns(f"{tag}k{j}", w_(6144, KC, T)[:, 4 * j:4 * j + 4, :])
                for j in range(2):
                    take(f"{tag}v{j}", w_(8192, HALVES, D)[:, :, j * 512:(j + 1) * 512])

            def attention(tag, n, gain, ready):
                QT, PT = w_(10240, KC, T), w_(2048, KC, T)
                if ready:
                    rms(H, *ready)
                columns(XT, gain)
                take_columns(f"{tag}q0", QT[:, 0:4, :])
                softmax(n, 1.0 / 16, w_(0, 2, 4, T))
                probs_columns(n - (tag == "C"), PT)
                act.wait_ge(S("attended"), "ABC".index(tag) + 1)
                A(XT[:, 0:4, :], ps[:, 4:6, :].rearrange("p a (b t) -> p (a b) t", t=T), ACT.Copy).then_inc(S("attended_by_act"), 1)

            act.wait_ge(S("vectors_turned"), 1)
            A(cols[:, 0:VEC_ROWS], ps[:, 4, 0:VEC_ROWS], ACT.Copy).then_inc(S("cols_ready"), 1)
            act.wait_ge(S("cols_ready"), 1)
            rms(H, "x_loaded", 16)
            columns(XT, ("ev_norm_mix", 0))
            take_columns("in_h", w_(0, 4, T))
            take_columns("in_gb", w_(1024, 4, T))
            memory_norm("A")
            memory_projections("A", ("xa_norm_mem", 0))
            act.wait_ge(S("pool_mixed"), 1)
            for g in range(4):
                last = A(w_(10240, KC, T)[:, 4 + g, :], ps[:, 4 + g // 2, g % 2 * T:g % 2 * T + T], ACT.Copy,
                         scale=vec("ev_pool_scale", g))
            last.then_inc(S("mixed_by_act"), 1)
            attention("A", 1, ("xa_norm", 0), ("h_updated", 1))
            rms(H, "h_updated", 2)
            columns(XT, ("ev_norm_ffn", 0))
            for f in range(FFN_TURNS):
                act.wait_ge(S("ffn_hidden_products"), f + 1)
                if f >= 2:
                    act.wait_ge(S("ffn_hidden"), f - 1)
                A(w_(2048 + 512 * (f % 2), 512), PAIRS[f % 2][:, 0, :], ACT.Silu).then_inc(S("ffn_silu"), 1)
            rms(H, "ffn_added", 1)
            columns(XT, ("od_norm_mix", 0))
            for j in range(2):
                u = UNIT[f"gate{j}"]
                unit_ready(act, u)
                if j:
                    act.wait_ge(S("glu"), 1)
                src = PAIRS[u % 2].rearrange("p a (b t) -> p (a b) t", t=T)
                for b in range(4):
                    last = A(w_(2304, 4, T)[:, b, :], src[:, b, :], ACT.Sigmoid, bias=vec("od_pw1_b", 8 + 4 * j + b))
                last.then_inc(S(f"unit_read{u % 2}"), 1)
                if j == 0:
                    memory_norm("B")
            memory_projections("B", ("xa_norm_mem", 8))
            root(src=w_(4608, T), dst=w_(4864, T))
            act.wait_ge(S("standard"), 1)
            for kc in range(KC):
                last = A(w_(2304, KC, T)[:, kc, :], w_(2304, KC, T)[:, kc, :], ACT.Silu, scale=vec("od_ln_g", kc),
                         bias=vec("od_ln_b", kc))
            last.then_inc(S("conformed"), 1)
            attention("B", 2, ("xa_norm", 8), ("h_updated", 3))

            def experts(k, gain):
                c = MOES[k]
                NS, C, halves = c["slots"], c["members"] * c["chunks"], stream(c)
                N = len(halves)
                Y, SG = w_(512, D), w_(2048, PANEL)
                uses = {q: sum(1 for j in range(N) if j % NS == q) for q in range(NS)}

                def gathered_high(turn):
                    act.wait_ge(moe_sem(k, "gathered"), turn + 1)
                    if gain:
                        for kc in range(KC):
                            last = A(x_high[:, kc, :], ps[:, 5 + kc // 4, kc % 4 * P:kc % 4 * P + P], ACT.Copy,
                                     scale=vec(gain, kc))
                    else:
                        for b in range(2):
                            last = A(x_high[:, 4 * b:4 * b + 4, :], ps[:, 5 + b, :].rearrange("p (k t) -> p k t", t=P), ACT.Copy)
                    last.then_inc(moe_sem(k, "gathered_high"), 1)

                gathered_high(0)
                act.wait_ge(moe_sem(k, "turns_ready"), 1)
                turns = act.value_load(count[0:1, k - 1:k], min_val=c["groups"], max_val=2 * c["groups"])
                with act.Fori(0, turns) as it:

                    def silu(ch):
                        act.wait_ge(moe_sem(k, "read"), it * N + (chunk_at(ch) + 2 + SPLITS))
                        A(SG, ps[:, 0, :], ACT.Silu).then_inc(moe_sem(k, "silu"), 1)

                    def hidden_high(ch):
                        act.wait_ge(moe_sem(k, "hidden_turned"), it * C + (ch + 1))
                        A(h_high[:, :, :], ps[:, 4, :].rearrange("p (k t) -> p k t", t=P), ACT.Copy)\
                            .then_inc(moe_sem(k, "hidden_high"), 1)

                    for j in range(N):
                        for ch in range(C):
                            if j == chunk_at(ch) + 4:
                                silu(ch)
                            if j == chunk_at(ch) + 8:
                                hidden_high(ch)
                        act.wait_ge(moe_sem(k, f"landed{j % NS}"), it * (16 * uses[j % NS]) + 16 * (j // NS + 1))
                        act.wait_ge(moe_sem(k, "read"), it * N + (j + 1))
                        A(w_high[:, j % SPLITS, :], ring[:, j % NS, :], ACT.Copy).then_inc(moe_sem(k, "high"), 1)
                    hidden_high(C - 1)
                    gathered_high(it + 1)
                    act.wait_ge(moe_sem(k, "read"), it * N + (N + SPLITS))
                    A(Y[:, 0:512], ps[:, 2, :], ACT.Copy).then_inc(moe_sem(k, "outputs_by_act"), 1)

            rms(H, "h_updated", 4)
            columns(XT, ("od_norm_moe", 0))
            act.wait_ge(S("logit_gap"), 1)
            A(PAIRW[:, 1, :], PAIRW[:, 0, :], ACT.Exp).then_inc(S("gap_exp"), 1)
            experts(1, "od_norm_moe")
            rms(H, "moe_done", 1)
            root()
            columns(XT, None)
            take_columns("dqk", w_(1024, 4, T))
            u = UNIT["hq"]
            unit_ready(act, u)
            A(w_(2048, 4, T), PAIRS[u % 2].rearrange("p a (b t) -> p (a b) t", t=T), ACT.Silu).then_inc(S(f"unit_read{u % 2}"), 1)
            act.wait_ge(S("lam_sums"), 1)
            A(lame, lamp, ACT.Exp).then_inc(S("lam_exp"), 1)
            act.wait_ge(S("fox_logits"), 1)
            step(A(ffa, ffl, ACT.Abs))
            step(A(ffa, ffa, ACT.Exp, scale=-1.0))
            A(ffa, ffa, ACT.Ln, bias=1.0).then_inc(S("fox_log1p"), 1)
            HFZ, HFA, KR = w_(9216, 2, 512), w_(4096, 2, 512), w_(8192, 2, 512)
            act.wait_ge(S("forget_logits"), 1)
            step(A(HFA, HFZ, ACT.Abs))
            step(A(HFA, HFA, ACT.Exp, scale=-1.0))
            A(HFA, HFA, ACT.Ln, bias=1.0).then_inc(S("forget_log1p"), 1)
            A(KR, HFZ, ACT.Sigmoid, scale=-1.0).then_inc(S("recurrent_keys"), 1)
            take("hi", w_(5120, 2, 512))
            u = UNIT["hg"]
            unit_ready(act, u)
            A(w_(6144, 2, 512), PAIRS[u % 2], ACT.Silu).then_inc(S(f"unit_read{u % 2}"), 1)
            act.wait_ge(S("keys_turned"), 1)
            A(w_(3072, 4, T), ps[:, 4:6, :].rearrange("p a (b t) -> p (a b) t", t=T), ACT.Copy).then_inc(S("keys_columns"), 1)
            PR, PT = w_(8192, 2, 4, T), w_(10240, KC, T)
            softmax(3, 1.0, PR, PR)
            probs_columns(3, PT)
            softmax(4, 1.0, PR, PR)
            softmax(5, 1.0, w_(10240, 2, 4, T), w_(10240, 2, 4, T))
            probs_columns(4, PT)
            root(src=dss, dst=dstd)
            for lv in range(8):
                act.wait_ge(S("level_spans"), lv + 1)
                if lv:
                    act.wait_ge(S("level_decayed"), lv)
                else:
                    act.wait_ge(S("diff_done"), 1)
                A(w_(8192, 4, T), ps[:, 4:6, :].rearrange("p a (b t) -> p (a b) t", t=T), ACT.Exp).then_inc(S("level_exp"), 1)
            root(src=dss, dst=dstd)
            columns(XT, None)
            columns(XT, None)
            root()
            memory_projections("C", None)
            attention("C", 6, None, None)
            root()
            columns(XT, None)
            act.wait_ge(S("logits_ready"), 2)
            A(LG, ps[:, 4, 0:32].rearrange("p (a e) -> p a e", e=16), ACT.Sigmoid).then_inc(S("router_scores"), 1)
            experts(2, None)
            root()

        @block.vector
        def _(dve):
            V = nc.vector
            step = Steps(dve, S("vector_step"))
            n_ = {"sq": 0, "rt": 0, "xs": 0, "turn": 0, "b0": 0, "b1": 0}
            MUL, ADD, SUB = ALU.mult, ALU.add, ALU.subtract

            def rsqrt(dst=None, src=None):
                n_["rt"] += 1
                dve.wait_ge(S("deviation_ready"), n_["rt"])
                step(V.reciprocal(dst if dst is not None else rstd, src if src is not None else std))

            def rms(src, dst, eps):
                n_["sq"] += 1
                dve.wait_ge(S("squares_summed"), n_["sq"])
                V.tensor_scalar(var, ssq, 1.0 / D, eps, MUL, ADD).then_inc(S("variance_ready"), 1)
                rsqrt()
                for tc in range(2):
                    last = V.tensor_scalar(dst[:, tc, :], src[:, tc, :], rstd[:, tc:tc + 1], None, MUL)
                last.then_inc(S("xs_ready"), 1)

            def columns(dst, gain):
                n_["turn"] += 1
                dve.wait_ge(S("turned"), n_["turn"])
                for kc in range(4, 8):
                    src = ps[:, 4 + kc // 2, kc % 2 * T:kc % 2 * T + T]
                    if gain is None:
                        last = V.tensor_copy(dst[:, kc, :], src)
                    else:
                        last = V.tensor_scalar(dst[:, kc, :], src, vec(gain[0], gain[1] + kc), None, MUL)
                last.then_inc(S("columns_by_vector"), 1)

            def take(name, dst):
                u = UNIT[name]
                unit_ready(dve, u)
                V.tensor_copy(dst, PAIRS[u % 2]).then_inc(S(f"unit_read{u % 2}"), 1)

            def take_columns(name, dst):
                u = UNIT[name]
                unit_ready(dve, u)
                V.tensor_copy(dst, PAIRS[u % 2].rearrange("p a (b t) -> p (a b) t", t=T)).then_inc(S(f"unit_read{u % 2}"), 1)

            def add_unit(name, j, scale=None, signal=None):
                u = UNIT[name]
                unit_ready(dve, u)
                h = H[:, :, j * 512:(j + 1) * 512]
                if scale is None:
                    ins = V.tensor_tensor(h, h, PAIRS[u % 2], ADD)
                else:
                    ins = V.scalar_tensor_tensor(h, h, scale, PAIRS[u % 2], MUL, ADD)
                ins.then_inc(S(f"unit_read{u % 2}"), 1)

            def update_done(name):
                u = UNIT[name]
                for w in (u - 1, u):
                    dve.wait_ge(S(f"unit_read{w % 2}"), w // 2 + 1)

            def use_row(b, last):
                last.then_inc(S(f"brow{b}_used"), 1)
                dve.wait_ge(S(f"brow{b}_used"), n_[f"b{b}"])

            def row(b):
                n_[f"b{b}"] += 1
                dve.wait_ge(S(f"brow{b}_loaded"), 16 * n_[f"b{b}"])
                return brow[:, b, :]

            def layer_norm(signal):
                step(V.tensor_reduce(mean, H[:, :, :], X, ADD))
                step(V.tensor_scalar(mean, mean, 1.0 / D, None, MUL))
                for tc in range(2):
                    last = V.tensor_scalar(H[:, tc, :], H[:, tc, :], mean[:, tc:tc + 1], None, SUB)
                step(last)
                for tc in range(2):
                    last = V.tensor_tensor_reduce(out=w_(0, HALVES, D)[:, tc, :], in0=H[:, tc, :], in1=H[:, tc, :], scale=1.0, scalar=0.0,
                                                  op0=MUL, op1=ADD, accum_out=ssq[:, tc:tc + 1])
                step(last)
                V.tensor_scalar(var, ssq, 1.0 / D, LN_EPS, MUL, ADD).then_inc(S("variance_ready"), 1)
                rsqrt()
                g = row(gain_row[0])
                for tc in range(2):
                    last = V.scalar_tensor_tensor(H[:, tc, :], H[:, tc, :], rstd[:, tc:tc + 1], g, MUL, MUL)
                use_row(gain_row[0], last)
                b = row(1 - gain_row[0])
                last = V.tensor_tensor(H[:, :, :], H[:, :, :], b.rearrange("p (a n) -> p a n", a=1).broadcast_to([P, 2, D]), ADD)
                use_row(1 - gain_row[0], last)
                gain_row[0] = 1
                dve.sem_inc(S(signal), 1)

            gain_row = [0]

            def scores_max(n, src, scale, out_n):
                step(V.tensor_reduce(mx, src, X, ALU.max))
                V.tensor_scalar(nbias, mx, -scale, None, MUL).then_inc(S("softmax_bias"), 1)

            def normalise(n, probs):
                dve.wait_ge(S("exponentials"), n)
                step(V.reciprocal(rden, den))
                flat = probs.rearrange("p a h t -> p (a h) t")
                return V.tensor_tensor(flat, flat, rden.rearrange("p (a b) -> p a b", b=1).broadcast_to([P, 8, T]), MUL)

            def probs_columns(n, dst):
                dve.wait_ge(S("probs_turned"), n)
                V.tensor_copy(dst[:, 4:8, :], ps[:, 6:8, :].rearrange("p a (b t) -> p (a b) t", t=T)).then_inc(S("probsT_by_vector"), 1)

            def attention(tag, n, gain):
                QT, PT = w_(10240, KC, T), w_(2048, KC, T)
                if gain:
                    rms(H, XS, EPS)
                columns(XT, gain)
                take_columns(f"{tag}q1", QT[:, 4:8, :])
                dve.wait_ge(S("scores_ready"), n)
                scores_max(n, ps[:, 4:8, :].rearrange("p a (b t) -> p (a b) t", t=T), 1.0 / 16, n)
                normalise(n, w_(0, 2, 4, T)).then_inc(S("probs_ready"), 1)
                probs_columns(n - (tag == "C"), PT)
                dve.wait_ge(S("attended"), "ABC".index(tag) + 1)
                V.tensor_copy(XT[:, 4:8, :], ps[:, 6:8, :].rearrange("p a (b t) -> p (a b) t", t=T)).then_inc(S("attended_by_vector"), 1)
                for j in range(2):
                    add_unit(f"{tag}o{j}", j, ALPHA if tag == "C" else None)
                update_done(f"{tag}o1")

            dve.wait_ge(S("x_loaded"), 16)
            dve.wait_ge(S("cols_ready"), 1)
            rms(H, XS, EPS)
            columns(XT, ("ev_norm_mix", 0))
            AP_, UP = w_(2048, 4, 258), w_(3084, 4, 272)
            V.memset(AP_, 0.0)
            step(V.memset(UP, 0.0))
            u = UNIT["in_gc"]
            unit_ready(dve, u)
            dve.wait_ge(S(f"unit_read{UNIT['in_h'] % 2}"), 1)
            V.tensor_tensor(AP_[:, :, 1:257], w_(0, 4, T), PAIRS[u % 2].rearrange("p a (b t) -> p (a b) t", t=T), MUL)\
                .then_inc(S(f"unit_read{u % 2}"), 1)
            take_columns("in_u", UP[:, :, 8:264])
            dve.wait_ge(S("unit_read0"), 2)
            dve.wait_ge(S("unit_read1"), 2)
            MIXT, INV, PO = w_(10240, KC, T), w_(4736, 4, T), w_(0, 4, T)
            CT = MIXT[:, 0:4, :]
            rms(XS, XS, EPS)
            columns(XT, ("xa_norm_mem", 0))
            dve.wait_ge(S("window_loaded"), 16)
            for k in range(3):
                for b in range(4):
                    wv = vec("ev_conv_a", 4 * k + b)
                    if k == 0:
                        last = V.tensor_scalar(CT[:, b, :], AP_[:, b, 0:T], wv, None, MUL)
                    else:
                        last = V.scalar_tensor_tensor(CT[:, b, :], AP_[:, b, k:k + T], wv, CT[:, b, :], MUL, ADD)
                step(last)
            V.tensor_tensor(MIXT[:, 0:4, :], CT, w_(1024, 4, T), MUL).then_inc(S("mixed_by_vector"), 1)
            SA, SB_ = w_(4172, 272), w_(4444, 272)
            for g, win in enumerate(WINDOWS):
                cur, size, nxt = UP[:, g, :], 1, SA
                while size < win:
                    n = 272 - 2 * size
                    step(V.tensor_tensor(nxt[:, 0:n], cur[:, 0:n], cur[:, size:size + n], ADD))
                    cur, nxt, size = nxt, (SB_ if nxt is SA else SA), size * 2
                at = 8 - win // 2
                step(V.tensor_tensor(PO[:, g, :], cur[:, at:at + T], INV[:, g, :], MUL))
                last = V.tensor_tensor(PO[:, g, :], PO[:, g, :], UP[:, g, 8:264], SUB)
                step(last)
            dve.sem_inc(S("pooled"), 1)
            dve.wait_ge(S("mixed_by_act"), 1)
            dve.wait_ge(S("mixed_by_vector"), 1)
            for j in range(2):
                add_unit(f"mix{j}", j)
            update_done("mix1")
            dve.sem_inc(S("h_updated"), 1)
            attention("A", 1, ("xa_norm", 0))
            dve.sem_inc(S("h_updated"), 1)
            rms(H, XS, EPS)
            columns(XT, ("ev_norm_ffn", 0))
            for f in range(FFN_TURNS):
                dve.wait_ge(S("ffn_silu"), f + 1)
                if f >= 3:
                    dve.wait_ge(S("ffn_down_products"), f - 2)
                V.tensor_tensor(w_(512 * (f % 3), 512), w_(2048 + 512 * (f % 2), 512), PAIRS[f % 2][:, 1, :], MUL)\
                    .then_inc(S("ffn_hidden"), 1)
            dve.wait_ge(S("ffn_down_products"), FFN_TURNS)
            V.tensor_tensor(H[:, :, :], H[:, :, :], ps[:, 4:8, :].rearrange("p (a b) n -> p a (b n)", a=2), ADD)\
                .then_inc(S("ffn_added"), 1)
            dve.wait_ge(S("ffn_added"), 1)
            rms(H, XS, EPS)
            columns(XT, ("od_norm_mix", 0))
            HC, CO, SQ = w_(0, KC, 286), w_(2304, KC, T), w_(0, KC, T)
            MEAN, VAR, STD, RST = w_(4352, T), w_(4608, T), w_(4864, T), w_(5120, T)
            step(V.memset(HC, 0.0))
            for j in range(2):
                u, ug = UNIT[f"value{j}"], UNIT[f"gate{j}"]
                unit_ready(dve, u)
                dve.wait_ge(S(f"unit_read{ug % 2}"), ug // 2 + 1)
                src = PAIRS[u % 2].rearrange("p a (b t) -> p (a b) t", t=T)
                for b in range(4):
                    last = V.scalar_tensor_tensor(HC[:, 4 * j + b, 15:15 + T], src[:, b, :], vec("od_pw1_b", 4 * j + b),
                                                  w_(2304, 4, T)[:, b, :], ADD, MUL)
                last.then_inc(S(f"unit_read{u % 2}"), 1)
                dve.wait_ge(S(f"unit_read{u % 2}"), u // 2 + 1)
                dve.sem_inc(S("glu"), 1)
                if j == 0:
                    rms(XS, XS, EPS)
            columns(XT, ("xa_norm_mem", 8))
            for k in range(CONV):
                for kc in range(KC):
                    wv = vec("od_dw_w", KC * k + kc)
                    if k == 0:
                        last = V.tensor_scalar(CO[:, kc, :], HC[:, kc, 0:T], wv, vec("od_dw_b", kc), MUL, ADD)
                    else:
                        last = V.scalar_tensor_tensor(CO[:, kc, :], HC[:, kc, k:k + T], wv, CO[:, kc, :], MUL, ADD)
                step(last)
            dve.sem_inc(S("convolved"), 1)
            dve.wait_ge(S("feature_sums"), 1)
            step(V.tensor_scalar(MEAN, ps[:, 4, 0:T], 1.0 / D, None, MUL))
            rep = lambda a: a.rearrange("p (a t) -> p a t", a=1).broadcast_to([P, KC, T])
            step(V.tensor_tensor(CO, CO, rep(MEAN), SUB))
            V.tensor_tensor(SQ, CO, CO, MUL).then_inc(S("squared"), 1)
            dve.wait_ge(S("feature_sums"), 2)
            V.tensor_scalar(VAR, ps[:, 5, 0:T], 1.0 / D, EPS, MUL, ADD).then_inc(S("variance_ready"), 1)
            rsqrt(RST, STD)
            V.tensor_tensor(CO, CO, rep(RST), MUL).then_inc(S("standard"), 1)
            b = row(0)
            use_row(0, V.tensor_tensor(H[:, :, :], H[:, :, :], b.rearrange("p (a n) -> p a n", a=1).broadcast_to([P, 2, D]), ADD))
            for j in range(2):
                add_unit(f"pw2_{j}", j)
            update_done("pw2_1")
            dve.sem_inc(S("h_updated"), 1)
            attention("B", 2, ("xa_norm", 8))
            dve.sem_inc(S("h_updated"), 1)

            def first_best(values, a, n, best, pick, tmp):
                v3 = lambda t: t.rearrange("p (a n) -> p a n", n=1).broadcast_to([P, a, n])
                iom = IOM[:, 0:n].rearrange("p (a n) -> p a n", a=1).broadcast_to([P, a, n])
                step(V.tensor_reduce(best, values, X, ALU.max))
                step(V.tensor_tensor(tmp, values, v3(best), ALU.is_equal))
                step(V.tensor_tensor(tmp, tmp, iom, MUL))
                step(V.tensor_reduce(VI[:, 0:a], tmp, X, ALU.min))
                step(V.tensor_tensor(pick, iom, v3(VI[:, 0:a]), ALU.is_equal))

            def remove(values, pick):
                step(V.scalar_tensor_tensor(values, pick, -REMOVED, values, MUL, ADD))

            def ranks(k):
                c = MOES[k]
                G, M = c["groups"], c["members"]
                dve.wait_ge(S("ranks_ready"), k)
                r = ps[:, 5, 0:16].rearrange("p (a e) -> p a e", e=8)[:, :, 0:G]
                step(V.scalar_tensor_tensor(RK[:, :, 0:G], r, 1.0, SEL[:, :, 0:G], ADD, MUL))
                step(V.tensor_scalar(RK[:, :, 0:G], RK[:, :, 0:G], -1.0, None, ADD))
                V.tensor_scalar(RK[:, :, G:2 * G], RK[:, :, 0:G], -float(P), None, ADD)
                V.memset(RK[:, :, 2 * G:2 * G + 1], -1.0)
                V.memset(CB[:, :, 2 * G * M:(2 * G + 1) * M], 0.0)
                V.tensor_copy(CB[:, :, G * M:2 * G * M], CB[:, :, 0:G * M])
                step(V.tensor_reduce(CMAX, ps[:, 5, 16:16 + G], X, ALU.max))
                step(V.tensor_scalar(CMAX, CMAX, float(P), float(G), ALU.is_gt, MUL))
                V.tensor_scalar(count[:, k - 1:k], CMAX, float(G), None, ADD).then_inc(moe_sem(k, "turns_ready"), 1)

            def experts(k, dst, gain):
                c = MOES[k]
                M, C, halves = c["members"], c["members"] * c["chunks"], stream(c)
                N, NS = len(halves), c["slots"]
                PR, PT, Y, HID, SG = w_(0, 2, P), w_(256, 2, P), w_(512, D), w_(1536, PANEL), w_(2048, PANEL)
                iota = c_("iota")

                def pick(turn):
                    for tc in range(2):
                        V.tensor_copy(CBS[:, tc, 0:M], CB[:, tc, bass.ds(turn * M, M)])
                        last = V.tensor_scalar(PR[:, tc, :], iota, RK[:, tc, bass.ds(turn, 1)], None, ALU.is_equal)
                    last.then_inc(moe_sem(k, "picked"), 1)

                def gathered_low(turn):
                    dve.wait_ge(moe_sem(k, "gathered_high"), turn + 1)
                    if gain:
                        for kc in range(KC):
                            V.scalar_tensor_tensor(x_low[:, kc, :], ps[:, 5 + kc // 4, kc % 4 * P:kc % 4 * P + P], vec(gain, kc),
                                                   x_high[:, kc, :].bitcast(F32), MUL, SUB)
                    else:
                        V.tensor_tensor(x_low[:, :, :], ps[:, 5:7, :].rearrange("p b (k t) -> p (b k) t", t=P),
                                        x_high[:, :, :].bitcast(F32), SUB)
                    V.tensor_copy(GS[:, 0:M], ps[:, 7, 0:M]).then_inc(moe_sem(k, "gathered_split"), 1)

                def picks_ready(turn):
                    dve.wait_ge(moe_sem(k, "picks_turned"), turn + 1)
                    V.tensor_copy(PT, ps[:, 7, T:2 * T].rearrange("p (a t) -> p a t", t=P)).then_inc(moe_sem(k, "picks_ready"), 1)

                dve.sem_inc(moe_sem(k, "silu"), 1)
                dve.sem_inc(moe_sem(k, "gated"), 1)
                pick(0)
                gathered_low(0)
                picks_ready(0)
                dve.wait_ge(moe_sem(k, "turns_ready"), 1)
                turns = dve.value_load(count[0:1, k - 1:k], min_val=c["groups"], max_val=2 * c["groups"])
                with dve.Fori(0, turns) as it:

                    def hidden_rows(ch):
                        dve.wait_ge(moe_sem(k, "read"), it * N + (chunk_at(ch) + 4 + SPLITS))
                        dve.wait_ge(moe_sem(k, "silu"), it * C + (ch + 2))
                        m = ch // c["chunks"]
                        V.scalar_tensor_tensor(HID, ps[:, 1, :], GS[:, m:m + 1], SG, MUL, MUL).then_inc(moe_sem(k, "gated"), 1)

                    def hidden_low(ch):
                        dve.wait_ge(moe_sem(k, "hidden_high"), it * C + (ch + 1))
                        V.tensor_tensor(h_low[:, :, :], ps[:, 4, :].rearrange("p (k t) -> p k t", t=P),
                                        h_high[:, :, :].bitcast(F32), SUB).then_inc(moe_sem(k, "hidden_split"), 1)

                    for j in range(N):
                        if j == 6:
                            pick(it + 1)
                        for ch in range(C):
                            if j == chunk_at(ch) + 6:
                                hidden_rows(ch)
                            if j == chunk_at(ch) + 8:
                                hidden_low(ch)
                        dve.wait_ge(moe_sem(k, "high"), it * N + (j + 1))
                        V.tensor_tensor(w_low[:, j % SPLITS, :], ring[:, j % NS, :], w_high[:, j % SPLITS, :].bitcast(F32), SUB)\
                            .then_inc(moe_sem(k, "split"), 1)
                    hidden_low(C - 1)
                    gathered_low(it + 1)
                    dve.wait_ge(moe_sem(k, "read"), it * N + (N + SPLITS))
                    V.tensor_copy(Y[:, 512:1024], ps[:, 3, :]).then_inc(moe_sem(k, "outputs_by_vector"), 1)
                    for j in range(4):
                        dve.wait_ge(moe_sem(k, "scattered"), it * 4 + (j + 1))
                        d = dst[:, j // 2, j % 2 * 512:(j % 2 + 1) * 512]
                        V.tensor_tensor(d, d, ps[:, 5 + j % 2, :], ADD).then_inc(moe_sem(k, "added"), 1)
                    picks_ready(it + 1)
                    dve.wait_ge(moe_sem(k, "added"), it * 4 + 4)

            rms(H, XS, EPS)
            columns(XT, ("od_norm_moe", 0))
            dve.wait_ge(S("const_loaded"), 16)
            step(V.tensor_scalar(IOM, c_("iota")[:, 0:16], -99.0, None, ADD))
            dve.wait_ge(S("logits_ready"), 1)
            e8 = lambda t: t[:, :, 0:8]
            step(V.tensor_copy(e8(LG), ps[:, 4, 0:32].rearrange("p (a e) -> p a e", e=16)[:, :, 0:8]))
            first_best(e8(LG), 2, 8, V0[:, 0:2], e8(O0), e8(TA))
            remove(e8(LG), e8(O0))
            first_best(e8(LG), 2, 8, V1[:, 0:2], e8(O1), e8(TA))
            V.tensor_tensor(PAIRW[:, 0, :], V1[:, 0:2], V0[:, 0:2], SUB).then_inc(S("logit_gap"), 1)
            step(V.tensor_tensor(SEL, e8(O0), e8(O1), ADD))
            dve.sem_inc(S("chosen"), 1)
            dve.wait_ge(S("gap_exp"), 1)
            step(V.tensor_scalar(PAIRW[:, 2, :], PAIRW[:, 1, :], 1.0, None, ADD))
            step(V.reciprocal(PAIRW[:, 2, :], PAIRW[:, 2, :]))
            r3 = lambda t, n: t.rearrange("p (a n) -> p a n", n=1).broadcast_to([P, 2, n])
            step(V.scalar_tensor_tensor(e8(CB), e8(O1), 1.0, r3(PAIRW[:, 1, :], 8), MUL, MUL))
            step(V.tensor_tensor(e8(CB), e8(CB), e8(O0), ADD))
            step(V.tensor_tensor(e8(CB), e8(CB), r3(PAIRW[:, 2, :], 8), MUL))
            ranks(1)
            experts(1, H, "od_norm_moe")
            dve.sem_inc(S("moe_done"), 1)
            n_["sq"] += 1
            dve.wait_ge(S("squares_summed"), n_["sq"])
            V.tensor_scalar(var, ssq, 1.0 / D, EPS, MUL, ADD).then_inc(S("variance_ready"), 1)
            rsqrt()
            g = row(1)
            for tc in range(2):
                last = V.scalar_tensor_tensor(H[:, tc, :], H[:, tc, :], rstd[:, tc:tc + 1], g, MUL, MUL)
            use_row(1, last)
            layer_norm("h_ready")
            columns(XT, None)
            take_columns("fqk", w_(0, 4, T))
            dve.wait_ge(S("small_loaded"), 16 * 10)
            step(V.tensor_tensor(lam4[:, 0::2, :], lam4[:, 0::2, :], lam4[:, 1::2, :], MUL))
            V.tensor_reduce(lamp, lam4[:, 0::2, :], X, ADD).then_inc(S("lam_sums"), 1)
            dve.wait_ge(S("lam_exp"), 1)
            step(V.tensor_tensor(nlam, lame[:, 1:2], lame[:, 0:1], SUB))
            step(V.tensor_scalar(nlam, nlam, -LAM_INIT, None, ADD))
            u = UNIT["fv"]
            unit_ready(dve, u)
            V.tensor_tensor(ffl, PAIRS[u % 2][:, :, 256:260], foxb.rearrange("p (a n) -> p a n", a=1).broadcast_to([P, 2, 4]), ADD)
            V.tensor_copy(w_(7168, 2, 256), PAIRS[u % 2][:, :, 0:256]).then_inc(S(f"unit_read{u % 2}"), 1)
            dve.wait_ge(S(f"unit_read{u % 2}"), u // 2 + 1)
            V.tensor_scalar(logf_fox, ffl, 0.0, None, ALU.min).then_inc(S("fox_logits"), 1)
            dve.wait_ge(S("fox_log1p"), 1)
            dve.wait_ge(S("fox_logits"), 1)
            V.tensor_tensor(logf_fox, logf_fox, ffa, SUB).then_inc(S("fox_log"), 1)
            u = UNIT["dv"]
            unit_ready(dve, u)
            V.tensor_copy(w_(7680, 2, 256), PAIRS[u % 2][:, :, 0:256]).then_inc(S(f"unit_read{u % 2}"), 1)
            HFZ, HFA = w_(9216, 2, 512), w_(4096, 2, 512)
            take("hf", HFZ)
            u = UNIT["hf"]
            dve.wait_ge(S(f"unit_read{u % 2}"), u // 2 + 1)
            dve.sem_inc(S("forget_logits"), 1)
            dve.wait_ge(S("forget_log1p"), 1)
            step(V.scalar_tensor_tensor(HFA, HFZ, 0.0, HFA, ALU.min, SUB))
            DB = XT[:, :, :].rearrange("p (a h) t -> p a h t", a=2)
            dve.wait_ge(S("fox_sums"), 2)
            cs = ffa
            step(V.tensor_copy(cs, ps[:, 4, 0:8].rearrange("p (a e) -> p a e", e=4)))
            masks = row(0).rearrange("p (k a t) -> p k a t", k=2, a=2)
            u = UNIT["hg"]
            for w in (u - 1, u):
                unit_ready(dve, w)
            for tc in range(2):
                for place, h in enumerate(HEAD_ORDER):
                    last = V.scalar_tensor_tensor(DB[:, tc, place, :], ps[:, 6 + h // 2, h % 2 * T:h % 2 * T + T], -1.0,
                                                  masks[:, 0, tc, :], MUL, ADD)
            step(last)
            for tc in range(2):
                for place, h in enumerate(HEAD_ORDER):
                    last = V.tensor_scalar(DB[:, tc, place, :], DB[:, tc, place, :], cs[:, tc, h:h + 1], None, ADD)
            step(last)
            dve.sem_inc(S("fox_bias"), 1)
            PR, PR2, PT = w_(8192, 2, 4, T), w_(10240, 2, 4, T), w_(10240, KC, T)

            def masked_scores(n, scale, bias, dst):
                dve.wait_ge(S("scores_ready"), n)
                for tc in range(2):
                    last = V.scalar_tensor_tensor(dst[:, tc, :, :], ps[:, 4 + 2 * tc:6 + 2 * tc, :].rearrange("p a (b t) -> p (a b) t", t=T),
                                                  scale, bias(tc), MUL, ADD)
                step(last)

            dve.wait_ge(S("keys_turned"), 1)
            masked_scores(3, 0.125, lambda tc: DB[:, tc, :, :], PR)
            dve.sem_inc(S("fox_scored"), 1)
            scores_max(3, PR.rearrange("p a h t -> p (a h) t"), 1.0, 3)
            normalise(3, PR).then_inc(S("probs_ready"), 1)
            probs_columns(3, PT)
            dve.wait_ge(S("small_attended"), 1)
            V.tensor_copy(XS[:, :, 0:256], ps[:, 4, :].rearrange("p (a n) -> p a n", a=2)).then_inc(S("small_read"), 1)
            for which in range(2):
                dst = (PR, PR2)[which]
                masked_scores(4 + which, 32.0 ** -0.5,
                              lambda tc: masks[:, 1, tc:tc + 1, :].broadcast_to([P, 4, T]), dst)
                if which == 0:
                    dve.sem_inc(S("diff_map"), 1)
                scores_max(4 + which, dst.rearrange("p a h t -> p (a h) t"), 1.0, 0)
                step(normalise(4 + which, dst))
            use_row(0, V.scalar_tensor_tensor(PR.rearrange("p a h t -> p (a h t)"), PR2.rearrange("p a h t -> p (a h t)"), nlam[:, 0:1],
                                              PR.rearrange("p a h t -> p (a h t)"), MUL, ADD))
            dve.sem_inc(S("probs_ready"), 1)
            probs_columns(4, PT)
            dve.wait_ge(S("small_attended"), 2)
            OD = XS[:, :, 256:512]
            V.tensor_copy(OD, ps[:, 4, :].rearrange("p (a n) -> p a n", a=2)).then_inc(S("small_read"), 1)
            dve.wait_ge(S("small_read"), 2)

            def head_norm(src, scratch, n, d, gain, extra):
                step(V.tensor_tensor(scratch, src, src, MUL))
                step(V.tensor_reduce(dss, scratch, X, ADD))
                V.tensor_scalar(dss, dss, 1.0 / d, LN_EPS, MUL, ADD).then_inc(S("variance_ready"), 1)
                rsqrt(drs, dstd)
                for tc in range(2):
                    last = V.scalar_tensor_tensor(src[:, tc], src[:, tc], extra,
                                                  drs[:, tc, :].rearrange("p (h n) -> p h n", n=1).broadcast_to([P, 4, d]), MUL, MUL)
                step(last)
                for tc in range(2):
                    last = V.tensor_tensor(src[:, tc], src[:, tc], gain.rearrange("p (a n) -> p a n", a=1).broadcast_to([P, 4, d]), MUL)
                step(last)

            h4 = lambda t: t.rearrange("p a (h d) -> p a h d", h=4)
            head_norm(h4(OD), h4(w_(8192, 2, 256)), 4, 64, dgain, 1.0 - LAM_INIT)
            dve.sem_inc(S("diff_done"), 1)
            E, QE, KE, ST = w_(8192, 4, T), w_(9216, 4, T), w_(10240, 4, T), w_(11264, 8, P)
            QH, KH = w_(2048, 4, T), w_(3072, 4, T)
            step(V.memset(ST, 0.0))
            dve.wait_ge(S("keys_columns"), 1)
            dve.wait_ge(S("levels_loaded"), 16)
            CR = w_(8192, 4, P)
            scores = ps[:, 0:2, :].rearrange("p a (b t) -> p (a b) t", t=P)
            for lv in range(9):
                dve.wait_ge(S("level_scores"), lv + 1)
                if lv < 8:
                    mask = (IDENT if lv == 0 else c_(f"pair{lv - 1}")).bitcast(I32)
                    V.copy_predicated(ST, mask.rearrange("p (a t) -> p a t", a=1).broadcast_to([P, 8, P]), scores)\
                        .then_inc(S("level_merged"), 1)
                    dve.wait_ge(S("level_merged"), lv + 1)
                    dve.wait_ge(S("level_exp"), lv + 1)
                    V.tensor_tensor(QE, QH, E, MUL)
                    V.tensor_tensor(KE, KH, E, MUL).then_inc(S("level_decayed"), 1)
                    dve.wait_ge(S("level_decayed"), lv + 1)
                else:
                    V.tensor_copy(CR, ps[:, 0, :].rearrange("p (h t) -> p h t", t=P)).then_inc(S("level_merged"), 1)
            dve.wait_ge(S("recurrence_out"), 1)
            OH = XS[:, :, 512:1024]
            step(V.tensor_copy(OH, ps[:, 2:4, :]))
            head_norm(h4(OH), h4(w_(9216, 2, 512)), 4, 128, hgain, 1.0)
            V.tensor_tensor(OH, OH, w_(6144, 2, 512), MUL).then_inc(S("xs_ready"), 1)
            dve.wait_ge(S("xs_ready"), 9)
            columns(XT, None)
            for j in range(2):
                add_unit(f"out{j}", j, ALPHA)
            update_done("out1")
            columns(XT, None)
            layer_norm("h_ready")
            attention("C", 6, None)
            layer_norm("h_ready")
            V.tensor_scalar(XS[:, :, :], H[:, :, :], ALPHA, None, MUL)
            columns(XT, None)
            dve.wait_ge(S("router_scores"), 1)
            step(V.tensor_tensor(BI, LG, rbias.rearrange("p (a n) -> p a n", a=1).broadcast_to([P, 2, 16]), ADD))
            g4 = lambda t: t.rearrange("p a (g m) -> p (a g) m", m=4)
            WK = TA
            first_best(g4(BI), 8, 4, V0, g4(O0), g4(TA))
            step(V.tensor_copy(O1, BI))
            remove(O1, O0)
            step(V.tensor_reduce(V1, g4(O1), X, ALU.max))
            step(V.tensor_tensor(V0, V0, V1, ADD))
            gs = V0.rearrange("p (a g) -> p a g", g=4)
            first_best(gs, 2, 4, V1[:, 0:2], SEL[:, :, 0:4], TA[:, :, 0:4])
            dve.sem_inc(S("chosen"), 1)
            step(V.tensor_scalar(O1[:, :, 0:4], SEL[:, :, 0:4], -1.0, REMOVED, ADD, MUL))
            step(V.tensor_copy(V0.rearrange("p (a g) -> p a g", g=4), O1[:, :, 0:4]))
            step(V.tensor_tensor(g4(BI), g4(BI), V0.rearrange("p (a n) -> p a n", n=1).broadcast_to([P, 8, 4]), ADD))
            first_best(BI, 2, 16, V1[:, 0:2], O0, TA)
            remove(BI, O0)
            first_best(BI, 2, 16, V1[:, 0:2], O1, TA)
            step(V.tensor_tensor(O0, O0, O1, ADD))
            step(V.tensor_tensor(O0, O0, LG, MUL))
            step(V.tensor_reduce(V1[:, 0:2], O0, X, ADD))
            step(V.reciprocal(V1[:, 0:2], V1[:, 0:2]))
            step(V.tensor_tensor(CB[:, :, 0:16], O0, r3(V1[:, 0:2], 16), MUL))
            ranks(2)
            experts(2, XS, None)
            step(V.tensor_copy(H[:, :, :], XS[:, :, :]))
            layer_norm("h_ready")
            dve.sem_inc(S("h_final"), 1)


_NAMES = ("x mem ev_norm_mix ev_w_in ev_conv_a ev_pool_w ev_pool_scale ev_w_out ev_norm_ffn ev_ffn_gu ev_ffn_down "
          "od_norm_mix od_pw1_w od_pw1_b od_dw_w od_dw_b od_ln_g od_ln_b od_pw2_w od_pw2_b od_norm_moe od_router "
          "od_moe_gu od_moe_down xa_norm xa_norm_mem xa_wq xa_wkv xa_wo final_norm mem_2 ln_in_g_2 ln_in_b_2 w_in_2 "
          "fox_fb_2 lam_q1_2 lam_k1_2 lam_q2_2 lam_k2_2 diff_norm_g_2 hgrn_norm_g_2 w_out_2 mem_wq_2 mem_wk_2 "
          "mem_wv_2 mem_wo_2 router_w_2 router_b_2 w1_2 w3_2 w2_2 ln_g_2 ln_b_2").split()


def kernel(**inputs):
    import concourse.bacc as bacc
    from concourse.bass_utils import run_bass_kernel_spmd

    nc = bacc.Bacc("TRN2", target_bir_lowering=False, num_devices=1)
    arrays, ins = {}, {}
    for name in _NAMES:
        a = np.ascontiguousarray(inputs[name])
        arrays["in_" + name] = a
        ins[name] = nc.dram_tensor("in_" + name, a.shape, F32, kind="ExternalInput").ap()
    arrays["constants"] = CONSTANTS
    const_in = nc.dram_tensor("constants", CONSTANTS.shape, F32, kind="ExternalInput").ap()
    out = nc.dram_tensor("out", (1, T, D), F32, kind="ExternalOutput").ap()
    program(nc, ins, const_in, out)
    r = run_bass_kernel_spmd(nc, [arrays], core_ids=[0])
    return r.results[0]["out"]
```

```python
from contextlib import ExitStack

import numpy as np

import concourse.bass as bass
from concourse import mybir

F32 = mybir.dt.float32
F32R = mybir.dt.float32r
I32 = mybir.dt.int32
ALU = mybir.AluOpType
ACT = mybir.ActivationFunctionType
X = mybir.AxisListType.X

P = 128
T = 256
HALVES = T // P
D = 1024
KC = D // P
PANEL = 512
HALF = KC * PANEL // 2
SLOTS = 3
SPLITS = 3
D_FF = 2816
EPS, LN_EPS = 1e-6, 1e-5
ALPHA = 2.0 ** 0.25
LAM_INIT = 0.2
WINDOWS = (2, 4, 8, 16)
CONV = 31
TAPS_ON_PE = 2
DIAGONALS = 6
MASKED = -1e30
REMOVED = 3e38
HEAD_ORDER = (0, 2, 1, 3)

CONST_COLS = {}


def constant_table():
    r = np.arange(P)
    parts = []

    def put(name, a):
        CONST_COLS[name] = (sum(p.shape[1] for p in parts), a.shape[1])
        parts.append(np.asarray(a, np.float32))

    put("ident", np.eye(P))
    put("ones", np.ones((P, P)))
    put("upto", r[:, None] <= r[None, :])
    put("before", r[:, None] < r[None, :])
    put("iota", np.broadcast_to(r[None, :], (P, P)))
    resident = sum(p.shape[1] for p in parts)
    for lv in range(7):
        m = 1 << lv
        start = r // (2 * m) * (2 * m)
        border = start + m - 1
        late = r % (2 * m) >= m
        span = np.where(late[None, :], (r[:, None] > border[None, :]) & (r[:, None] <= r[None, :]),
                        (r[:, None] > r[None, :]) & (r[:, None] <= border[None, :]))
        put(f"span{lv}", span)
    put("after", r[:, None] > r[None, :])
    for lv in range(7):
        m = 1 << lv
        put(f"pair{lv}", (r[:, None] // (2 * m) == r[None, :] // (2 * m))
            & (r[:, None] % (2 * m) < m) & (r[None, :] % (2 * m) >= m))
    q, k = np.arange(T), np.arange(T)
    for name, ok in (("causal", k[None, :] <= q[:, None]), ("chunked", k[None, :] // 64 <= q[:, None] // 64)):
        a = np.where(ok, 0.0, MASKED).reshape(HALVES, P, T).transpose(1, 0, 2).reshape(P, HALVES * T)
        put(name, a)
    inv = []
    for w in WINDOWS:
        lo = np.maximum(q - w // 2, 0)
        hi = np.minimum(q + w - 1 - w // 2, T - 1) + 1
        inv.append(1.0 / (hi - lo).astype(np.float32))
    put("window", np.broadcast_to(np.concatenate(inv)[None], (P, len(WINDOWS) * T)))
    return np.concatenate(parts, 1), resident


CONSTANTS, RESIDENT = constant_table()

VECTORS = [("ev_norm_mix", 8), ("ev_conv_a", 12), ("ev_pool_scale", 4), ("ev_norm_ffn", 8), ("od_norm_mix", 8),
           ("od_pw1_b", 16), ("od_dw_b", 8), ("od_ln_g", 8), ("od_ln_b", 8), ("od_norm_moe", 8),
           ("xa_norm", 16), ("xa_norm_mem", 16), ("od_dw_w", 248)]
VEC_AT = {}
for _name, _rows in VECTORS:
    VEC_AT[_name] = sum(r for _, r in VECTORS[:len(VEC_AT)])
VEC_TILES = -(-sum(r for _, r in VECTORS) // P)
VEC_ROWS = sum(r for _, r in VECTORS)
VEC_LOADS = sum((VEC_AT[n] + r - 1) // P - VEC_AT[n] // P + 1 for n, r in VECTORS)

UNITS = []
UNIT = {}


def _unit(name, weight, c0, n, columns, src, layer=0):
    UNIT[name] = len(UNITS)
    UNITS.append((weight, layer, c0, n, columns, src))


def _memory_units(tag, layer, wk, wv, v0):
    for j in range(2):
        _unit(f"{tag}k{j}", wk, j * PANEL, PANEL, True, "memory", layer)
    for j in range(2):
        _unit(f"{tag}v{j}", wv, v0 + j * PANEL, PANEL, False, "memory", layer)


def _query_units(tag, layer, wq, wo):
    for j in range(2):
        _unit(f"{tag}q{j}", wq, j * PANEL, PANEL, True, "x", layer)
    for j in range(2):
        _unit(f"{tag}o{j}", wo, j * PANEL, PANEL, False, "attended", layer)


for _j, _n in enumerate(("h", "gb", "gc", "u")):
    _unit("in_" + _n, "ev_w_in", _j * PANEL, PANEL, True, "x")
_memory_units("A", 0, "xa_wkv", "xa_wkv", D)
for _j in range(2):
    _unit(f"mix{_j}", "ev_w_out", _j * PANEL, PANEL, False, "mixed")
_query_units("A", 0, "xa_wq", "xa_wo")
FFN_AT = len(UNITS)
for _j in range(2):
    _unit(f"gate{_j}", "od_pw1_w", D + _j * PANEL, PANEL, True, "x")
    _unit(f"value{_j}", "od_pw1_w", _j * PANEL, PANEL, True, "x")
_memory_units("B", 1, "xa_wkv", "xa_wkv", D)
for _j in range(2):
    _unit(f"pw2_{_j}", "od_pw2_w", _j * PANEL, PANEL, False, "conformed")
_query_units("B", 1, "xa_wq", "xa_wo")
MOE1_AT = len(UNITS)
_unit("fqk", "w_in_2", 0, 512, True, "x")
_unit("dqk", "w_in_2", 772, 512, True, "x")
_unit("hq", "w_in_2", 1540, 512, True, "x")
_unit("fv", "w_in_2", 512, 260, False, "x")
_unit("dv", "w_in_2", 1284, 256, False, "x")
_unit("hf", "w_in_2", 2052, 512, False, "x")
_unit("hi", "w_in_2", 2564, 512, False, "x")
_unit("hg", "w_in_2", 3076, 512, False, "x")
for _j in range(2):
    _unit(f"out{_j}", "w_out_2", _j * PANEL, PANEL, False, "x")
_memory_units("C", 0, "mem_wk_2", "mem_wv_2", 0)
_query_units("C", 0, "mem_wq_2", "mem_wo_2")
FFN_TURNS = D_FF // T

MOES = {
    1: dict(groups=8, members=1, chunks=7, slots=7, experts=8),
    2: dict(groups=4, members=4, chunks=1, slots=6, experts=16),
}


def stream(c):
    n = c["members"] * c["chunks"]
    order = [("gate", 0), ("up", 0)]
    for k in range(1, n):
        order += [("gate", k), ("up", k), ("down", k - 1)]
    order.append(("down", n - 1))
    return [(kind, k, half) for kind, k in order for half in range(2)]


def chunk_at(k):
    return 0 if k == 0 else 4 + 6 * (k - 1)


def ffn_half(kind, f):
    if kind == "gu":
        return 3 * f - 1 if f else 0
    return min(3 * f + 4, 3 * FFN_TURNS - 1)


def program(nc, ins, const_in, out):
    ctx = ExitStack()
    with ctx:
        def sb(name, shape, dt=F32):
            return ctx.enter_context(nc.sbuf_tensor(name, shape, dt))

        sems = {}

        def S(name):
            if name not in sems:
                sems[name] = ctx.enter_context(nc.semaphore(name))
            return sems[name]

        ring = sb("ring", [P, 7, HALF])
        w_high = sb("w_high", [P, SPLITS, HALF], F32R)
        w_low = sb("w_low", [P, SPLITS, HALF], F32R)
        parts = sb("parts", [P, 3 * KC * P], F32R)
        x_high, x_low = (parts[:, i * D:(i + 1) * D].rearrange("p (k t) -> p k t", t=P) for i in range(2))
        h_high, h_low = (parts[:, 2 * D + i * 512:2 * D + (i + 1) * 512].rearrange("p (k t) -> p k t", t=P) for i in range(2))
        const = sb("const", [P, RESIDENT])
        H = sb("H", [P, HALVES, D])
        XS = sb("XS", [P, HALVES, D])
        XT = ring[:, 6, :].rearrange("p (k t) -> p k t", t=T)
        XT_high = sb("XT_high", [P, KC, T], F32R)
        XT_low = parts[:, 0:KC * T].rearrange("p (k t) -> p k t", t=T)
        work = sb("work", [P, 12 * 1024])
        brow = sb("brow", [P, 2, D])
        cols = sb("cols", [P, VEC_TILES * P])
        small = sb("small", [P, 512])
        count = sb("count", [P, 2], I32)
        ps = ctx.enter_context(nc.psum_tensor("ps", [P, 8, 512], F32))

        def c_(name):
            a, n = CONST_COLS[name]
            if a >= RESIDENT:
                return ring[:, 6, a - RESIDENT:a - RESIDENT + n]
            return const[:, a:a + n]

        def w_(off, *shape):
            n = int(np.prod(shape))
            v = work[:, off:off + n]
            if len(shape) == 2:
                return v.rearrange("p (a b) -> p a b", b=shape[1])
            if len(shape) == 3:
                return v.rearrange("p (a b c) -> p a b c", b=shape[1], c=shape[2])
            return v

        small_top = [0]

        def sm(*shape):
            n = int(np.prod(shape))
            v = small[:, small_top[0]:small_top[0] + n]
            small_top[0] += n
            assert small_top[0] <= 512
            if len(shape) == 2:
                return v.rearrange("p (a b) -> p a b", b=shape[1])
            return v

        def vec(name, r=0):
            a = VEC_AT[name] + r
            return cols[:, a:a + 1]

        IDENT, ONES = c_("ident"), c_("ones")
        prob = {n: w_(8192 if n in (3, 4) else 0, 2, 4, T) for n in range(1, 6)}
        ssq, var, std, rstd = sm(2), sm(2), sm(2), sm(2)
        mean = sm(2)
        mx, nbias, den, rden = sm(8), sm(8), sm(8), sm(8)
        lam4 = sm(4, 32)
        lamp, lame, nlam = sm(2), sm(2), sm(1)
        dgain = sm(64)
        foxb = sm(4)
        ffl, ffa, logf_fox = sm(2, 4), sm(2, 4), sm(2, 4)
        dss, dstd, drs = sm(2, 4), sm(2, 4), sm(2, 4)
        rbias = sm(16)
        hgain = c_("ident")
        big_small = sb("big_small", [P, 640])
        gates = sb("gates", [P, 120])
        hgain = big_small[:, 0:128]
        router = big_small[:, 128:256].rearrange("p (k e) -> p k e", e=16)
        LG = big_small[:, 256:288].rearrange("p (a e) -> p a e", e=16)
        BI = big_small[:, 288:320].rearrange("p (a e) -> p a e", e=16)
        TA = big_small[:, 320:352].rearrange("p (a e) -> p a e", e=16)
        O0 = big_small[:, 352:384].rearrange("p (a e) -> p a e", e=16)
        O1 = big_small[:, 384:416].rearrange("p (a e) -> p a e", e=16)
        CB = gates[:, 0:72].rearrange("p (a e) -> p a e", e=36)
        RK = gates[:, 72:106].rearrange("p (a e) -> p a e", e=17)
        CBS = gates[:, 106:114].rearrange("p (a e) -> p a e", e=4)
        GS = gates[:, 114:118]
        SEL = big_small[:, 512:528].rearrange("p (a e) -> p a e", e=8)
        V0, V1 = big_small[:, 528:536], big_small[:, 536:544]
        VI = big_small[:, 544:552]
        IOM = big_small[:, 552:568]
        PAIRW = big_small[:, 568:574].rearrange("p (k a) -> p k a", a=2)
        CMAX = big_small[:, 574:575]
        TOT = big_small[:, 576:584]
        router1 = sb("router1", [P, KC, 8])
        poolw = brow[:, 0, 0:512].rearrange("p (g n) -> p g n", n=P)

        sources = {"x": XT, "memory": XT, "mixed": w_(10240, KC, T), "attended": XT, "conformed": w_(2304, KC, T)}
        FH, FL = (parts[:, 2 * D + i * 512:2 * D + (i + 1) * 512].rearrange("p (k t) -> p k t", t=T) for i in range(2))
        PAIRS = [ps[:, 0:2, :], ps[:, 2:4, :]]

        def k_major(w, layer, c0, n):
            return w[layer, :, c0:c0 + n].rearrange("(k p) n -> p k n", p=P)

        pieces_split, split_at, plain_count = [], {}, [0, 0]
        panels = []
        unit_panel = {}
        for u in range(len(UNITS) + 1):
            if u == FFN_AT:
                gu, dn = ins["ev_ffn_gu"], ins["ev_ffn_down"]
                ffn_at = len(pieces_split)
                for f in range(FFN_TURNS):
                    panels.append(([((0, 256), k_major(gu, 0, f * T, T)), ((256, 256), k_major(gu, 0, D_FF + f * T, T))],
                                   "parts_split", ffn_at + ffn_half("gu", f) + 2))
                    pieces_split += [(len(panels) - 1, "columns", 0, PANEL), (len(panels) - 1, "columns", 1, PANEL)]
                    if f:
                        pieces_split.append((len(panels) - 2, "rows", 0, D))
                    panels.append(([("rows", dn[0, f * T:(f + 1) * T, :].rearrange("(k p) n -> p k n", p=P))],
                                   "parts_split", ffn_at + ffn_half("down", f) + 1))
                pieces_split.append((len(panels) - 1, "rows", 0, D))
            if u == MOE1_AT:
                moe1_panel = len(panels)
            if u == len(UNITS):
                break
            weight, layer, c0, n, columns, src = UNITS[u]
            unit_panel[u] = len(panels)
            if src in ("x", "attended"):
                split_at[u] = len(pieces_split)
                pieces_split += [(len(panels), "columns" if columns else "features", half, n) for half in range(2)]
                release = ("parts_split", split_at[u] + 2)
            else:
                plain_count[u % 2] += 1
                release = (f"unit_ready{u % 2}", plain_count[u % 2])
            panels.append(([((0, n), k_major(ins[weight], layer, c0, n))],) + release)

        def slot(i):
            return (i - moe1_panel) % SLOTS if i >= moe1_panel else i % SLOTS

        landed, landed_count = [], {}
        for i, (pieces, _, _) in enumerate(panels):
            landed_count[slot(i)] = landed_count.get(slot(i), 0) + 16 * len(pieces)
            landed.append((slot(i), landed_count[slot(i)]))

        def slot_kn(i):
            return ring[:, 2 * i:2 * i + 2, :].rearrange("p a (k n) -> p (a k) n", n=PANEL)

        def slot_rows(i):
            return ring[:, 2 * i:2 * i + 2, :].rearrange("p a (k n) -> p (a k) n", n=D)

        def half_source(q):
            i, kind, half, n = pieces_split[q]
            if kind == "rows":
                return ring[:, 2 * slot(i), :]
            if kind == "features":
                return slot_kn(slot(i))[:, 4 * half:4 * half + 4, 0:n]
            if q in range(ffn_at, ffn_at + 3 * FFN_TURNS):
                return slot_kn(slot(i)).rearrange("p k (g n) -> p k g n", g=2)[:, :, :, half * P:(half + 1) * P]
            return slot_kn(slot(i))[:, :, half * T:(half + 1) * T]

        def half_tile(q, parts):
            t, (_, kind, _, n) = parts[:, q % SPLITS, :], pieces_split[q]
            if kind == "rows":
                return t
            if kind == "features":
                return t.rearrange("p (k n) -> p k n", n=PANEL)[:, :, 0:n]
            if q in range(ffn_at, ffn_at + 3 * FFN_TURNS):
                return t.rearrange("p (k g n) -> p k g n", g=2, n=P)
            return t.rearrange("p (k n) -> p k n", n=T)

        def halves_to(name, more=0):
            return split_at[UNIT[name]] + 2 + more

        def wait_panel(eng, i):
            s, v = landed[i]
            eng.wait_ge(S(f"landed{s}"), v)

        def unit_ready(eng, u):
            if u in split_at:
                eng.wait_ge(S("parts_read"), split_at[u] + 2)
            else:
                _, sem, value = panels[unit_panel[u]]
                eng.wait_ge(S(sem), value)

        class Steps:

            def __init__(self, eng, sem, base=0):
                self.eng, self.sem, self.base, self.n = eng, sem, base, 0

            def __call__(self, ins):
                self.n += 1
                ins.then_inc(self.sem, 1)
                self.eng.wait_ge(self.sem, self.base + self.n)

        def level_tiles(lv):
            return [w_(o, 4, T) for o in ((8192, 9216, 10240), (0, 1024, 7168))[lv % 2]]

        block = ctx.enter_context(nc.Block())

        def moe_sem(k, name):
            return S(f"moe{k}_{name}")

        @block.sync
        def _(sync):
            def load(i, wait):
                pieces, sem, value = panels[i]
                if wait:
                    sync.wait_ge(S(panels[i - SLOTS][1]), panels[i - SLOTS][2])
                for where, src in pieces:
                    n = src.shape[2]
                    if where == "rows":
                        dst = slot_rows(slot(i))[:, 0:src.shape[1], :]
                    else:
                        dst = slot_kn(slot(i))[:, :, where[0]:where[0] + n]
                    sync.dma_start(dst, src).then_inc(S(f"landed{slot(i)}"), 16)

            def experts(k, source):
                c = MOES[k]
                slots, halves = c["slots"], stream(c)
                sync.sem_inc(moe_sem(k, "split"), slots)

                def group(g, turn):
                    for j, (kind, chunk, half) in enumerate(halves):
                        sync.wait_ge(moe_sem(k, "split"), turn * len(halves) + (j + 1))
                        src = source(kind, g, chunk, half)
                        dst = ring[:, j % slots, :].rearrange("p (k n) -> p k n", n=src.shape[2])
                        sync.dma_start(dst, src).then_inc(moe_sem(k, f"landed{j % slots}"), 16)

                with sync.Fori(0, c["groups"]) as g:
                    group(g, g)
                sync.wait_ge(moe_sem(k, "turns_ready"), 1)
                turns = sync.value_load(count[0:1, k - 1:k], min_val=c["groups"], max_val=2 * c["groups"])
                with sync.If(turns > c["groups"]):
                    with sync.Fori(0, c["groups"]) as g:
                        group(g, g + c["groups"])
                with sync.Else():
                    sync.nop()
                if k == 1:
                    sync.wait_ge(moe_sem(k, "split"), turns * len(halves) + slots)

            last = {0: 0, 1: 10, 2: 14, 3: 36, 4: 46}
            n_dense = moe1_panel
            for i in range(n_dense):
                load(i, i >= SLOTS)
            for i in range(moe1_panel - SLOTS, moe1_panel):
                sync.wait_ge(S(panels[i][1]), panels[i][2])
            gu1, dn1 = ins["od_moe_gu"], ins["od_moe_down"]

            def first_mixture(kind, g, chunk, half):
                if kind == "down":
                    r = chunk * PANEL + half * 256
                    return dn1[0, bass.ds(g, 1), r:r + 256, :].rearrange("a (k p) n -> p (a k) n", p=P)
                c0 = chunk * PANEL + (7 * PANEL if kind == "up" else 0)
                return gu1[0, bass.ds(g, 1), half * 512:(half + 1) * 512, c0:c0 + PANEL]\
                    .rearrange("a (k p) n -> p (a k) n", p=P)

            experts(1, first_mixture)
            for i in range(moe1_panel, len(panels)):
                load(i, i - SLOTS >= moe1_panel)
            for i in range(len(panels) - SLOTS, len(panels)):
                sync.wait_ge(S(panels[i][1]), panels[i][2])

            second = {"gate": ins["w1_2"], "up": ins["w3_2"], "down": ins["w2_2"]}

            def second_mixture(kind, g, member, half):
                rows = 256 if kind == "down" else 512
                v = second[kind][0].rearrange("(g m) a b -> g m a b", m=4)
                return v[bass.ds(g, 1), member, half * rows:(half + 1) * rows, :].rearrange("a (k p) n -> p (a k) n", p=P)

            experts(2, second_mixture)

        @block.gpsimd
        def _(pool):
            pool.dma_start(H[:, :, :], ins["x"][0].rearrange("(a p) d -> p a d", p=P)).then_inc(S("x_loaded"), 16)
            vrows = w_(0, VEC_TILES, P)
            for name, rows in VECTORS:
                v = ins[name]
                flat = v.rearrange("a (r q) -> (a r) q", q=P) if len(v.shape) == 2 else \
                    v.rearrange("a k (r q) -> (a k r) q", q=P)
                at, done = VEC_AT[name], 0
                while done < rows:
                    t, r = divmod(at + done, P)
                    n = min(rows - done, P - r)
                    pool.dma_start(vrows[r:r + n, t, :], flat[done:done + n, :]).then_inc(S("vectors_loaded"), 16)
                    done += n
            pool.dma_start(const[:, :], const_in[:, 0:RESIDENT]).then_inc(S("const_loaded"), 16)
            a, n = CONST_COLS["window"]
            pool.dma_start(w_(4736, 4 * T), const_in[:, a:a + n]).then_inc(S("window_loaded"), 16)
            pool.dma_start(poolw, ins["ev_pool_w"][0].rearrange("g c d -> c g d")).then_inc(S("poolw_loaded"), 16)
            pool.dma_start(router1[:, :, :], ins["od_router"][0].rearrange("(k p) e -> p k e", p=P)).then_inc(S("small_loaded"), 16)
            pool.dma_start(router, ins["router_w_2"].rearrange("(k p) e -> p k e", p=P)).then_inc(S("small_loaded"), 16)
            for dst, src in ((rbias, ins["router_b_2"]), (foxb, ins["fox_fb_2"][0]), (dgain, ins["diff_norm_g_2"][0]),
                             (hgain, ins["hgrn_norm_g_2"][0]), (lam4[:, 0, :], ins["lam_q1_2"][0]),
                             (lam4[:, 1, :], ins["lam_k1_2"][0]), (lam4[:, 2, :], ins["lam_q2_2"][0]),
                             (lam4[:, 3, :], ins["lam_k2_2"][0])):
                pool.dma_start(dst, src.partition_broadcast(P)).then_inc(S("small_loaded"), 16)

            def memory(turns, name):
                pool.wait_ge(S("turned"), 4 * turns)
                pool.dma_start(XS[:, :, :], ins[name][0].rearrange("(a p) d -> p a d", p=P)).then_inc(S("memory_loaded"), 16)

            loads = {0: 0, 1: 0}

            def row(b, src):
                if loads[b]:
                    pool.wait_ge(S(f"brow{b}_used"), loads[b])
                loads[b] += 1
                pool.dma_start(brow[:, b, :], src).then_inc(S(f"brow{b}_loaded"), 16)

            row(1, ins["final_norm"].partition_broadcast(P))
            memory(1, "mem")
            pool.wait_ge(S("pool_mixed"), 1)
            row(0, ins["od_pw2_b"][0].partition_broadcast(P))
            memory(5, "mem")
            row(0, ins["ln_in_g_2"].partition_broadcast(P))
            row(1, ins["ln_in_b_2"].partition_broadcast(P))
            a = CONST_COLS["causal"][0]
            row(0, const_in[:, a:a + D])
            pool.wait_ge(S("fox_scored"), 1)
            pool.dma_start(ring[:, 6, 0:a - RESIDENT], const_in[:, RESIDENT:a])\
                .then_inc(S("levels_loaded"), 16)
            row(1, ins["ln_g_2"][0, 0].partition_broadcast(P))
            row(0, ins["ln_b_2"][0, 0].partition_broadcast(P))
            memory(10, "mem_2")
            for j in (1, 2):
                row(1, ins["ln_g_2"][0, j].partition_broadcast(P))
                row(0, ins["ln_b_2"][0, j].partition_broadcast(P))
            pool.wait_ge(S("h_final"), 1)
            pool.dma_start(out[0].rearrange("(a p) d -> p a d", p=P), H[:, :, :]).then_inc(S("out_stored"), 16)
            pool.wait_ge(S("out_stored"), 16)

        @block.tensor
        def _(pe):
            mm = nc.tensor.matmul
            seen = {"act": 0, "vector": 0, "attended": 0}

            def project(name, first=False):
                u = UNIT[name]
                _, _, _, n, columns, src = UNITS[u]
                x, pair = sources[src], PAIRS[u % 2]
                if u >= 2:
                    pe.wait_ge(S(f"unit_read{u % 2}"), u // 2)
                if u in split_at:
                    return project_parts(u, columns, n, pair, src, first)
                wait_panel(pe, unit_panel[u])
                w = slot_kn(slot(unit_panel[u]))
                if columns:
                    for fb in range(n // P):
                        for kc in range(KC):
                            last = mm(pair[:, fb // 2, fb % 2 * T:fb % 2 * T + T], w[:, kc, fb * P:(fb + 1) * P],
                                      x[:, kc, :], start=(kc == 0), stop=(kc == KC - 1))
                else:
                    for tc in range(HALVES):
                        for kc in range(KC):
                            last = mm(pair[:, tc, 0:n], x[:, kc, tc * P:(tc + 1) * P], w[:, kc, 0:n],
                                      start=(kc == 0), stop=(kc == KC - 1))
                last.then_inc(S(f"unit_ready{u % 2}"), 1)

            def project_parts(u, columns, n, pair, src, first):
                def columns_part(kc):
                    if first and kc % 2 == 0:
                        if src == "attended":
                            pe.wait_ge(S("attended_low"), 4 * (seen["attended"] - 1) + kc // 2 + 1)
                        else:
                            pe.wait_ge(S("columns_by_vector"), seen["vector"] - 4 + kc // 2 + 1)

                for half in range(2):
                    q = split_at[u] + half
                    pe.wait_ge(S("parts_split"), q + 1)
                    wh, wl = half_tile(q, w_high), half_tile(q, w_low)
                    if columns:
                        for fb in range(2):
                            for kc in range(KC):
                                if half == 0 and fb == 0:
                                    columns_part(kc)
                                f = slice(fb * P, (fb + 1) * P)
                                last = product(pair[:, half, fb * T:(fb + 1) * T], (wh[:, kc, f], wl[:, kc, f]),
                                               (XT_high[:, kc, :], XT_low[:, kc, :]), start=(kc == 0), stop=(kc == KC - 1))
                    else:
                        for tc in range(HALVES):
                            for k in range(4):
                                kc, t = 4 * half + k, slice(tc * P, (tc + 1) * P)
                                if tc == 0:
                                    columns_part(kc)
                                last = product(pair[:, tc, 0:n], (XT_high[:, kc, t], XT_low[:, kc, t]),
                                               (wh[:, k, :], wl[:, k, :]), start=(kc == 0), stop=(kc == KC - 1))
                    last.then_inc(S("parts_read"), 1)

            def turn(src, ready, n, parts=True):
                pe.wait_ge(S(ready), n)
                if seen["act"]:
                    pe.wait_ge(S("columns_by_act"), seen["act"])
                    pe.wait_ge(S("columns_by_vector"), seen["vector"])
                seen["act"] += 4 if parts else 2
                seen["vector"] += 4 if parts else 2
                for kc in range(KC):
                    for tc in range(HALVES):
                        o = kc % 2 * T + tc * P
                        last = nc.tensor.transpose(ps[:, 4 + kc // 2, o:o + P], src[:, tc, kc * P:(kc + 1) * P], IDENT)
                    if kc % 2:
                        last.then_inc(S("turned"), 1)

            def columns_ready():
                pe.wait_ge(S("columns_by_act"), seen["act"])
                pe.wait_ge(S("columns_by_vector"), seen["vector"])

            def product(out_, x_parts, w_parts, start, stop):
                (xh, xl), (wh, wl) = x_parts, w_parts
                mm(out_, xh, wh, start=start, stop=False)
                mm(out_, xl, wh, start=False, stop=False)
                return mm(out_, xh, wl, start=False, stop=stop)

            def turn_probabilities(n):
                pr = prob[n]
                for tc in range(2):
                    pe.wait_ge(S("probs_ready"), 2 * n - 1 + tc)
                    for h in range(4):
                        for mc in range(2):
                            j = h * 2 + mc
                            last = nc.tensor.transpose(ps[:, j // 2, j % 2 * T + tc * P:j % 2 * T + (tc + 1) * P],
                                                       pr[:, tc, h, mc * P:(mc + 1) * P], IDENT)
                last.then_inc(S("probs_turned"), 1)
                pe.wait_ge(S("probsT_by_act"), n)
                pe.wait_ge(S("probsT_by_vector"), n)

            def memory_projections(tag, ready, value):
                turn(XS, ready, value, parts=False)
                columns_ready()
                for j in range(2):
                    project(f"{tag}k{j}")
                for j in range(2):
                    project(f"{tag}v{j}")

            def attention(tag, n, src, ready, value):
                turn(src, ready, value)
                for j in range(2):
                    project(f"{tag}q{j}", first=(j == 0))
                QT, KT, V, PT = w_(10240, KC, T), w_(6144, KC, T), w_(8192, HALVES, D), w_(2048, KC, T)
                for name in (f"{tag}v0", f"{tag}v1", f"{tag}q0", f"{tag}q1"):
                    u = UNIT[name]
                    pe.wait_ge(S(f"unit_read{u % 2}"), u // 2 + 1)
                for tc in range(2):
                    for h in range(4):
                        j = tc * 4 + h
                        for c in range(2):
                            last = mm(ps[:, 4 + j // 2, j % 2 * T:j % 2 * T + T], QT[:, 2 * h + c, tc * P:(tc + 1) * P],
                                      KT[:, 2 * h + c, :], start=(c == 0), stop=(c == 1))
                    last.then_inc(S("scores_ready"), 1)
                turn_probabilities(n - (tag == "C"))
                for f in range(KC):
                    for mc in range(2):
                        last = mm(ps[:, 4 + f // 2, f % 2 * T:f % 2 * T + T], V[:, mc, f * P:(f + 1) * P],
                                  PT[:, f // 2 * 2 + mc, :], start=(mc == 0), stop=(mc == 1))
                    if f % 2:
                        last.then_inc(S("attended"), 1)
                seen["attended"] += 1
                for j in range(2):
                    project(f"{tag}o{j}", first=(j == 0))

            pe.wait_ge(S("vectors_loaded"), 16 * VEC_LOADS)
            pe.wait_ge(S("const_loaded"), 16)
            for t in range(VEC_TILES):
                n = min(P, VEC_ROWS - t * P)
                last = nc.tensor.transpose(ps[:, 4, t * P:t * P + n], w_(0, VEC_TILES, P)[0:n, t, :], IDENT[0:n, 0:n])
            last.then_inc(S("vectors_turned"), 1)
            pe.wait_ge(S("cols_ready"), 1)
            turn(XS, "xs_ready", 1)
            for n in ("h", "gb", "gc", "u"):
                project("in_" + n, first=(n == "h"))
            memory_projections("A", "xs_ready", 2)
            pe.wait_ge(S("poolw_loaded"), 16)
            pe.wait_ge(S("pooled"), 1)
            for g in range(4):
                last = mm(ps[:, 4 + g // 2, g % 2 * T:g % 2 * T + T], poolw[:, g, :], w_(0, 4, T)[:, g, :],
                          start=True, stop=True)
            last.then_inc(S("pool_mixed"), 1)
            pe.wait_ge(S("mixed_by_act"), 1)
            pe.wait_ge(S("mixed_by_vector"), 1)
            for j in range(2):
                project(f"mix{j}")
            attention("A", 1, XS, "xs_ready", 3)
            turn(XS, "xs_ready", 4)
            columns_ready()
            for u in (FFN_AT - 1, FFN_AT - 2):
                pe.wait_ge(S(f"unit_read{u % 2}"), u // 2 + 1)

            def ffn_parts(kind, f, half=0):
                q = ffn_at + ffn_half(kind, f) + half
                pe.wait_ge(S("parts_split"), q + 1)
                return w_high[:, q % SPLITS, :], w_low[:, q % SPLITS, :]

            def hidden(f):
                pair = PAIRS[f % 2]
                if f >= 2:
                    pe.wait_ge(S("ffn_hidden"), f - 1)
                for half in range(2):
                    wh, wl = ffn_parts("gu", f, half)
                    for part in range(2):
                        for kc in range(KC):
                            c = kc * 2 * P + part * P
                            last = product(pair[:, part, half * T:(half + 1) * T], (wh[:, c:c + P], wl[:, c:c + P]),
                                           (XT_high[:, kc, :], XT_low[:, kc, :]), start=(kc == 0), stop=(kc == KC - 1))
                    last.then_inc(S("parts_read"), 1)

            def down(f):
                wh, wl = ffn_parts("down", f)
                pe.wait_ge(S("ffn_hidden_split"), f + 1)
                for tc in range(2):
                    for n in range(2):
                        for fb in range(2):
                            t, o = slice(tc * P, (tc + 1) * P), fb * D + n * 512
                            last = product(ps[:, 4 + tc * 2 + n, :], (FH[:, fb, t], FL[:, fb, t]),
                                           (wh[:, o:o + 512], wl[:, o:o + 512]), start=(f == 0 and fb == 0),
                                           stop=(f == FFN_TURNS - 1 and fb == 1))
                last.then_inc(S("parts_read"), 1)

            hidden(0)
            for f in range(1, FFN_TURNS):
                hidden(f)
                down(f - 1)
            down(FFN_TURNS - 1)
            pe.wait_ge(S("ffn_added"), 1)
            turn(XS, "xs_ready", 5)
            for j in range(2):
                project(f"gate{j}", first=(j == 0))
                project(f"value{j}")
            memory_projections("B", "xs_ready", 6)
            CO, SQ, HC = w_(2304, KC, T), w_(0, KC, T), w_(0, KC, T + CONV - 1)
            pe.wait_ge(S("glu"), 2)
            for b in range(TAPS_ON_PE):
                for k in range(CONV):
                    i = b * CONV + k
                    pe.wait_ge(S("diagonal_ready"), i + 1)
                    mm(ps[:, 4 + b, 0:T], w_(5376, DIAGONALS, P)[:, i % DIAGONALS, :], HC[:, KC - TAPS_ON_PE + b, k:k + T],
                       start=(k == 0), stop=(k == CONV - 1)).then_inc(S("diagonal_used"), 1)
            pe.wait_ge(S("convolved_by_act"), 1)
            pe.wait_ge(S("convolved"), 1)
            for kc in range(KC):
                last = mm(ps[:, 4, 0:T], ONES, CO[:, kc, :], start=(kc == 0), stop=(kc == KC - 1))
            last.then_inc(S("feature_sums"), 1)
            pe.wait_ge(S("squared"), 1)
            for kc in range(KC):
                last = mm(ps[:, 5, 0:T], ONES, SQ[:, kc, :], start=(kc == 0), stop=(kc == KC - 1))
            last.then_inc(S("feature_sums"), 1)
            pe.wait_ge(S("conformed"), 1)
            for j in range(2):
                project(f"pw2_{j}")
            attention("B", 2, XS, "xs_ready", 7)

            def route(k, ready, value, src):
                turn(src, ready, value)
                columns_ready()
                pe.wait_ge(S("small_loaded"), 16 * 10)
                E, G = MOES[k]["experts"], MOES[k]["groups"]
                rt = router1 if k == 1 else router
                for tc in range(2):
                    for kc in range(KC):
                        for part in (XT_high, XT_low):
                            last = mm(ps[:, 4, tc * 16:tc * 16 + E], part[:, kc, tc * P:(tc + 1) * P].bitcast(F32), rt[:, kc, :],
                                      start=(kc == 0 and part is XT_high), stop=(kc == KC - 1 and part is XT_low))
                last.then_inc(S("logits_ready"), 1)
                pe.wait_ge(S("chosen"), k)
                before = c_("before")
                mm(ps[:, 5, 0:G], before, SEL[:, 0, 0:G], start=True, stop=True)
                mm(ps[:, 5, 8:8 + G], ONES, SEL[:, 0, 0:G], start=True, stop=False)
                mm(ps[:, 5, 8:8 + G], before, SEL[:, 1, 0:G], start=False, stop=True)
                mm(ps[:, 5, 16:16 + G], ONES, SEL[:, 0, 0:G], start=True, stop=False)
                mm(ps[:, 5, 16:16 + G], ONES, SEL[:, 1, 0:G], start=False, stop=True).then_inc(S("ranks_ready"), 1)

            def experts(k, x):
                c = MOES[k]
                M, NS, C, halves = c["members"], c["slots"], c["members"] * c["chunks"], stream(c)
                N = len(halves)
                PR, PT, Y, HID = w_(0, 2, P), w_(256, 2, P), w_(512, D), w_(1536, 4, P)

                def gather(turn):
                    pe.wait_ge(moe_sem(k, "picked"), turn + 1)
                    for tc in range(2):
                        mm(ps[:, 7, 0:M], PR[:, tc, :], CBS[:, tc, 0:M], start=(tc == 0), stop=(tc == 1))
                    for kc in range(KC):
                        for tc in range(2):
                            last = mm(ps[:, 5 + kc // 4, kc % 4 * P:kc % 4 * P + P], x[:, tc, kc * P:(kc + 1) * P],
                                      PR[:, tc, :], start=(tc == 0), stop=(tc == 1))
                    last.then_inc(moe_sem(k, "gathered"), 1)

                def turn_picks():
                    for tc in range(2):
                        last = nc.tensor.transpose(ps[:, 7, T + tc * P:T + (tc + 1) * P], PR[:, tc, :], IDENT)
                    last.then_inc(moe_sem(k, "picks_turned"), 1)

                pe.sem_inc(moe_sem(k, "read"), SPLITS)
                gather(0)
                pe.wait_ge(moe_sem(k, "gathered_split"), 1)
                turn_picks()
                pe.wait_ge(moe_sem(k, "turns_ready"), 1)
                turns = pe.value_load(count[0:1, k - 1:k], min_val=c["groups"], max_val=2 * c["groups"])
                with pe.Fori(0, turns) as it:
                    pe.wait_ge(moe_sem(k, "gathered_split"), it + 1)

                    def turn_hidden(ch):
                        pe.wait_ge(moe_sem(k, "gated"), it * C + (ch + 2))
                        for fb in range(4):
                            last = nc.tensor.transpose(ps[:, 4, fb * P:(fb + 1) * P], HID[:, fb, :], IDENT)
                        last.then_inc(moe_sem(k, "hidden_turned"), 1)

                    for j, (kind, ch, half) in enumerate(halves):
                        pe.wait_ge(moe_sem(k, "split"), it * N + (j + 1 + NS))
                        wh, wl = w_high[:, j % SPLITS, :], w_low[:, j % SPLITS, :]
                        if kind == "down":
                            if half == 0:
                                if ch == C - 1:
                                    gather(it + 1)
                                pe.wait_ge(moe_sem(k, "hidden_split"), it * C + (ch + 1))
                            for f in range(2):
                                fb = 2 * half + f
                                for n in range(2):
                                    o = f * D + n * 512
                                    last = product(ps[:, 2 + n, :], (h_high[:, fb, :], h_low[:, fb, :]),
                                                   (wh[:, o:o + 512], wl[:, o:o + 512]),
                                                   start=(ch == 0 and fb == 0), stop=(ch == C - 1 and fb == 3))
                        else:
                            bank = 0 if kind == "gate" else 1
                            if half == 0:
                                pe.wait_ge(moe_sem(k, "silu" if kind == "gate" else "gated"), it * C + (ch + 1))
                            for f in range(4):
                                kc, o = 4 * half + f, f * PANEL
                                last = product(ps[:, bank, :], (x_high[:, kc, :], x_low[:, kc, :]),
                                               (wh[:, o:o + PANEL], wl[:, o:o + PANEL]),
                                               start=(kc == 0), stop=(kc == KC - 1))
                        last.then_inc(moe_sem(k, "read"), 1)
                        for t in range(C):
                            if j == chunk_at(t) + 5:
                                turn_hidden(t)
                    pe.wait_ge(moe_sem(k, "outputs_by_act"), it + 1)
                    pe.wait_ge(moe_sem(k, "outputs_by_vector"), it + 1)
                    pe.wait_ge(moe_sem(k, "gathered_split"), it + 2)
                    pe.wait_ge(moe_sem(k, "picks_ready"), it + 1)
                    for j in range(4):
                        if j >= 2:
                            pe.wait_ge(moe_sem(k, "added"), it * 4 + (j - 1))
                        mm(ps[:, 5 + j % 2, :], PT[:, j // 2, :], Y[:, j % 2 * 512:(j % 2 + 1) * 512],
                           start=True, stop=True).then_inc(moe_sem(k, "scattered"), 1)
                    turn_picks()
                    pe.wait_ge(moe_sem(k, "added"), it * 4 + 4)
                pe.wait_ge(moe_sem(k, "picks_ready"), turns + 1)

            route(1, "xs_ready", 8, XS)
            experts(1, XS)
            turn(H, "h_ready", 1)
            for n in ("fqk", "dqk", "hq", "fv", "dv", "hf", "hi", "hg"):
                project(n, first=(n == "fqk"))
            FQK, DQK, QH, KH = w_(0, 4, T), w_(1024, 4, T), w_(2048, 4, T), w_(3072, 4, T)
            LF, HI = w_(4096, 2, 512), w_(5120, 2, 512)
            FV, DV = w_(7168, 2, 256), w_(7680, 2, 256)
            PT = w_(10240, KC, T)
            pe.wait_ge(S("fox_log"), 1)
            upto, ones = c_("upto"), ONES
            mm(ps[:, 4, 0:4], upto, logf_fox[:, 0, :], start=True, stop=True)
            mm(ps[:, 4, 4:8], ones, logf_fox[:, 0, :], start=True, stop=False)
            mm(ps[:, 4, 4:8], upto, logf_fox[:, 1, :], start=False, stop=True).then_inc(S("fox_sums"), 1)
            for h in range(4):
                o = ps[:, 6 + h // 2, h % 2 * T:h % 2 * T + T]
                mm(o[:, 0:P], logf_fox[:, 0, h:h + 1].broadcast_to([P, P]), upto, start=True, stop=True)
                mm(o[:, P:T], logf_fox[:, 0, h:h + 1].broadcast_to([P, P]), ones, start=True, stop=False)
                last = mm(o[:, P:T], logf_fox[:, 1, h:h + 1].broadcast_to([P, P]), upto, start=False, stop=True)
            last.then_inc(S("fox_sums"), 1)
            pe.wait_ge(S("fox_bias"), 1)
            pe.wait_ge(S("recurrent_keys"), 1)
            KR = w_(8192, 2, 512)
            for h in range(4):
                for tc in range(2):
                    last = nc.tensor.transpose(ps[:, 4 + h // 2, h % 2 * T + tc * P:h % 2 * T + (tc + 1) * P],
                                               KR[:, tc, h * P:(h + 1) * P], IDENT)
            last.then_inc(S("keys_turned"), 1)
            pe.wait_ge(S("keys_columns"), 1)

            def small_attention(n, scores, v):
                scores()
                turn_probabilities(n)
                for tc in range(2):
                    for place, h in enumerate(HEAD_ORDER):
                        for mc in range(2):
                            last = mm(ps[:, 4, tc * T + h * 64:tc * T + h * 64 + 64], PT[:, place * 2 + mc, tc * P:(tc + 1) * P],
                                      v[:, mc, h * 64:(h + 1) * 64], start=(mc == 0), stop=(mc == 1))
                last.then_inc(S("small_attended"), 1)

            def fox_scores():
                u = UNIT["hg"]
                pe.wait_ge(S(f"unit_read{(u - 1) % 2}"), (u - 1) // 2 + 1)
                pe.wait_ge(S(f"unit_read{u % 2}"), u // 2 + 1)
                for tc in range(2):
                    for place, h in enumerate(HEAD_ORDER):
                        j, p0 = tc * 4 + place, 64 * (h % 2)
                        last = mm(ps[:, 4 + j // 2, j % 2 * T:j % 2 * T + T],
                                  FQK[p0:p0 + 64, h // 2, tc * P:(tc + 1) * P], FQK[p0:p0 + 64, 2 + h // 2, :],
                                  start=True, stop=True)
                last.then_inc(S("scores_ready"), 2)

            def diff_scores(which):
                for tc in range(2):
                    for place, h in enumerate(HEAD_ORDER):
                        j, p0 = tc * 4 + place, 64 * (h % 2) + 32 * which
                        last = mm(ps[:, 4 + j // 2, j % 2 * T:j % 2 * T + T],
                                  DQK[p0:p0 + 32, h // 2, tc * P:(tc + 1) * P], DQK[p0:p0 + 32, 2 + h // 2, :],
                                  start=True, stop=True)
                last.then_inc(S("scores_ready"), 2)

            small_attention(3, fox_scores, FV)
            pe.wait_ge(S("small_read"), 1)

            def both_maps():
                diff_scores(0)
                pe.wait_ge(S("diff_map"), 1)
                diff_scores(1)

            small_attention(4, both_maps, DV)
            pe.wait_ge(S("small_read"), 2)
            ST = w_(11264, 8, P)
            for h in range(4):
                for tc in range(2):
                    last = mm(ps[:, h // 2, h % 2 * T + tc * P:h % 2 * T + (tc + 1) * P],
                              KH[:, h, tc * P:(tc + 1) * P], QH[:, h, tc * P:(tc + 1) * P], start=True, stop=True)
            last.then_inc(S("level_scores"), 1)
            pe.wait_ge(S("levels_loaded"), 16)

            def level_spans(lv):
                if lv >= 2:
                    pe.wait_ge(S("level_exp"), lv - 1)
                for h in range(4):
                    for tc in range(2):
                        sp = c_(f"span{lv}") if lv < 7 else (c_("after") if tc == 0 else upto)
                        last = mm(ps[:, 4 + lv % 2 * 2 + h // 2, h % 2 * T + tc * P:h % 2 * T + (tc + 1) * P],
                                  LF[:, tc, h * P:(h + 1) * P], sp, start=True, stop=True)
                last.then_inc(S("level_spans"), 1)

            level_spans(0)
            level_spans(1)
            for lv in range(8):
                if lv + 2 < 8:
                    level_spans(lv + 2)
                _, QE, KE = level_tiles(lv)
                pe.wait_ge(S("level_decayed"), lv + 1)
                if lv:
                    pe.wait_ge(S("level_merged"), lv)
                if lv < 7:
                    for h in range(4):
                        for tc in range(2):
                            last = mm(ps[:, (lv + 1) % 2 * 2 + h // 2, h % 2 * T + tc * P:h % 2 * T + (tc + 1) * P],
                                      KE[:, h, tc * P:(tc + 1) * P], QE[:, h, tc * P:(tc + 1) * P], start=True, stop=True)
                else:
                    for h in range(4):
                        last = mm(ps[:, 0, h * P:(h + 1) * P], KE[:, h, 0:P], QE[:, h, P:T], start=True, stop=True)
                last.then_inc(S("level_scores"), 1)
            pe.wait_ge(S("level_merged"), 9)
            CR = w_(8192, 4, P)
            for h in range(4):
                v = lambda tc: HI[:, tc, h * P:(h + 1) * P]
                mm(ps[:, 2, h * P:(h + 1) * P], ST[:, 2 * h, :], v(0), start=True, stop=True)
                mm(ps[:, 3, h * P:(h + 1) * P], ST[:, 2 * h + 1, :], v(1), start=True, stop=False)
                last = mm(ps[:, 3, h * P:(h + 1) * P], CR[:, h, :], v(0), start=False, stop=True)
            last.then_inc(S("recurrence_out"), 1)
            turn(XS, "xs_ready", 9)
            for j in range(2):
                project(f"out{j}", first=(j == 0))
            memory_projections("C", "memory_loaded", 48)
            attention("C", 6, H, "h_ready", 2)
            route(2, "h_ready", 3, H)
            experts(2, H)

        @block.scalar
        def _(act):
            A = nc.scalar.activation
            n_ = {"sq": 0, "sqrt": 0, "turn": 0, "high": 0, "ln": 0}
            step = Steps(act, S("scalar_step"))

            def squares(src, ready, n, junk, shared):
                act.wait_ge(S(ready), n)
                if n_["sq"]:
                    act.wait_ge(S("variance_ready"), n_["sqrt"])
                n_["sq"] += 1
                if not shared:
                    step(A(junk[:, 1, :], src[:, 1, :], ACT.Square, accum_out=ssq[:, 1:2]))
                A(junk[:, 0, :], src[:, 0, :], ACT.Square, accum_out=ssq[:, 0:1]).then_inc(S("squares_summed"), 1)

            def root(n=2, src=None, dst=None):
                n_["sqrt"] += 1
                act.wait_ge(S("variance_ready"), n_["sqrt"])
                A(dst if dst is not None else std, src if src is not None else var, ACT.Sqrt).then_inc(S("deviation_ready"), 1)

            def layer_norm(src=H):
                n_["ln"] += 1
                act.wait_ge(S("mean_ready"), n_["ln"])
                act.wait_ge(S("variance_ready"), n_["sqrt"])
                for tc in range(2):
                    last = A(w_(2048, HALVES, D)[:, tc, :], src[:, tc, :], ACT.Square, bias=mean[:, tc:tc + 1],
                             accum_out=ssq[:, tc:tc + 1])
                last.then_inc(S("centred_squares"), 1)
                root()

            def rms(src, ready, n, junk=XS, shared=True):
                squares(src, ready, n, junk, shared)
                root()

            def columns(dst, gain, banks=(4, 5)):
                n_["turn"] += 1
                act.wait_ge(S("turned"), 4 * n_["turn"] - 2)
                for kc in range(4):
                    src = ps[:, 4 + kc // 2, kc % 2 * T:kc % 2 * T + T]
                    if gain is None:
                        last = A(dst[:, kc, :], src, ACT.Copy)
                    else:
                        last = A(dst[:, kc, :], src, ACT.Copy, scale=vec(gain[0], gain[1] + kc))
                    if kc % 2:
                        last.then_inc(S("columns_by_act"), 1)

            def columns_high(gain):
                n_["turn"] += 1
                for kc in range(KC):
                    if kc % 2 == 0:
                        act.wait_ge(S("turned"), 4 * n_["turn"] - 3 + kc // 2)
                    src = ps[:, 4 + kc // 2, kc % 2 * T:kc % 2 * T + T]
                    if gain is None:
                        last = A(XT_high[:, kc, :], src, ACT.Copy)
                    else:
                        last = A(XT_high[:, kc, :], src, ACT.Copy, scale=vec(gain[0], gain[1] + kc))
                    if kc % 2:
                        last.then_inc(S("columns_by_act"), 1)

            def highs(end):
                while n_["high"] < end:
                    q = n_["high"]
                    wait_panel(act, pieces_split[q][0])
                    if q >= SPLITS:
                        act.wait_ge(S("parts_read"), q - SPLITS + 1)
                    A(half_tile(q, w_high), half_source(q), ACT.Copy).then_inc(S("parts_high"), 1)
                    n_["high"] += 1

            def take(name, dst, func=ACT.Copy, **kw):
                u = UNIT[name]
                unit_ready(act, u)
                A(dst, PAIRS[u % 2], func, **kw).then_inc(S(f"unit_read{u % 2}"), 1)

            def take_columns(name, dst):
                u = UNIT[name]
                unit_ready(act, u)
                A(dst, PAIRS[u % 2].rearrange("p a (b t) -> p (a b) t", t=T), ACT.Copy).then_inc(S(f"unit_read{u % 2}"), 1)

            def softmax(n, scale, dst, src_sbuf=None):
                for j in range(8):
                    if j % 4 == 0:
                        act.wait_ge(S("softmax_bias"), 2 * n - 1 + j // 4)
                    src = ps[:, 4 + j // 2, j % 2 * T:j % 2 * T + T] if src_sbuf is None else src_sbuf[:, j // 4, j % 4, :]
                    last = A(dst[:, j // 4, j % 4, :], src, ACT.Exp, bias=nbias[:, j:j + 1], scale=scale,
                             accum_out=den[:, j:j + 1])
                    if j % 4 == 3:
                        last.then_inc(S("exponentials"), 1)

            def probs_columns(n, dst):
                act.wait_ge(S("probs_turned"), n)
                A(dst[:, 0:4, :], ps[:, 0:2, :].rearrange("p a (b t) -> p (a b) t", t=T), ACT.Copy).then_inc(S("probsT_by_act"), 1)

            def memory_norm(tag):
                rms(XS, "memory_loaded", 16 * ("ABC".index(tag) + 1), junk=w_(10240, HALVES, D), shared=False)

            def memory_projections(tag, gain):
                if gain:
                    columns(XT, gain)
                for j in range(2):
                    take_columns(f"{tag}k{j}", w_(6144, KC, T)[:, 4 * j:4 * j + 4, :])
                for j in range(2):
                    take(f"{tag}v{j}", w_(8192, HALVES, D)[:, :, j * 512:(j + 1) * 512])

            def attention(tag, n, gain, ready):
                QT, PT = w_(10240, KC, T), w_(2048, KC, T)
                highs(halves_to(f"{tag}q0", 1))
                if ready:
                    rms(H, *ready)
                columns_high(gain)
                highs(halves_to(f"{tag}q1"))
                take_columns(f"{tag}q0", QT[:, 0:4, :])
                highs(halves_to(f"{tag}q1", 3))
                softmax(n, 1.0 / 16, w_(0, 2, 4, T))
                probs_columns(n - (tag == "C"), PT)
                for b in range(4):
                    act.wait_ge(S("attended"), 4 * "ABC".index(tag) + b + 1)
                    A(XT_high[:, 2 * b:2 * b + 2, :], ps[:, 4 + b, :].rearrange("p (b t) -> p b t", t=T), ACT.Copy)\
                        .then_inc(S("attended_high"), 1)
                highs(halves_to(f"{tag}o1"))

            act.wait_ge(S("vectors_turned"), 1)
            A(cols[:, 0:VEC_ROWS], ps[:, 4, 0:VEC_ROWS], ACT.Copy).then_inc(S("cols_ready"), 1)
            act.wait_ge(S("cols_ready"), 1)
            rms(H, "x_loaded", 16)
            highs(halves_to("in_h", 1))
            columns_high(("ev_norm_mix", 0))
            highs(halves_to("in_gb"))
            take_columns("in_h", w_(0, 4, T))
            highs(halves_to("in_gc"))
            take_columns("in_gb", w_(1024, 4, T))
            highs(halves_to("in_u"))
            memory_norm("A")
            memory_projections("A", ("xa_norm_mem", 0))
            act.wait_ge(S("pool_mixed"), 1)
            for g in range(4):
                last = A(w_(10240, KC, T)[:, 4 + g, :], ps[:, 4 + g // 2, g % 2 * T:g % 2 * T + T], ACT.Copy,
                         scale=vec("ev_pool_scale", g))
            last.then_inc(S("mixed_by_act"), 1)
            attention("A", 1, ("xa_norm", 0), ("h_updated", 1))
            highs(ffn_at + 2)
            rms(H, "h_updated", 2)
            columns_high(("ev_norm_ffn", 0))

            def ffn_silu(f):
                act.wait_ge(S("parts_read"), ffn_at + ffn_half("gu", f) + 2)
                if f >= 2:
                    act.wait_ge(S("ffn_hidden"), f - 1)
                A(w_(2048 + 512 * (f % 2), 512), PAIRS[f % 2][:, 0, :], ACT.Silu).then_inc(S("ffn_silu"), 1)

            for f in range(FFN_TURNS):
                highs(ffn_at + ffn_half("gu", f) + 1)
                if f:
                    ffn_silu(f - 1)
                highs(ffn_at + ffn_half("gu", f) + 2)
                if f:
                    highs(ffn_at + ffn_half("down", f - 1) + 1)
            ffn_silu(FFN_TURNS - 1)
            highs(ffn_at + 3 * FFN_TURNS)
            highs(halves_to("gate0"))
            rms(H, "ffn_added", 1)
            columns_high(("od_norm_mix", 0))
            highs(halves_to("value0"))
            for j in range(2):
                u = UNIT[f"gate{j}"]
                unit_ready(act, u)
                if j:
                    act.wait_ge(S("glu"), 1)
                src = PAIRS[u % 2].rearrange("p a (b t) -> p (a b) t", t=T)
                for b in range(4):
                    last = A(w_(2304, 4, T)[:, b, :], src[:, b, :], ACT.Sigmoid, bias=vec("od_pw1_b", 8 + 4 * j + b))
                last.then_inc(S(f"unit_read{u % 2}"), 1)
                if j == 0:
                    highs(halves_to("gate1"))
                    memory_norm("B")
                    highs(halves_to("value1"))
            memory_projections("B", ("xa_norm_mem", 8))
            for b in range(TAPS_ON_PE):
                for k in range(CONV):
                    i = b * CONV + k
                    if i >= DIAGONALS:
                        act.wait_ge(S("diagonal_used"), i - DIAGONALS + 1)
                    A(w_(5376, DIAGONALS, P)[:, i % DIAGONALS, :], IDENT, ACT.Copy,
                      scale=vec("od_dw_w", KC * k + KC - TAPS_ON_PE + b)).then_inc(S("diagonal_ready"), 1)
            act.wait_ge(S("diagonal_used"), TAPS_ON_PE * CONV)
            for b in range(TAPS_ON_PE):
                kc = KC - TAPS_ON_PE + b
                last = A(w_(2304, KC, T)[:, kc, :], ps[:, 4 + b, 0:T], ACT.Identity, bias=vec("od_dw_b", kc))
            last.then_inc(S("convolved_by_act"), 1)
            root(src=w_(4608, T), dst=w_(4864, T))
            act.wait_ge(S("standard"), 1)
            for kc in range(KC):
                last = A(w_(2304, KC, T)[:, kc, :], w_(2304, KC, T)[:, kc, :], ACT.Silu, scale=vec("od_ln_g", kc),
                         bias=vec("od_ln_b", kc))
            last.then_inc(S("conformed"), 1)
            attention("B", 2, ("xa_norm", 8), ("h_updated", 3))

            def experts(k, gain):
                c = MOES[k]
                NS, C, halves = c["slots"], c["members"] * c["chunks"], stream(c)
                N = len(halves)
                Y, SG = w_(512, D), w_(2048, PANEL)
                uses = {q: sum(1 for j in range(N) if j % NS == q) for q in range(NS)}

                def gathered_high(turn):
                    act.wait_ge(moe_sem(k, "gathered"), turn + 1)
                    if gain:
                        for kc in range(KC):
                            last = A(x_high[:, kc, :], ps[:, 5 + kc // 4, kc % 4 * P:kc % 4 * P + P], ACT.Copy,
                                     scale=vec(gain, kc))
                    else:
                        for b in range(2):
                            last = A(x_high[:, 4 * b:4 * b + 4, :], ps[:, 5 + b, :].rearrange("p (k t) -> p k t", t=P), ACT.Copy)
                    last.then_inc(moe_sem(k, "gathered_high"), 1)

                gathered_high(0)
                act.wait_ge(moe_sem(k, "turns_ready"), 1)
                turns = act.value_load(count[0:1, k - 1:k], min_val=c["groups"], max_val=2 * c["groups"])
                with act.Fori(0, turns) as it:

                    def silu(ch):
                        act.wait_ge(moe_sem(k, "read"), it * N + (chunk_at(ch) + 2 + SPLITS))
                        A(SG, ps[:, 0, :], ACT.Silu).then_inc(moe_sem(k, "silu"), 1)

                    def hidden_high(ch):
                        act.wait_ge(moe_sem(k, "hidden_turned"), it * C + (ch + 1))
                        A(h_high[:, :, :], ps[:, 4, :].rearrange("p (k t) -> p k t", t=P), ACT.Copy)\
                            .then_inc(moe_sem(k, "hidden_high"), 1)

                    for j in range(N):
                        for ch in range(C):
                            if j == chunk_at(ch) + 4:
                                silu(ch)
                            if j == chunk_at(ch) + 8:
                                hidden_high(ch)
                        act.wait_ge(moe_sem(k, f"landed{j % NS}"), it * (16 * uses[j % NS]) + 16 * (j // NS + 1))
                        act.wait_ge(moe_sem(k, "read"), it * N + (j + 1))
                        A(w_high[:, j % SPLITS, :], ring[:, j % NS, :], ACT.Copy).then_inc(moe_sem(k, "high"), 1)
                    hidden_high(C - 1)
                    gathered_high(it + 1)
                    act.wait_ge(moe_sem(k, "read"), it * N + (N + SPLITS))
                    A(Y[:, 0:512], ps[:, 2, :], ACT.Copy).then_inc(moe_sem(k, "outputs_by_act"), 1)

            rms(H, "h_updated", 4)
            columns_high(("od_norm_moe", 0))
            act.wait_ge(S("logit_gap"), 1)
            A(PAIRW[:, 1, :], PAIRW[:, 0, :], ACT.Exp).then_inc(S("gap_exp"), 1)
            experts(1, "od_norm_moe")
            rms(H, "moe_done", 1, shared=False)
            highs(halves_to("fqk", -1))
            layer_norm()
            highs(halves_to("fqk", 1))
            columns_high(None)
            highs(halves_to("hq"))
            take_columns("dqk", w_(1024, 4, T))
            highs(halves_to("fv"))
            u = UNIT["hq"]
            unit_ready(act, u)
            A(w_(2048, 4, T), PAIRS[u % 2].rearrange("p a (b t) -> p (a b) t", t=T), ACT.Silu).then_inc(S(f"unit_read{u % 2}"), 1)
            act.wait_ge(S("lam_sums"), 1)
            A(lame, lamp, ACT.Exp).then_inc(S("lam_exp"), 1)
            highs(halves_to("dv"))
            act.wait_ge(S("fox_logits"), 1)
            step(A(ffa, ffl, ACT.Abs))
            step(A(ffa, ffa, ACT.Exp, scale=-1.0))
            A(ffa, ffa, ACT.Ln, bias=1.0).then_inc(S("fox_log1p"), 1)
            highs(halves_to("hi"))
            HFZ, HFA, KR = w_(9216, 2, 512), w_(4096, 2, 512), w_(8192, 2, 512)
            act.wait_ge(S("forget_logits"), 1)
            step(A(HFA, HFZ, ACT.Abs))
            step(A(HFA, HFA, ACT.Exp, scale=-1.0))
            A(HFA, HFA, ACT.Ln, bias=1.0).then_inc(S("forget_log1p"), 1)
            A(KR, HFZ, ACT.Sigmoid, scale=-1.0).then_inc(S("recurrent_keys"), 1)
            highs(halves_to("hg"))
            take("hi", w_(5120, 2, 512))
            u = UNIT["hg"]
            unit_ready(act, u)
            A(w_(6144, 2, 512), PAIRS[u % 2], ACT.Silu).then_inc(S(f"unit_read{u % 2}"), 1)
            act.wait_ge(S("keys_turned"), 1)
            A(w_(3072, 4, T), ps[:, 4:6, :].rearrange("p a (b t) -> p (a b) t", t=T), ACT.Copy).then_inc(S("keys_columns"), 1)
            PR, PT = w_(8192, 2, 4, T), w_(10240, KC, T)
            softmax(3, 1.0, PR, PR)
            probs_columns(3, PT)
            softmax(4, 1.0, PR, PR)
            softmax(5, 1.0, w_(10240, 2, 4, T), w_(10240, 2, 4, T))
            probs_columns(4, PT)
            root(src=dss, dst=dstd)
            for lv in range(8):
                act.wait_ge(S("level_spans"), lv + 1)
                if lv >= 2:
                    act.wait_ge(S("level_decayed"), lv - 1)
                elif lv == 0:
                    act.wait_ge(S("diff_done"), 1)
                A(level_tiles(lv)[0], ps[:, 4 + lv % 2 * 2:6 + lv % 2 * 2, :].rearrange("p a (b t) -> p (a b) t", t=T), ACT.Exp)\
                    .then_inc(S("level_exp"), 1)
            highs(halves_to("out0", 1))
            root(src=dss, dst=dstd)
            columns_high(None)
            highs(halves_to("out1"))
            columns(XT, None)
            layer_norm()
            memory_projections("C", None)
            attention("C", 6, None, None)
            layer_norm()
            columns_high(None)
            act.wait_ge(S("logits_ready"), 2)
            A(LG, ps[:, 4, 0:32].rearrange("p (a e) -> p a e", e=16), ACT.Sigmoid).then_inc(S("router_scores"), 1)
            experts(2, None)
            layer_norm(XS)

        @block.vector
        def _(dve):
            V = nc.vector
            step = Steps(dve, S("vector_step"))
            n_ = {"sq": 0, "rt": 0, "xs": 0, "turn": 0, "act": 0, "halves": 0, "ln": 0, "b0": 0, "b1": 0}
            MUL, ADD, SUB = ALU.mult, ALU.add, ALU.subtract

            def rsqrt(dst=None, src=None):
                n_["rt"] += 1
                dve.wait_ge(S("deviation_ready"), n_["rt"])
                step(V.reciprocal(dst if dst is not None else rstd, src if src is not None else std))

            def rms(src, dst, eps):
                n_["sq"] += 1
                if src is H:
                    step(V.tensor_tensor_reduce(out=dst[:, 1, :], in0=src[:, 1, :], in1=src[:, 1, :], scale=1.0, scalar=0.0,
                                                op0=MUL, op1=ADD, accum_out=ssq[:, 1:2]))
                dve.wait_ge(S("squares_summed"), n_["sq"])
                V.tensor_scalar(var, ssq, 1.0 / D, eps, MUL, ADD).then_inc(S("variance_ready"), 1)
                rsqrt()
                for tc in range(2):
                    last = V.tensor_scalar(dst[:, tc, :], src[:, tc, :], rstd[:, tc:tc + 1], None, MUL)
                last.then_inc(S("xs_ready"), 1)

            def columns(dst, gain):
                n_["turn"] += 1
                n_["act"] += 2
                dve.wait_ge(S("turned"), 4 * n_["turn"])
                for kc in range(4, 8):
                    src = ps[:, 4 + kc // 2, kc % 2 * T:kc % 2 * T + T]
                    if gain is None:
                        last = V.tensor_copy(dst[:, kc, :], src)
                    else:
                        last = V.tensor_scalar(dst[:, kc, :], src, vec(gain[0], gain[1] + kc), None, MUL)
                    if kc % 2:
                        last.then_inc(S("columns_by_vector"), 1)

            def columns_low(gain):
                n_["turn"] += 1
                for kc in range(KC):
                    if kc % 2 == 0:
                        n_["act"] += 1
                        dve.wait_ge(S("columns_by_act"), n_["act"])
                    src, high = ps[:, 4 + kc // 2, kc % 2 * T:kc % 2 * T + T], XT_high[:, kc, :].bitcast(F32)
                    if gain is None:
                        last = V.tensor_tensor(XT_low[:, kc, :], src, high, SUB)
                    else:
                        last = V.scalar_tensor_tensor(XT_low[:, kc, :], src, vec(gain[0], gain[1] + kc), high, MUL, SUB)
                    if kc % 2:
                        last.then_inc(S("columns_by_vector"), 1)

            def lows(end):
                while n_["halves"] < end:
                    q = n_["halves"]
                    dve.wait_ge(S("parts_high"), q + 1)
                    V.tensor_tensor(half_tile(q, w_low), half_source(q), half_tile(q, w_high).bitcast(F32), SUB)\
                        .then_inc(S("parts_split"), 1)
                    n_["halves"] += 1

            def take(name, dst):
                u = UNIT[name]
                unit_ready(dve, u)
                V.tensor_copy(dst, PAIRS[u % 2]).then_inc(S(f"unit_read{u % 2}"), 1)

            def take_columns(name, dst):
                u = UNIT[name]
                unit_ready(dve, u)
                V.tensor_copy(dst, PAIRS[u % 2].rearrange("p a (b t) -> p (a b) t", t=T)).then_inc(S(f"unit_read{u % 2}"), 1)

            def add_unit(name, j, scale=None, signal=None):
                u = UNIT[name]
                unit_ready(dve, u)
                h = H[:, :, j * 512:(j + 1) * 512]
                if scale is None:
                    ins = V.tensor_tensor(h, h, PAIRS[u % 2], ADD)
                else:
                    ins = V.scalar_tensor_tensor(h, h, scale, PAIRS[u % 2], MUL, ADD)
                ins.then_inc(S(f"unit_read{u % 2}"), 1)

            def update_done(name):
                u = UNIT[name]
                for w in (u - 1, u):
                    dve.wait_ge(S(f"unit_read{w % 2}"), w // 2 + 1)

            def use_row(b, last):
                last.then_inc(S(f"brow{b}_used"), 1)
                dve.wait_ge(S(f"brow{b}_used"), n_[f"b{b}"])

            def row(b):
                n_[f"b{b}"] += 1
                dve.wait_ge(S(f"brow{b}_loaded"), 16 * n_[f"b{b}"])
                return brow[:, b, :]

            def layer_norm(signal, src=H):
                n_["ln"] += 1
                step(V.tensor_reduce(mean, src[:, :, :], X, ADD))
                V.tensor_scalar(mean, mean, -1.0 / D, None, MUL).then_inc(S("mean_ready"), 1)
                dve.wait_ge(S("mean_ready"), n_["ln"])
                g, centred = row(gain_row[0]), w_(0, HALVES, D)
                for tc in range(2):
                    last = V.scalar_tensor_tensor(centred[:, tc, :], src[:, tc, :], mean[:, tc:tc + 1], g, ADD, MUL)
                use_row(gain_row[0], last)
                dve.wait_ge(S("centred_squares"), n_["ln"])
                V.tensor_scalar(var, ssq, 1.0 / D, LN_EPS, MUL, ADD).then_inc(S("variance_ready"), 1)
                rsqrt()
                b = row(1 - gain_row[0])
                for tc in range(2):
                    last = V.scalar_tensor_tensor(H[:, tc, :], centred[:, tc, :], rstd[:, tc:tc + 1], b, MUL, ADD)
                use_row(1 - gain_row[0], last)
                gain_row[0] = 1
                dve.sem_inc(S(signal), 1)

            gain_row = [0]

            def scores_max(src, scale, tc):
                h = slice(4 * tc, 4 * tc + 4)
                step(V.tensor_reduce(mx[:, h], src, X, ALU.max))
                V.tensor_scalar(nbias[:, h], mx[:, h], -scale, None, MUL).then_inc(S("softmax_bias"), 1)

            def normalise(n, probs, tc):
                h = slice(4 * tc, 4 * tc + 4)
                dve.wait_ge(S("exponentials"), 2 * n - 1 + tc)
                step(V.reciprocal(rden[:, h], den[:, h]))
                return V.tensor_tensor(probs[:, tc], probs[:, tc], rden[:, h].rearrange("p (a b) -> p a b", b=1).broadcast_to([P, 4, T]), MUL)

            def probs_columns(n, dst):
                dve.wait_ge(S("probs_turned"), n)
                V.tensor_copy(dst[:, 4:8, :], ps[:, 2:4, :].rearrange("p a (b t) -> p (a b) t", t=T)).then_inc(S("probsT_by_vector"), 1)

            def attention(tag, n, gain):
                QT, PT = w_(10240, KC, T), w_(2048, KC, T)
                if gain:
                    rms(H, XS, EPS)
                lows(halves_to(f"{tag}q0", -1))
                columns_low(gain)
                lows(halves_to(f"{tag}q1"))
                take_columns(f"{tag}q1", QT[:, 4:8, :])
                lows(halves_to(f"{tag}q1", 1))
                for tc in range(2):
                    dve.wait_ge(S("scores_ready"), 2 * n - 1 + tc)
                    scores_max(ps[:, 4 + 2 * tc:6 + 2 * tc, :].rearrange("p a (b t) -> p (a b) t", t=T), 1.0 / 16, tc)
                lows(halves_to(f"{tag}q1", 3))
                for tc in range(2):
                    normalise(n, w_(0, 2, 4, T), tc).then_inc(S("probs_ready"), 1)
                probs_columns(n - (tag == "C"), PT)
                for b in range(4):
                    dve.wait_ge(S("attended_high"), 4 * "ABC".index(tag) + b + 1)
                    V.tensor_tensor(XT_low[:, 2 * b:2 * b + 2, :], ps[:, 4 + b, :].rearrange("p (b t) -> p b t", t=T),
                                    XT_high[:, 2 * b:2 * b + 2, :].bitcast(F32), SUB).then_inc(S("attended_low"), 1)
                lows(halves_to(f"{tag}o1"))
                for j in range(2):
                    add_unit(f"{tag}o{j}", j, ALPHA if tag == "C" else None)
                    if j == 0 and tag == "A":
                        lows(ffn_at + 2)
                update_done(f"{tag}o1")

            dve.wait_ge(S("x_loaded"), 16)
            dve.wait_ge(S("cols_ready"), 1)
            rms(H, XS, EPS)
            lows(halves_to("in_h", -1))
            columns_low(("ev_norm_mix", 0))
            lows(halves_to("in_gc"))
            AP_, UP = w_(2048, 4, 258), w_(3084, 4, 272)
            V.memset(AP_, 0.0)
            step(V.memset(UP, 0.0))
            lows(halves_to("in_u"))
            u = UNIT["in_gc"]
            unit_ready(dve, u)
            dve.wait_ge(S(f"unit_read{UNIT['in_h'] % 2}"), 1)
            V.tensor_tensor(AP_[:, :, 1:257], w_(0, 4, T), PAIRS[u % 2].rearrange("p a (b t) -> p (a b) t", t=T), MUL)\
                .then_inc(S(f"unit_read{u % 2}"), 1)
            take_columns("in_u", UP[:, :, 8:264])
            dve.wait_ge(S("unit_read0"), 2)
            dve.wait_ge(S("unit_read1"), 2)
            MIXT, INV, PO = w_(10240, KC, T), w_(4736, 4, T), w_(0, 4, T)
            CT = MIXT[:, 0:4, :]
            rms(XS, XS, EPS)
            columns(XT, ("xa_norm_mem", 0))
            dve.wait_ge(S("window_loaded"), 16)
            for k in range(3):
                for b in range(4):
                    wv = vec("ev_conv_a", 4 * k + b)
                    if k == 0:
                        last = V.tensor_scalar(CT[:, b, :], AP_[:, b, 0:T], wv, None, MUL)
                    else:
                        last = V.scalar_tensor_tensor(CT[:, b, :], AP_[:, b, k:k + T], wv, CT[:, b, :], MUL, ADD)
                step(last)
            V.tensor_tensor(MIXT[:, 0:4, :], CT, w_(1024, 4, T), MUL).then_inc(S("mixed_by_vector"), 1)
            SA, SB_ = w_(4172, 272), w_(4444, 272)
            for g, win in enumerate(WINDOWS):
                cur, size, nxt = UP[:, g, :], 1, SA
                while size < win:
                    n = 272 - 2 * size
                    step(V.tensor_tensor(nxt[:, 0:n], cur[:, 0:n], cur[:, size:size + n], ADD))
                    cur, nxt, size = nxt, (SB_ if nxt is SA else SA), size * 2
                at = 8 - win // 2
                step(V.tensor_tensor(PO[:, g, :], cur[:, at:at + T], INV[:, g, :], MUL))
                last = V.tensor_tensor(PO[:, g, :], PO[:, g, :], UP[:, g, 8:264], SUB)
                step(last)
            dve.sem_inc(S("pooled"), 1)
            dve.wait_ge(S("mixed_by_act"), 1)
            dve.wait_ge(S("mixed_by_vector"), 1)
            for j in range(2):
                add_unit(f"mix{j}", j)
            update_done("mix1")
            dve.sem_inc(S("h_updated"), 1)
            attention("A", 1, ("xa_norm", 0))
            dve.sem_inc(S("h_updated"), 1)
            rms(H, XS, EPS)
            columns_low(("ev_norm_ffn", 0))
            F, f_parts = w_(0, 512), lambda t: t.rearrange("p k t -> p (k t)")

            def ffn_hidden(f):
                dve.wait_ge(S("ffn_silu"), f + 1)
                V.tensor_tensor(F, w_(2048 + 512 * (f % 2), 512), PAIRS[f % 2][:, 1, :], MUL).then_inc(S("ffn_hidden"), 1)
                dve.wait_ge(S("ffn_hidden"), f + 1)
                if f:
                    dve.wait_ge(S("parts_read"), ffn_at + ffn_half("down", f - 1) + 1)
                step(V.tensor_copy(f_parts(FH), F))
                V.tensor_tensor(f_parts(FL), F, f_parts(FH).bitcast(F32), SUB).then_inc(S("ffn_hidden_split"), 1)
                dve.wait_ge(S("ffn_hidden_split"), f + 1)

            for f in range(FFN_TURNS):
                lows(ffn_at + ffn_half("gu", f) + 1)
                if f:
                    ffn_hidden(f - 1)
                lows(ffn_at + ffn_half("gu", f) + 2)
                if f:
                    lows(ffn_at + ffn_half("down", f - 1) + 1)
            ffn_hidden(FFN_TURNS - 1)
            lows(ffn_at + 3 * FFN_TURNS)
            lows(halves_to("gate0", -1))
            dve.wait_ge(S("parts_read"), ffn_at + 3 * FFN_TURNS)
            V.tensor_tensor(H[:, :, :], H[:, :, :], ps[:, 4:8, :].rearrange("p (a b) n -> p a (b n)", a=2), ADD)\
                .then_inc(S("ffn_added"), 1)
            dve.wait_ge(S("ffn_added"), 1)
            rms(H, XS, EPS)
            lows(halves_to("gate0"))
            columns_low(("od_norm_mix", 0))
            lows(halves_to("value0"))
            HC, CO, SQ = w_(0, KC, 286), w_(2304, KC, T), w_(0, KC, T)
            MEAN, VAR, STD, RST = w_(4352, T), w_(4608, T), w_(4864, T), w_(5120, T)
            step(V.memset(HC, 0.0))
            for j in range(2):
                if j == 0:
                    lows(halves_to("gate1"))
                u, ug = UNIT[f"value{j}"], UNIT[f"gate{j}"]
                unit_ready(dve, u)
                dve.wait_ge(S(f"unit_read{ug % 2}"), ug // 2 + 1)
                src = PAIRS[u % 2].rearrange("p a (b t) -> p (a b) t", t=T)
                for b in range(4):
                    last = V.scalar_tensor_tensor(HC[:, 4 * j + b, 15:15 + T], src[:, b, :], vec("od_pw1_b", 4 * j + b),
                                                  w_(2304, 4, T)[:, b, :], ADD, MUL)
                last.then_inc(S(f"unit_read{u % 2}"), 1)
                dve.wait_ge(S(f"unit_read{u % 2}"), u // 2 + 1)
                dve.sem_inc(S("glu"), 1)
                if j == 0:
                    rms(XS, XS, EPS)
                    lows(halves_to("value1"))
            columns(XT, ("xa_norm_mem", 8))
            for k in range(CONV):
                for kc in range(KC - TAPS_ON_PE):
                    wv = vec("od_dw_w", KC * k + kc)
                    if k == 0:
                        last = V.tensor_scalar(CO[:, kc, :], HC[:, kc, 0:T], wv, vec("od_dw_b", kc), MUL, ADD)
                    else:
                        last = V.scalar_tensor_tensor(CO[:, kc, :], HC[:, kc, k:k + T], wv, CO[:, kc, :], MUL, ADD)
                step(last)
            dve.sem_inc(S("convolved"), 1)
            dve.wait_ge(S("feature_sums"), 1)
            step(V.tensor_scalar(MEAN, ps[:, 4, 0:T], 1.0 / D, None, MUL))
            rep = lambda a: a.rearrange("p (a t) -> p a t", a=1).broadcast_to([P, KC, T])
            step(V.tensor_tensor(CO, CO, rep(MEAN), SUB))
            V.tensor_tensor(SQ, CO, CO, MUL).then_inc(S("squared"), 1)
            dve.wait_ge(S("feature_sums"), 2)
            V.tensor_scalar(VAR, ps[:, 5, 0:T], 1.0 / D, EPS, MUL, ADD).then_inc(S("variance_ready"), 1)
            rsqrt(RST, STD)
            V.tensor_tensor(CO, CO, rep(RST), MUL).then_inc(S("standard"), 1)
            b = row(0)
            use_row(0, V.tensor_tensor(H[:, :, :], H[:, :, :], b.rearrange("p (a n) -> p a n", a=1).broadcast_to([P, 2, D]), ADD))
            for j in range(2):
                add_unit(f"pw2_{j}", j)
            update_done("pw2_1")
            dve.sem_inc(S("h_updated"), 1)
            attention("B", 2, ("xa_norm", 8))
            dve.sem_inc(S("h_updated"), 1)

            def first_best(values, a, n, best, pick, tmp):
                v3 = lambda t: t.rearrange("p (a n) -> p a n", n=1).broadcast_to([P, a, n])
                iom = IOM[:, 0:n].rearrange("p (a n) -> p a n", a=1).broadcast_to([P, a, n])
                step(V.tensor_reduce(best, values, X, ALU.max))
                step(V.tensor_tensor(tmp, values, v3(best), ALU.is_equal))
                step(V.tensor_tensor(tmp, tmp, iom, MUL))
                step(V.tensor_reduce(VI[:, 0:a], tmp, X, ALU.min))
                step(V.tensor_tensor(pick, iom, v3(VI[:, 0:a]), ALU.is_equal))

            def remove(values, pick):
                step(V.scalar_tensor_tensor(values, pick, -REMOVED, values, MUL, ADD))

            def ranks(k):
                c = MOES[k]
                G, M = c["groups"], c["members"]
                dve.wait_ge(S("ranks_ready"), k)
                r = ps[:, 5, 0:16].rearrange("p (a e) -> p a e", e=8)[:, :, 0:G]
                step(V.scalar_tensor_tensor(RK[:, :, 0:G], r, 1.0, SEL[:, :, 0:G], ADD, MUL))
                step(V.tensor_scalar(RK[:, :, 0:G], RK[:, :, 0:G], -1.0, None, ADD))
                V.tensor_scalar(RK[:, :, G:2 * G], RK[:, :, 0:G], -float(P), None, ADD)
                V.memset(RK[:, :, 2 * G:2 * G + 1], -1.0)
                V.memset(CB[:, :, 2 * G * M:(2 * G + 1) * M], 0.0)
                V.tensor_copy(CB[:, :, G * M:2 * G * M], CB[:, :, 0:G * M])
                step(V.tensor_reduce(CMAX, ps[:, 5, 16:16 + G], X, ALU.max))
                step(V.tensor_scalar(CMAX, CMAX, float(P), float(G), ALU.is_gt, MUL))
                V.tensor_scalar(count[:, k - 1:k], CMAX, float(G), None, ADD).then_inc(moe_sem(k, "turns_ready"), 1)

            def experts(k, dst, gain):
                c = MOES[k]
                M, C, halves = c["members"], c["members"] * c["chunks"], stream(c)
                N, NS = len(halves), c["slots"]
                PR, PT, Y, HID, SG = w_(0, 2, P), w_(256, 2, P), w_(512, D), w_(1536, PANEL), w_(2048, PANEL)
                iota = c_("iota")

                def pick(turn):
                    for tc in range(2):
                        V.tensor_copy(CBS[:, tc, 0:M], CB[:, tc, bass.ds(turn * M, M)])
                        last = V.tensor_scalar(PR[:, tc, :], iota, RK[:, tc, bass.ds(turn, 1)], None, ALU.is_equal)
                    last.then_inc(moe_sem(k, "picked"), 1)

                def gathered_low(turn):
                    dve.wait_ge(moe_sem(k, "gathered_high"), turn + 1)
                    if gain:
                        for kc in range(KC):
                            V.scalar_tensor_tensor(x_low[:, kc, :], ps[:, 5 + kc // 4, kc % 4 * P:kc % 4 * P + P], vec(gain, kc),
                                                   x_high[:, kc, :].bitcast(F32), MUL, SUB)
                    else:
                        V.tensor_tensor(x_low[:, :, :], ps[:, 5:7, :].rearrange("p b (k t) -> p (b k) t", t=P),
                                        x_high[:, :, :].bitcast(F32), SUB)
                    V.tensor_copy(GS[:, 0:M], ps[:, 7, 0:M]).then_inc(moe_sem(k, "gathered_split"), 1)

                def picks_ready(turn):
                    dve.wait_ge(moe_sem(k, "picks_turned"), turn + 1)
                    V.tensor_copy(PT, ps[:, 7, T:2 * T].rearrange("p (a t) -> p a t", t=P)).then_inc(moe_sem(k, "picks_ready"), 1)

                dve.sem_inc(moe_sem(k, "silu"), 1)
                dve.sem_inc(moe_sem(k, "gated"), 1)
                pick(0)
                gathered_low(0)
                picks_ready(0)
                dve.wait_ge(moe_sem(k, "turns_ready"), 1)
                turns = dve.value_load(count[0:1, k - 1:k], min_val=c["groups"], max_val=2 * c["groups"])
                with dve.Fori(0, turns) as it:

                    def hidden_rows(ch):
                        dve.wait_ge(moe_sem(k, "read"), it * N + (chunk_at(ch) + 4 + SPLITS))
                        dve.wait_ge(moe_sem(k, "silu"), it * C + (ch + 2))
                        m = ch // c["chunks"]
                        V.scalar_tensor_tensor(HID, ps[:, 1, :], GS[:, m:m + 1], SG, MUL, MUL).then_inc(moe_sem(k, "gated"), 1)

                    def hidden_low(ch):
                        dve.wait_ge(moe_sem(k, "hidden_high"), it * C + (ch + 1))
                        V.tensor_tensor(h_low[:, :, :], ps[:, 4, :].rearrange("p (k t) -> p k t", t=P),
                                        h_high[:, :, :].bitcast(F32), SUB).then_inc(moe_sem(k, "hidden_split"), 1)

                    for j in range(N):
                        if j == 6:
                            pick(it + 1)
                        for ch in range(C):
                            if j == chunk_at(ch) + 6:
                                hidden_rows(ch)
                            if j == chunk_at(ch) + 8:
                                hidden_low(ch)
                        dve.wait_ge(moe_sem(k, "high"), it * N + (j + 1))
                        V.tensor_tensor(w_low[:, j % SPLITS, :], ring[:, j % NS, :], w_high[:, j % SPLITS, :].bitcast(F32), SUB)\
                            .then_inc(moe_sem(k, "split"), 1)
                    hidden_low(C - 1)
                    gathered_low(it + 1)
                    dve.wait_ge(moe_sem(k, "read"), it * N + (N + SPLITS))
                    V.tensor_copy(Y[:, 512:1024], ps[:, 3, :]).then_inc(moe_sem(k, "outputs_by_vector"), 1)
                    for j in range(4):
                        dve.wait_ge(moe_sem(k, "scattered"), it * 4 + (j + 1))
                        d = dst[:, j // 2, j % 2 * 512:(j % 2 + 1) * 512]
                        V.tensor_tensor(d, d, ps[:, 5 + j % 2, :], ADD).then_inc(moe_sem(k, "added"), 1)
                    picks_ready(it + 1)
                    dve.wait_ge(moe_sem(k, "added"), it * 4 + 4)

            rms(H, XS, EPS)
            columns_low(("od_norm_moe", 0))
            dve.wait_ge(S("const_loaded"), 16)
            step(V.tensor_scalar(IOM, c_("iota")[:, 0:16], -99.0, None, ADD))
            dve.wait_ge(S("logits_ready"), 1)
            e8 = lambda t: t[:, :, 0:8]
            step(V.tensor_copy(e8(LG), ps[:, 4, 0:32].rearrange("p (a e) -> p a e", e=16)[:, :, 0:8]))
            first_best(e8(LG), 2, 8, V0[:, 0:2], e8(O0), e8(TA))
            remove(e8(LG), e8(O0))
            first_best(e8(LG), 2, 8, V1[:, 0:2], e8(O1), e8(TA))
            V.tensor_tensor(PAIRW[:, 0, :], V1[:, 0:2], V0[:, 0:2], SUB).then_inc(S("logit_gap"), 1)
            step(V.tensor_tensor(SEL, e8(O0), e8(O1), ADD))
            dve.sem_inc(S("chosen"), 1)
            dve.wait_ge(S("gap_exp"), 1)
            step(V.tensor_scalar(PAIRW[:, 2, :], PAIRW[:, 1, :], 1.0, None, ADD))
            step(V.reciprocal(PAIRW[:, 2, :], PAIRW[:, 2, :]))
            r3 = lambda t, n: t.rearrange("p (a n) -> p a n", n=1).broadcast_to([P, 2, n])
            step(V.scalar_tensor_tensor(e8(CB), e8(O1), 1.0, r3(PAIRW[:, 1, :], 8), MUL, MUL))
            step(V.tensor_tensor(e8(CB), e8(CB), e8(O0), ADD))
            step(V.tensor_tensor(e8(CB), e8(CB), r3(PAIRW[:, 2, :], 8), MUL))
            ranks(1)
            experts(1, H, "od_norm_moe")
            dve.sem_inc(S("moe_done"), 1)
            n_["sq"] += 1
            dve.wait_ge(S("squares_summed"), n_["sq"])
            V.tensor_scalar(var, ssq, 1.0 / D, EPS, MUL, ADD).then_inc(S("variance_ready"), 1)
            rsqrt()
            g = row(1)
            for tc in range(2):
                last = V.scalar_tensor_tensor(H[:, tc, :], H[:, tc, :], rstd[:, tc:tc + 1], g, MUL, MUL)
            use_row(1, last)
            layer_norm("h_ready")
            lows(halves_to("fqk", -1))
            columns_low(None)
            lows(halves_to("dqk"))
            take_columns("fqk", w_(0, 4, T))
            lows(halves_to("hq"))
            dve.wait_ge(S("small_loaded"), 16 * 10)
            step(V.tensor_tensor(lam4[:, 0::2, :], lam4[:, 0::2, :], lam4[:, 1::2, :], MUL))
            V.tensor_reduce(lamp, lam4[:, 0::2, :], X, ADD).then_inc(S("lam_sums"), 1)
            dve.wait_ge(S("lam_exp"), 1)
            step(V.tensor_tensor(nlam, lame[:, 1:2], lame[:, 0:1], SUB))
            step(V.tensor_scalar(nlam, nlam, -LAM_INIT, None, ADD))
            lows(halves_to("fv"))
            u = UNIT["fv"]
            unit_ready(dve, u)
            V.tensor_tensor(ffl, PAIRS[u % 2][:, :, 256:260], foxb.rearrange("p (a n) -> p a n", a=1).broadcast_to([P, 2, 4]), ADD)
            V.tensor_copy(w_(7168, 2, 256), PAIRS[u % 2][:, :, 0:256]).then_inc(S(f"unit_read{u % 2}"), 1)
            dve.wait_ge(S(f"unit_read{u % 2}"), u // 2 + 1)
            V.tensor_scalar(logf_fox, ffl, 0.0, None, ALU.min).then_inc(S("fox_logits"), 1)
            lows(halves_to("dv"))
            dve.wait_ge(S("fox_log1p"), 1)
            dve.wait_ge(S("fox_logits"), 1)
            V.tensor_tensor(logf_fox, logf_fox, ffa, SUB).then_inc(S("fox_log"), 1)
            u = UNIT["dv"]
            unit_ready(dve, u)
            V.tensor_copy(w_(7680, 2, 256), PAIRS[u % 2][:, :, 0:256]).then_inc(S(f"unit_read{u % 2}"), 1)
            HFZ, HFA = w_(9216, 2, 512), w_(4096, 2, 512)
            lows(halves_to("hf"))
            take("hf", HFZ)
            u = UNIT["hf"]
            dve.wait_ge(S(f"unit_read{u % 2}"), u // 2 + 1)
            dve.sem_inc(S("forget_logits"), 1)
            lows(halves_to("hi"))
            dve.wait_ge(S("forget_log1p"), 1)
            step(V.scalar_tensor_tensor(HFA, HFZ, 0.0, HFA, ALU.min, SUB))
            lows(halves_to("hg"))
            DB = XT[:, :, :].rearrange("p (a h) t -> p a h t", a=2)
            dve.wait_ge(S("fox_sums"), 2)
            cs = ffa
            step(V.tensor_copy(cs, ps[:, 4, 0:8].rearrange("p (a e) -> p a e", e=4)))
            masks = row(0).rearrange("p (k a t) -> p k a t", k=2, a=2)
            u = UNIT["hg"]
            for w in (u - 1, u):
                unit_ready(dve, w)
            for tc in range(2):
                for place, h in enumerate(HEAD_ORDER):
                    last = V.scalar_tensor_tensor(DB[:, tc, place, :], ps[:, 6 + h // 2, h % 2 * T:h % 2 * T + T], -1.0,
                                                  masks[:, 0, tc, :], MUL, ADD)
            step(last)
            for tc in range(2):
                for place, h in enumerate(HEAD_ORDER):
                    last = V.tensor_scalar(DB[:, tc, place, :], DB[:, tc, place, :], cs[:, tc, h:h + 1], None, ADD)
            step(last)
            dve.sem_inc(S("fox_bias"), 1)
            PR, PR2, PT = w_(8192, 2, 4, T), w_(10240, 2, 4, T), w_(10240, KC, T)

            def masked_scores(n, scale, bias, dst):
                dve.wait_ge(S("scores_ready"), 2 * n)
                for tc in range(2):
                    last = V.scalar_tensor_tensor(dst[:, tc, :, :], ps[:, 4 + 2 * tc:6 + 2 * tc, :].rearrange("p a (b t) -> p (a b) t", t=T),
                                                  scale, bias(tc), MUL, ADD)
                step(last)

            dve.wait_ge(S("keys_turned"), 1)
            masked_scores(3, 0.125, lambda tc: DB[:, tc, :, :], PR)
            dve.sem_inc(S("fox_scored"), 1)
            for tc in range(2):
                scores_max(PR[:, tc], 1.0, tc)
            for tc in range(2):
                normalise(3, PR, tc).then_inc(S("probs_ready"), 1)
            probs_columns(3, PT)
            dve.wait_ge(S("small_attended"), 1)
            V.tensor_copy(XS[:, :, 0:256], ps[:, 4, :].rearrange("p (a n) -> p a n", a=2)).then_inc(S("small_read"), 1)
            for which in range(2):
                dst = (PR, PR2)[which]
                masked_scores(4 + which, 32.0 ** -0.5,
                              lambda tc: masks[:, 1, tc:tc + 1, :].broadcast_to([P, 4, T]), dst)
                if which == 0:
                    dve.sem_inc(S("diff_map"), 1)
                for tc in range(2):
                    scores_max(dst[:, tc], 1.0, tc)
                for tc in range(2):
                    last = normalise(4 + which, dst, tc)
                step(last)
            use_row(0, V.scalar_tensor_tensor(PR.rearrange("p a h t -> p (a h t)"), PR2.rearrange("p a h t -> p (a h t)"), nlam[:, 0:1],
                                              PR.rearrange("p a h t -> p (a h t)"), MUL, ADD))
            dve.sem_inc(S("probs_ready"), 2)
            probs_columns(4, PT)
            dve.wait_ge(S("small_attended"), 2)
            OD = XS[:, :, 256:512]
            V.tensor_copy(OD, ps[:, 4, :].rearrange("p (a n) -> p a n", a=2)).then_inc(S("small_read"), 1)
            dve.wait_ge(S("small_read"), 2)

            def head_norm(src, scratch, n, d, gain, extra):
                step(V.tensor_tensor(scratch, src, src, MUL))
                step(V.tensor_reduce(dss, scratch, X, ADD))
                V.tensor_scalar(dss, dss, 1.0 / d, LN_EPS, MUL, ADD).then_inc(S("variance_ready"), 1)
                rsqrt(drs, dstd)
                for tc in range(2):
                    last = V.scalar_tensor_tensor(src[:, tc], src[:, tc], extra,
                                                  drs[:, tc, :].rearrange("p (h n) -> p h n", n=1).broadcast_to([P, 4, d]), MUL, MUL)
                step(last)
                for tc in range(2):
                    last = V.tensor_tensor(src[:, tc], src[:, tc], gain.rearrange("p (a n) -> p a n", a=1).broadcast_to([P, 4, d]), MUL)
                step(last)

            h4 = lambda t: t.rearrange("p a (h d) -> p a h d", h=4)
            head_norm(h4(OD), h4(w_(8192, 2, 256)), 4, 64, dgain, 1.0 - LAM_INIT)
            dve.sem_inc(S("diff_done"), 1)
            ST, QH, KH, CR = w_(11264, 8, P), w_(2048, 4, T), w_(3072, 4, T), w_(8192, 4, P)
            step(V.memset(ST, 0.0))
            dve.wait_ge(S("keys_columns"), 1)
            dve.wait_ge(S("levels_loaded"), 16)

            def decay(lv):
                E, QE, KE = level_tiles(lv)
                dve.wait_ge(S("level_exp"), lv + 1)
                if lv >= 2:
                    dve.wait_ge(S("level_scores"), lv)
                V.tensor_tensor(QE, QH, E, MUL)
                V.tensor_tensor(KE, KH, E, MUL).then_inc(S("level_decayed"), 1)

            decay(0)
            for lv in range(9):
                if lv + 1 < 8:
                    decay(lv + 1)
                dve.wait_ge(S("level_scores"), lv + 1)
                if lv < 8:
                    scores = ps[:, lv % 2 * 2:lv % 2 * 2 + 2, :].rearrange("p a (b t) -> p (a b) t", t=P)
                    mask = (IDENT if lv == 0 else c_(f"pair{lv - 1}")).bitcast(I32)
                    V.copy_predicated(ST, mask.rearrange("p (a t) -> p a t", a=1).broadcast_to([P, 8, P]), scores)\
                        .then_inc(S("level_merged"), 1)
                    dve.wait_ge(S("level_merged"), lv + 1)
                else:
                    dve.wait_ge(S("level_decayed"), 8)
                    V.tensor_copy(CR, ps[:, 0, :].rearrange("p (h t) -> p h t", t=P)).then_inc(S("level_merged"), 1)
            dve.wait_ge(S("recurrence_out"), 1)
            OH = XS[:, :, 512:1024]
            step(V.tensor_copy(OH, ps[:, 2:4, :]))
            head_norm(h4(OH), h4(w_(9216, 2, 512)), 4, 128, hgain, 1.0)
            V.tensor_tensor(OH, OH, w_(6144, 2, 512), MUL).then_inc(S("xs_ready"), 1)
            dve.wait_ge(S("xs_ready"), 9)
            lows(halves_to("out0", -1))
            columns_low(None)
            lows(halves_to("out1"))
            for j in range(2):
                add_unit(f"out{j}", j, ALPHA)
            update_done("out1")
            columns(XT, None)
            layer_norm("h_ready")
            attention("C", 6, None)
            layer_norm("h_ready")
            columns_low(None)
            V.tensor_scalar(XS[:, :, :], H[:, :, :], ALPHA, None, MUL)
            dve.wait_ge(S("router_scores"), 1)
            step(V.tensor_tensor(BI, LG, rbias.rearrange("p (a n) -> p a n", a=1).broadcast_to([P, 2, 16]), ADD))
            g4 = lambda t: t.rearrange("p a (g m) -> p (a g) m", m=4)
            WK = TA
            first_best(g4(BI), 8, 4, V0, g4(O0), g4(TA))
            step(V.tensor_copy(O1, BI))
            remove(O1, O0)
            step(V.tensor_reduce(V1, g4(O1), X, ALU.max))
            step(V.tensor_tensor(V0, V0, V1, ADD))
            gs = V0.rearrange("p (a g) -> p a g", g=4)
            first_best(gs, 2, 4, V1[:, 0:2], SEL[:, :, 0:4], TA[:, :, 0:4])
            dve.sem_inc(S("chosen"), 1)
            step(V.tensor_scalar(O1[:, :, 0:4], SEL[:, :, 0:4], -1.0, REMOVED, ADD, MUL))
            step(V.tensor_copy(V0.rearrange("p (a g) -> p a g", g=4), O1[:, :, 0:4]))
            step(V.tensor_tensor(g4(BI), g4(BI), V0.rearrange("p (a n) -> p a n", n=1).broadcast_to([P, 8, 4]), ADD))
            first_best(BI, 2, 16, V1[:, 0:2], O0, TA)
            remove(BI, O0)
            first_best(BI, 2, 16, V1[:, 0:2], O1, TA)
            step(V.tensor_tensor(O0, O0, O1, ADD))
            step(V.tensor_tensor(O0, O0, LG, MUL))
            step(V.tensor_reduce(V1[:, 0:2], O0, X, ADD))
            step(V.reciprocal(V1[:, 0:2], V1[:, 0:2]))
            step(V.tensor_tensor(CB[:, :, 0:16], O0, r3(V1[:, 0:2], 16), MUL))
            ranks(2)
            experts(2, XS, None)
            layer_norm("h_ready", XS)
            dve.sem_inc(S("h_final"), 1)


_NAMES = ("x mem ev_norm_mix ev_w_in ev_conv_a ev_pool_w ev_pool_scale ev_w_out ev_norm_ffn ev_ffn_gu ev_ffn_down "
          "od_norm_mix od_pw1_w od_pw1_b od_dw_w od_dw_b od_ln_g od_ln_b od_pw2_w od_pw2_b od_norm_moe od_router "
          "od_moe_gu od_moe_down xa_norm xa_norm_mem xa_wq xa_wkv xa_wo final_norm mem_2 ln_in_g_2 ln_in_b_2 w_in_2 "
          "fox_fb_2 lam_q1_2 lam_k1_2 lam_q2_2 lam_k2_2 diff_norm_g_2 hgrn_norm_g_2 w_out_2 mem_wq_2 mem_wk_2 "
          "mem_wv_2 mem_wo_2 router_w_2 router_b_2 w1_2 w3_2 w2_2 ln_g_2 ln_b_2").split()


def kernel(**inputs):
    import concourse.bacc as bacc
    from concourse.bass_utils import run_bass_kernel_spmd

    nc = bacc.Bacc("TRN2", target_bir_lowering=False, num_devices=1)
    arrays, ins = {}, {}
    for name in _NAMES:
        a = np.ascontiguousarray(inputs[name])
        arrays["in_" + name] = a
        ins[name] = nc.dram_tensor("in_" + name, a.shape, F32, kind="ExternalInput").ap()
    arrays["constants"] = CONSTANTS
    const_in = nc.dram_tensor("constants", CONSTANTS.shape, F32, kind="ExternalInput").ap()
    out = nc.dram_tensor("out", (1, T, D), F32, kind="ExternalOutput").ap()
    program(nc, ins, const_in, out)
    r = run_bass_kernel_spmd(nc, [arrays], core_ids=[0])
    return r.results[0]["out"]
```
